# Optimizing a Trainium2 kernel written in Bass

```python
import jax, jax.numpy as jnp
from jax import lax
import numpy as np

D_MODEL = 1024
BATCH = 1
SEQ = 256
DEPTH = 1
DEC_BATCH = 8
DEC_SEQ = 1
PAST_LEN = 2048
PAGE_SIZE = 128

HEAD_DIM = 64
ATT_HEADS = 8
ATT_W = ATT_HEADS * HEAD_DIM
MEM_HEADS = 4
MEM_W = MEM_HEADS * HEAD_DIM
CONV_W = D_MODEL // 4
MIX_W = ATT_W + CONV_W + MEM_W
PROJ_W = 3 * ATT_W + MEM_W + 3 * CONV_W
N_MEM = 256
CONV_K = 3
MOBA_BLOCK = 256
MOBA_TOPK = 3
Q_BLOCK = 128
N_EXPERTS = 32
TOP_K = 4
D_FF = D_MODEL
SWIGLU_LIMIT = 7.0
SWIGLU_ALPHA = 1.702
EXPERT_BLOCK = 128
LN_EPS = 1e-5
DN_ALPHA = (2 * DEPTH) ** 0.25
DN_BETA = (8 * DEPTH) ** -0.25

kernel_name = 'moba_shortconv_memxattn_moe_step'

def _layernorm(x, g, b):
    xf = x.astype(jnp.float32)
    xc = xf - jnp.mean(xf, -1, keepdims=True)
    var = jnp.mean(xc * xc, -1, keepdims=True)
    return (xc * lax.rsqrt(var + LN_EPS) * g.astype(jnp.float32) + b.astype(jnp.float32)).astype(x.dtype)

def _rms(x):
    xf = x.astype(jnp.float32)
    return (xf * lax.rsqrt(jnp.mean(xf * xf, -1, keepdims=True) + LN_EPS)).astype(x.dtype)

def _alibi_slopes():
    return 2.0 ** (-8.0 * jnp.arange(1, ATT_HEADS + 1, dtype=jnp.float32) / ATT_HEADS)

def _pad_to_blocks(parts):
    length = sum(p.shape[1] for p in parts)
    pad = (-length) % MOBA_BLOCK
    parts = list(parts)
    if pad:
        p0 = parts[0]
        parts.append(jnp.zeros((p0.shape[0], pad) + p0.shape[2:], p0.dtype))
    return jnp.concatenate(parts, axis=1) if len(parts) > 1 else parts[0]

def _moba_attention(q, k, v, q_start, slopes):
    B, Sq, H, hd = q.shape
    NB = k.shape[1] // MOBA_BLOCK
    kblk = k.reshape(B, NB, MOBA_BLOCK, H, hd)
    vblk = v.reshape(B, NB, MOBA_BLOCK, H, hd)
    kmean = jnp.mean(kblk.astype(jnp.float32), axis=2)
    qc_len = Q_BLOCK if Sq % Q_BLOCK == 0 else Sq
    n_chunks = Sq // qc_len
    n_sel = min(MOBA_TOPK, NB)
    scale = hd ** -0.5
    head_idx = jnp.arange(H)[:, None, None]
    slot_rank = jnp.arange(n_sel)
    offs = jnp.arange(MOBA_BLOCK)

    def chunk(args):
        qc, b, c = args
        pos = q_start + c * qc_len + jnp.arange(qc_len)
        own = pos // MOBA_BLOCK
        gate = jnp.einsum('qhd,nhd->hqn', qc.astype(jnp.float32), kmean[b])
        gate = jnp.where(jnp.arange(NB)[None, None, :] < own[None, :, None], gate, -jnp.inf)
        _, sel = lax.top_k(gate, n_sel)
        own_b = jnp.broadcast_to(own[None, :, None], (H, qc_len, 1)).astype(sel.dtype)
        blocks = jnp.concatenate([sel, own_b], axis=-1)
        ksel = kblk[b][blocks, :, head_idx, :]
        vsel = vblk[b][blocks, :, head_idx, :]
        key_pos = blocks[..., None] * MOBA_BLOCK + offs
        slot_ok = jnp.concatenate([slot_rank[None, :] < own[:, None], jnp.ones((qc_len, 1), bool)], axis=-1)
        valid = slot_ok[None, :, :, None] & (key_pos <= pos[None, :, None, None])
        dist = (pos[None, :, None, None] - key_pos).astype(jnp.float32)
        logits = jnp.einsum('qhd,hqnkd->hqnk', qc, ksel, preferred_element_type=jnp.float32) * scale - slopes[:, None, None, None] * dist
        probs = jax.nn.softmax(jnp.where(valid, logits, -jnp.inf), axis=(-2, -1))
        return jnp.einsum('hqnk,hqnkd->qhd', probs.astype(vsel.dtype), vsel)

    idx = jnp.arange(B * n_chunks)
    out = lax.map(chunk, (q.reshape(B * n_chunks, qc_len, H, hd), idx // n_chunks, idx % n_chunks))
    return out.reshape(B, Sq, H, hd)

def _mem_attention(q, mem_k, mem_v):
    logits = jnp.einsum('bthd,bmhd->bhtm', q, mem_k, preferred_element_type=jnp.float32) * (HEAD_DIM ** -0.5)
    probs = jax.nn.softmax(logits, axis=-1)
    return jnp.einsum('bhtm,bmhd->bthd', probs.astype(mem_v.dtype), mem_v)

def _short_conv(u, prev, w):
    T = u.shape[1]
    up = jnp.concatenate([prev.astype(u.dtype), u], axis=1)
    y = sum(w[i] * up[:, i:i + T] for i in range(CONV_K))
    return y, up[:, T:]

def _project(x, w_in):
    B, T, _ = x.shape
    p = x @ w_in
    cuts = [ATT_W, 2 * ATT_W, 3 * ATT_W, 3 * ATT_W + MEM_W, 3 * ATT_W + MEM_W + CONV_W, 3 * ATT_W + MEM_W + 2 * CONV_W]
    q, k, v, qm, gb, gc, h = jnp.split(p, cuts, axis=-1)
    heads = lambda t, n: t.reshape(B, T, n, HEAD_DIM)
    return heads(q, ATT_HEADS), heads(k, ATT_HEADS), heads(v, ATT_HEADS), heads(qm, MEM_HEADS), gb, gc, h

def _moe(x, w_router, b_router, w_gate_up, b_gate_up, w_down, b_down):
    D = x.shape[-1]
    xt = x.reshape(-1, D)
    N = xt.shape[0]
    M = N * TOP_K
    logits = (xt @ w_router).astype(jnp.float32) + b_router.astype(jnp.float32)
    top_v, top_e = lax.top_k(logits, TOP_K)
    gate_w = jax.nn.softmax(top_v, axis=-1)
    flat_e = top_e.reshape(M)
    order = jnp.argsort(flat_e)
    e_s = flat_e[order]
    tok_s = order // TOP_K
    w_s = gate_w.reshape(M)[order]
    counts = jnp.bincount(flat_e, length=N_EXPERTS)
    padded = (counts + EXPERT_BLOCK - 1) // EXPERT_BLOCK * EXPERT_BLOCK
    pad_end = jnp.cumsum(padded)
    pad_start = pad_end - padded
    start = jnp.cumsum(counts) - counts
    dest = pad_start[e_s] + jnp.arange(M) - start[e_s]
    n_blocks = (M + N_EXPERTS * (EXPERT_BLOCK - 1) + EXPERT_BLOCK - 1) // EXPERT_BLOCK
    buf = jnp.zeros((n_blocks * EXPERT_BLOCK, D), xt.dtype).at[dest].set(xt[tok_s])
    block_e = jnp.minimum(jnp.searchsorted(pad_end, jnp.arange(n_blocks) * EXPERT_BLOCK, side='right'), N_EXPERTS - 1)

    def expert_block(args):
        xb, e = args
        gu = xb @ w_gate_up[e] + b_gate_up[e]
        g, u = jnp.split(gu, 2, axis=-1)
        g = jnp.minimum(g, SWIGLU_LIMIT)
        u = jnp.clip(u, -SWIGLU_LIMIT, SWIGLU_LIMIT)
        hid = (u + 1.0) * g * jax.nn.sigmoid(SWIGLU_ALPHA * g)
        return hid @ w_down[e] + b_down[e]

    out = lax.map(expert_block, (buf.reshape(n_blocks, EXPERT_BLOCK, D), block_e)).reshape(n_blocks * EXPERT_BLOCK, D)
    y = jax.ops.segment_sum(out[dest] * w_s[:, None].astype(out.dtype), tok_s, num_segments=N)
    return y.reshape(x.shape)

def _finish(x, o_att, o_conv, o_mem, g_mix, w_out, ln1_g, ln1_b, w_router, b_router, w_gate_up, b_gate_up, w_down, b_down, ln2_g, ln2_b):
    B, T, _ = x.shape
    mix = jnp.concatenate([_rms(o_att.reshape(B, T, ATT_W)), _rms(o_conv), _rms(o_mem.reshape(B, T, MEM_W))], axis=-1) * g_mix
    x1 = _layernorm(DN_ALPHA * x + mix @ w_out, ln1_g, ln1_b)
    return _layernorm(DN_ALPHA * x1 + _moe(x1, w_router, b_router, w_gate_up, b_gate_up, w_down, b_down), ln2_g, ln2_b)

def setup_inputs(seed: int = 0) -> dict:
    key = jax.random.key(seed)
    ks = jax.random.split(key, 24)
    n_pages = PAST_LEN // PAGE_SIZE
    n_used = DEC_BATCH * n_pages
    n_phys = n_used + max(1, n_used // 4)
    f32 = jnp.float32
    nrm = lambda k, shape, s: jax.random.normal(k, shape, f32) * s
    x_prompt = nrm(ks[0], (BATCH, SEQ, D_MODEL), 1.0)
    x_sample = nrm(ks[1], (DEC_BATCH, DEC_SEQ, D_MODEL), 1.0)
    cache_k = nrm(ks[2], (DEPTH, n_phys, PAGE_SIZE, ATT_HEADS, HEAD_DIM), 1.0)
    cache_v = nrm(ks[3], (DEPTH, n_phys, PAGE_SIZE, ATT_HEADS, HEAD_DIM), DN_BETA)
    cache_mem_k = nrm(ks[4], (DEPTH, DEC_BATCH, N_MEM, MEM_HEADS, HEAD_DIM), 1.0)
    cache_mem_v = nrm(ks[5], (DEPTH, DEC_BATCH, N_MEM, MEM_HEADS, HEAD_DIM), 1.0)
    state_conv = nrm(ks[6], (DEPTH, DEC_BATCH, CONV_K - 1, CONV_W), 1.0)
    page_table = jax.random.permutation(ks[7], n_phys)[:n_used].reshape(DEC_BATCH, n_pages).astype(jnp.int32)
    mem_prompt = nrm(ks[8], (BATCH, N_MEM, D_MODEL), 1.0)
    w_in = nrm(ks[9], (DEPTH, D_MODEL, PROJ_W), D_MODEL ** -0.5)
    w_in = w_in.at[:, :, 2 * ATT_W:3 * ATT_W].multiply(DN_BETA)
    w_mem_kv = nrm(ks[10], (DEPTH, D_MODEL, 2 * MEM_W), D_MODEL ** -0.5)
    w_conv = nrm(ks[11], (DEPTH, CONV_K, CONV_W), CONV_K ** -0.5)
    g_mix = 1.0 + nrm(ks[12], (DEPTH, MIX_W), 0.02)
    w_out = nrm(ks[13], (DEPTH, MIX_W, D_MODEL), MIX_W ** -0.5 * DN_BETA)
    ln1_g = 1.0 + nrm(ks[14], (DEPTH, D_MODEL), 0.02)
    ln1_b = nrm(ks[15], (DEPTH, D_MODEL), 0.02)
    w_router = nrm(ks[16], (DEPTH, D_MODEL, N_EXPERTS), D_MODEL ** -0.5)
    b_router = nrm(ks[17], (DEPTH, N_EXPERTS), 0.01)
    w_gate_up = nrm(ks[18], (DEPTH, N_EXPERTS, D_MODEL, 2 * D_FF), D_MODEL ** -0.5 * DN_BETA)
    b_gate_up = nrm(ks[19], (DEPTH, N_EXPERTS, 2 * D_FF), 0.01)
    w_down = nrm(ks[20], (DEPTH, N_EXPERTS, D_FF, D_MODEL), D_FF ** -0.5 * DN_BETA)
    b_down = nrm(ks[21], (DEPTH, N_EXPERTS, D_MODEL), 0.01)
    ln2_g = 1.0 + nrm(ks[22], (DEPTH, D_MODEL), 0.02)
    ln2_b = nrm(ks[23], (DEPTH, D_MODEL), 0.02)
    return {'x_prompt': x_prompt, 'x_sample': x_sample, 'cache_k': cache_k, 'cache_v': cache_v,
            'cache_mem_k': cache_mem_k, 'cache_mem_v': cache_mem_v, 'state_conv': state_conv,
            'page_table': page_table, 'mem_prompt': mem_prompt, 'w_in': w_in, 'w_mem_kv': w_mem_kv,
            'w_conv': w_conv, 'g_mix': g_mix, 'w_out': w_out, 'ln1_g': ln1_g, 'ln1_b': ln1_b,
            'w_router': w_router, 'b_router': b_router, 'w_gate_up': w_gate_up, 'b_gate_up': b_gate_up,
            'w_down': w_down, 'b_down': b_down, 'ln2_g': ln2_g, 'ln2_b': ln2_b}

def reference(x_prompt, x_sample, cache_k, cache_v, cache_mem_k, cache_mem_v, state_conv, page_table, mem_prompt,
              w_in, w_mem_kv, w_conv, g_mix, w_out, ln1_g, ln1_b, w_router, b_router, w_gate_up, b_gate_up,
              w_down, b_down, ln2_g, ln2_b):
    slopes = _alibi_slopes()
    past_len = page_table.shape[1] * PAGE_SIZE
    hp, hs = x_prompt, x_sample
    Bp = hp.shape[0]
    Bs = hs.shape[0]
    kp_rows, vp_rows, conv_p, memk_p, memv_p, ks_rows, vs_rows, conv_s = [], [], [], [], [], [], [], []
    for l in range(DEPTH):
        ffn = (g_mix[l], w_out[l], ln1_g[l], ln1_b[l], w_router[l], b_router[l], w_gate_up[l], b_gate_up[l],
               w_down[l], b_down[l], ln2_g[l], ln2_b[l])
        q, k, v, qm, gb, gc, h = _project(hp, w_in[l])
        o_att = _moba_attention(q, _pad_to_blocks([k]), _pad_to_blocks([v]), 0, slopes)
        mk, mv = jnp.split(mem_prompt @ w_mem_kv[l], 2, axis=-1)
        mk = mk.reshape(Bp, N_MEM, MEM_HEADS, HEAD_DIM)
        mv = mv.reshape(Bp, N_MEM, MEM_HEADS, HEAD_DIM)
        o_mem = _mem_attention(qm, mk, mv)
        cz, c_state = _short_conv(gc * h, jnp.zeros((Bp, CONV_K - 1, CONV_W), hp.dtype), w_conv[l])
        hp = _finish(hp, o_att, gb * cz, o_mem, *ffn)
        kp_rows.append(k)
        vp_rows.append(v)
        conv_p.append(c_state)
        memk_p.append(mk)
        memv_p.append(mv)
        q, k, v, qm, gb, gc, h = _project(hs, w_in[l])
        rows = (Bs, past_len, ATT_HEADS, HEAD_DIM)
        k_all = _pad_to_blocks([cache_k[l, page_table].reshape(rows), k])
        v_all = _pad_to_blocks([cache_v[l, page_table].reshape(rows), v])
        o_att = _moba_attention(q, k_all, v_all, past_len, slopes)
        o_mem = _mem_attention(qm, cache_mem_k[l], cache_mem_v[l])
        cz, c_state = _short_conv(gc * h, state_conv[l], w_conv[l])
        hs = _finish(hs, o_att, gb * cz, o_mem, *ffn)
        ks_rows.append(k)
        vs_rows.append(v)
        conv_s.append(c_state)
    return (hp, hs, jnp.stack(kp_rows), jnp.stack(vp_rows), jnp.stack(conv_p), jnp.stack(memk_p), jnp.stack(memv_p),
            jnp.stack(ks_rows), jnp.stack(vs_rows), jnp.stack(conv_s))


_drawn_inputs = setup_inputs


def setup_inputs(seed=0):
    import zlib

    import numpy as np

    out = dict(_drawn_inputs(seed))
    spreads = {}
    factors = {'g_mix': 10.314,
     'b_router': 21.952,
     'b_gate_up': 26.204,
     'b_down': 8.0,
     'ln2_g': 7.633,
     'ln2_b': 8.018}
    for name, (base, spread) in spreads.items():
        noise = np.random.default_rng([zlib.crc32(name.encode()), seed]).standard_normal(out[name].shape)
        drawn = base * np.exp(spread * noise) if base else spread * noise
        out[name] = __import__('jax').numpy.asarray(drawn.astype(out[name].dtype))
    for name, factor in factors.items():
        out[name] = (out[name] * factor).astype(out[name].dtype)
    return out
```

```python
from contextlib import ExitStack

import concourse.bass as bass
from concourse import mybir

ALU = mybir.AluOpType
ACT = mybir.ActivationFunctionType
AX = mybir.AxisListType
F32 = mybir.dt.float32
BF16 = mybir.dt.bfloat16
I32 = mybir.dt.int32
U32 = mybir.dt.uint32

BIG = 1.0e30
PARTS = 128


class Counter:

    def __init__(self, sem):
        self.sem, self.n = sem, 0

    def on(self, instruction):
        instruction.then_inc(self.sem, 1)
        self.n += 1
        return self.n


def layer_kernel(nc, x_prompt, x_sample, cache_k, cache_v, cache_mem_k, cache_mem_v, state_conv, page_table,
                 mem_prompt, w_in, w_mem_kv, w_conv, g_mix, w_out, ln1_g, ln1_b, w_router, b_router,
                 w_gate_up, b_gate_up, w_down, b_down, ln2_g, ln2_b,
                 y_prompt, y_sample, k_prompt, v_prompt, conv_prompt, mem_k_prompt, mem_v_prompt,
                 k_sample, v_sample, conv_sample, expert_rows):
    D = x_prompt.shape[2]
    NP = x_prompt.shape[1]
    NS = x_sample.shape[0]
    T = NP + NS
    KC = D // PARTS
    HD = 64
    HEADS = cache_k.shape[3]
    MHEADS = cache_mem_k.shape[3]
    AW = HEADS * HD
    MW = MHEADS * HD
    NMEM = mem_prompt.shape[1]
    PAGES = page_table.shape[1]
    NPHYS = cache_k.shape[1]
    PAST = PAGES * PARTS
    BLK = 256
    NBLK = PAST // BLK
    PC = w_in.shape[2] // PARTS
    E = w_router.shape[2]
    FF = w_down.shape[2]
    TOPK = 4
    SLOTS = 64
    MAX_BLOCKS = E + (T * TOPK) // (SLOTS + 1)
    HALF = D // 2
    QSCALE = HD ** -0.5
    ALPHA = 2.0 ** 0.25
    EPS = 1e-5
    LIMIT = 7.0
    SW_ALPHA = 1.702
    ROWS = NS * HEADS
    MROWS = NS * MHEADS
    assert ROWS == 64 and NP == 256 and PARTS == page_table.shape[1] * NS and PC == 20
    CQ, CK, CV, CM, CB, CC, CH = 0, 4, 8, 12, 14, 16, 18
    OATT, OCONV, OMEM = 0, 4, 6

    ctx = ExitStack()
    with ctx:
        def sb(name, shape, dt=F32):
            return ctx.enter_context(nc.sbuf_tensor(name, shape, dt))

        def sem(name):
            return ctx.enter_context(nc.semaphore(name))

        gate_up_w = sb("gate_up_w", [PARTS, KC, 2 * FF])
        down_w = sb("down_w", [PARTS, KC, D])
        ring = [sb("ring_a", [PARTS, PAGES * AW]), sb("ring_b", [PARTS, PAGES * AW])]
        x_rows = sb("x_rows", [PARTS, 3, D])
        x_cols = sb("x_cols", [PARTS, KC, T])
        work = sb("work", [PARTS, 2 * KC * NMEM])
        consts = sb("consts", [PARTS, 1280])
        small = sb("small", [PARTS, 1280])
        pages = sb("pages", [1, PARTS], I32)
        topi = sb("topi", [PARTS, 3, 8], U32)
        seli = sb("seli", [ROWS, 8], U32)
        rowi = sb("rowi", [PARTS, 8], I32)
        slot_rows = sb("slot_rows", [PARTS, 3, TOPK], I32)
        block_expert = sb("block_expert", [1, MAX_BLOCKS + 1], I32)
        n_blocks = sb("n_blocks", [1, 1], I32)
        bank = [ctx.enter_context(nc.psum_tensor(f"bank{i}", [PARTS, 512], F32))[:, :] for i in range(8)]

        used = {"c": 0, "s": 0}

        def const(n, rows=PARTS):
            a = used["c"]
            used["c"] += n
            assert used["c"] <= 1280
            return consts[0:rows, a:a + n]

        def scratch(n, rows=PARTS):
            a = used["s"]
            used["s"] += n
            assert used["s"] <= 1280
            return small[0:rows, a:a + n]

        w_in_a = gate_up_w
        RA, RB = ring
        w_in_b = RA[:, 0:KC * 512].rearrange("p (k n) -> p k n", k=KC)
        w_mem = RA[:, KC * 512:2 * KC * 512].rearrange("p (k n) -> p k n", k=KC)
        down_flat = down_w[:, :, :].rearrange("p k n -> p (k n)")
        p_cols = down_flat[:, 0:PC * T].rearrange("p (j t) -> p j t", j=PC)
        at = PC * T
        scores = down_flat[:, at:at + PAGES * ROWS].rearrange("p (g r) -> p g r", g=PAGES)
        at += PAGES * ROWS
        mem_cols = down_flat[:, at:at + 4 * NMEM].rearrange("p (j t) -> p j t", j=4)
        stage = down_flat[:, at:at + 4 * NMEM]
        at += 4 * NMEM
        q_new = down_flat[0:NS, at:at + AW]
        at += AW
        qm_new = down_flat[0:NS, at:at + MW]
        at += MW
        assert at <= KC * D
        head_slope_eye = gate_up_w[:, 0, 0:HEADS * PARTS].rearrange("p (h c) -> p h c", h=HEADS)
        squares = gate_up_w[:, 0, :].rearrange("p (j t) -> p j t", j=KC)
        ln1_gain, ln1_bias = gate_up_w[:, 1, 0:D], gate_up_w[:, 1, D:2 * D]
        k_new, v_new = gate_up_w[0:NS, 2, 0:AW], gate_up_w[0:NS, 2, AW:2 * AW]
        mem_mask = gate_up_w[:, 2, 2 * AW:3 * AW].rearrange("p (q c) -> p q c", q=2)
        mem_masked = gate_up_w[:, 2, 3 * AW:4 * AW].rearrange("p (q c) -> p q c", q=2)
        logits = gate_up_w[0:ROWS, 3, 0:PAST]
        w_o = gate_up_w[:, 4:8, :].rearrange("p s (u n) -> p (s u) n", u=2)
        mem_rows = work[:, 0:2 * D].rearrange("p (c d) -> p c d", c=2)
        mem_x = work[:, 2 * D:2 * D + KC * NMEM].rearrange("p (k t) -> p k t", k=KC)
        k_rows = work[:, 0:2 * AW].rearrange("p (c d) -> p c d", c=2)
        v_rows = work[:, 2 * AW:4 * AW].rearrange("p (c d) -> p c d", c=2)
        mkv_rows = work[:, 4 * AW:6 * AW].rearrange("p (c d) -> p c d", c=2)
        probs = work[:, 6 * AW:7 * AW].rearrange("p (b k) -> p b k", b=2)
        probs_t = work[:, 7 * AW:8 * AW].rearrange("p (b k) -> p b k", b=2)
        o_masked = k_rows
        o_cols = x_cols
        bias_f32 = RA[0:3 * E, 0:2 * FF + D]
        zero_rows = RA[:, 2 * FF + D:2 * FF + 2 * D]
        bias_parts = RA[0:3 * E, 6144:6144 + 1536].bitcast(BF16)
        rb = {"n": 0}

        def part_b(n, rows=PARTS):
            a = rb["n"]
            rb["n"] += n
            assert rb["n"] <= PAGES * AW
            return RB[0:rows, a:a + n]

        xg = part_b(HALF)
        xg_t = part_b(HALF).rearrange("p (j h s) -> p j h s", j=4, h=2)
        gate_v, up_v, sig_v, hid = part_b(HALF), part_b(HALF), part_b(HALF), part_b(HALF)
        ends_cmp = RB[0:1, rb["n"] - 4 * HALF:rb["n"] - 4 * HALF + (MAX_BLOCKS + 1) * E].rearrange("p (b e) -> p b e", e=E)
        oh_g = RB[:, rb["n"] - 3 * TOPK * E:rb["n"]].rearrange("p (c k e) -> p c k e", c=3, k=TOPK)
        assert (MAX_BLOCKS + 1) * E + 3 * TOPK * E <= 4 * HALF
        hid_t = part_b(HALF).rearrange("p (j h s) -> p j h s", j=4, h=2)
        out_rows = part_b(HALF)
        slot_eq = part_b(3 * TOPK * SLOTS).rearrange("p (c k s) -> p c k s", c=3, k=TOPK)
        slot_hot = part_b(3 * SLOTS).rearrange("p (c s) -> p c s", c=3)
        onehot = part_b(3 * TOPK * E).rearrange("p (c k e) -> p c k e", c=3, k=TOPK)
        ln2_gain, ln2_bias = part_b(D), part_b(D)
        gathered = gate_up_w[:, :, :].rearrange("p k (u n) -> p (k u) n", u=2)

        ident = const(PARTS)
        ones = const(PARTS)
        tri = const(PARTS)
        dist = const(2 * PARTS)
        head_mask = const(AW)
        eps = const(1)
        row_f = const(8)
        iota8 = const(8)
        hot8 = const(8)
        slope8 = const(8)
        slope = const(1)
        row_sel = const(4)
        grp_sel = const(4)
        q_sel = const(2)
        delta8 = const(ROWS, NS)
        dsel = const(8, ROWS)
        g_cols = scratch(KC)
        w_cols = scratch(6).rearrange("p (j i) -> p j i", j=2)
        s_cols = scratch(4 * NS).rearrange("p (j b r) -> p j b r", j=2, b=NS)
        mem_scores = scratch(2 * MROWS).rearrange("p (g r) -> p g r", g=2)
        mem_pt = scratch(2 * MROWS).rearrange("p (g r) -> p g r", g=2)
        s_own_prod = scratch(0)
        so = scratch(8, NS)
        so_spread = scratch(ROWS, NS)
        po_new = scratch(ROWS, NS)
        po_spread = scratch(8, ROWS)
        own = scratch(1, ROWS)
        stat = scratch(16, ROWS)
        gate8 = scratch(8, ROWS)
        top8 = scratch(8, ROWS)
        seli_f = scratch(8, ROWS)
        pen = scratch(8, ROWS)
        mstat = scratch(4, MROWS)
        neg_max = scratch(2)
        row_sum = scratch(2)
        row_inv = scratch(2)
        u_s = scratch(2 * NS).rearrange("p (j b) -> p j b", j=2)
        c_s = scratch(4 * NS).rearrange("p (a j b) -> p a j b", a=2, j=2)
        sq_s = scratch(KC * NS).rearrange("p (j t) -> p j t", j=KC)
        rms_s = scratch(3 * NS)
        ln_s = scratch(3 * 8).rearrange("p (c i) -> p c i", c=3)
        lg = scratch(3 * E).rearrange("p (c e) -> p c e", c=3)
        br_row = scratch(E)
        max8 = scratch(24).rearrange("p (c k) -> p c k", c=3)
        topf = scratch(24).rearrange("p (c k) -> p c k", c=3)
        w4 = scratch(3 * TOPK).rearrange("p (c k) -> p c k", c=3)
        w4s = scratch(3)
        chosen = scratch(3 * E).rearrange("p (c e) -> p c e", c=3)
        iota32 = scratch(E)
        nb = scratch(E)
        ends = scratch(E)
        starts = scratch(E)
        slots_g = scratch(3 * E).rearrange("p (c e) -> p c e", c=3)
        slot4 = scratch(3 * TOPK).rearrange("p (c k) -> p c k", c=3)
        slot_id = scratch(SLOTS)
        rms_p = probs
        w_r = work[:, 4 * AW:4 * AW + KC * E].rearrange("p (k e) -> p k e", k=KC)
        rep3 = work[:, 5 * AW:5 * AW + 2 * 3 * E].rearrange("p (a r e) -> p a r e", a=2, r=3)
        range96 = work[0:3 * E, 5 * AW + 192:5 * AW + 194]
        block_id = work[0:3 * E, 5 * AW + 200:5 * AW + 200 + SLOTS]
        block_ge = work[0:3 * E, 5 * AW + 264:5 * AW + 264 + SLOTS]
        bias_hot = work[0:3 * E, 5 * AW + 328:5 * AW + 328 + SLOTS // 2].bitcast(BF16)
        block_iota = work[0:1, 5 * AW + 360:5 * AW + 360 + MAX_BLOCKS + 1]
        block_ef = work[0:1, 5 * AW + 410:5 * AW + 410 + MAX_BLOCKS + 1]
        assert 410 + MAX_BLOCKS + 1 <= 512

        x_in, mem_in, pages_in, smalls_in = sem("x_in"), sem("mem_in"), sem("pages_in"), sem("smalls_in")
        w_q_in, w_kv_in, w_m_in, w_ch_in, w_mem_in = (sem("w_q_in"), sem("w_kv_in"), sem("w_m_in"),
                                                      sem("w_ch_in"), sem("w_mem_in"))
        ring_in = [sem("ring_a_in"), sem("ring_b_in")]
        w_out_in, ln1_in, router_in, ln2_in, bias_in = (sem("w_out_in"), sem("ln1_in"), sem("router_in"),
                                                        sem("ln2_in"), sem("bias_in"))
        gu_in = [sem(f"gate_up_in{k}") for k in range(KC)]
        dn_in = [sem(f"down_in{k}") for k in range(KC)]
        eye_ready, const_ready, rowi_ready, sel_ready = (sem("eye_ready"), sem("const_ready"), sem("rowi_ready"),
                                                         sem("sel_ready"))
        tile_ready, tile_copied = sem("tile_ready"), sem("tile_copied")
        qb_ready, k_scored = sem("query_spread"), sem("keys_scored")
        eyes_ready, logits_iota = sem("slope_eyes_ready"), sem("logits_iota_ready")
        sc_ready, mx_ready, exp_done, inv_ready = (sem("unit_scores"), sem("unit_max"), sem("unit_exp"),
                                                   sem("unit_inverse"))
        norm_done, pt_ready, pt_copied, pv_ready, o_copied = (sem("unit_norm"), sem("unit_turned"),
                                                              sem("unit_turned_copied"), sem("unit_pv"),
                                                              sem("unit_out_copied"))
        conv_done, conv_u = sem("conv_done"), sem("conv_u_ready")
        sq_ready, ss_ready, rt_ready, ri_ready, mix_ready = (sem("squares_ready"), sem("square_sums"),
                                                             sem("rms_root"), sem("rms_inverse"), sem("mix_ready"))
        proj_ready, res_ready, var_ready, root_ready, x1_ready = (sem("out_proj"), sem("centered_ready"),
                                                                  sem("variance_ready"), sem("root_ready"),
                                                                  sem("x1_ready"))
        x1t_ready, x1t_copied, lg_ready = sem("x1_turned"), sem("x1_turned_copied"), sem("router_logits")
        so_ready, own_ready, l_ready, sm_max, sm_exp, sm_p = (sem("own_spread"), sem("own_score"),
                                                              sem("score_rows"), sem("softmax_max"),
                                                              sem("softmax_exp"), sem("softmax_done"))
        ptt_ready, ptt_copied, po_ready, po_copied = (sem("probs_turned"), sem("probs_turned_copied"),
                                                      sem("own_prob_spread"), sem("own_prob_copied"))
        pv_done, om_ready, oc_ready, oc_copied = sem("page_values"), sem("o_masked"), sem("o_cols"), sem("o_cols_copied")
        unit_read = sem("values_read")
        mm_ready, mm_max, mm_exp, mm_norm, mmt_ready, mmt_copied = (sem("mem_rows"), sem("mem_max"), sem("mem_exp"),
                                                                   sem("mem_norm"), sem("mem_turned"),
                                                                   sem("mem_turned_copied"))
        mpv_done, mom_ready = sem("mem_values"), sem("mem_masked")
        xm_ready, xe_ready, ch_ready, cnt_ready, rp_ready, rg_ready, rg_copied = (
            sem("router_shift"), sem("router_exp"), sem("chosen_ready"), sem("counts_ready"), sem("ranges_spread"),
            sem("ranges_turned"), sem("ranges_copied"))
        table_ready, parts_ready = sem("block_table"), sem("bias_parts_ready")
        hot_ready, hot_used, gat_ready, gat_copied = (sem("slots_hot"), sem("slots_used"), sem("gathered"),
                                                      sem("gathered_copied"))
        xgt_ready, xgt_copied, gu_ready, gu_used = (sem("gathered_turned"), sem("gathered_turned_copied"),
                                                    sem("gate_up_done"), sem("gate_up_tiles_used"))
        g_ready, sg_ready, hd_ready, hdt_ready, hdt_copied = (sem("gate_clamped"), sem("sigmoid"), sem("hidden"),
                                                              sem("hidden_turned"), sem("hidden_turned_copied"))
        gu_read = sem("gate_up_read")
        dn_ready, dn_used, dn_copied, rows_out = (sem("down_done"), sem("down_tiles_used"), sem("down_copied"),
                                                  sem("expert_rows_out"))
        step_a, step_b, step_c, step_d = sem("slot_equal"), sem("slot_id_next"), sem("block_id_next"), sem("block_at_start")
        up_ready, bias_hot_ready, table_iota = sem("up_times_gate"), sem("bias_row_hot"), sem("block_numbers")
        spare_zeroed = sem("spare_rows_zeroed")
        experts_done = sem("experts_done")
        block_stored, all_stored = sem("block_rows_stored"), sem("all_blocks_stored")
        rows_stored, conv_stored, slot_rows_ready = sem("key_value_rows_stored"), sem("conv_stored"), sem("slot_rows_ready")
        row_in_sems = [sem(f"rows_in{c}") for c in range(3)]
        row_in = sem("rows_gathered")
        y_ready, out_done = sem("y_ready"), sem("outputs_stored")
        dve_n, act_n, pool_n = Counter(sem("dve_step")), Counter(sem("act_step")), Counter(sem("pool_step"))
        fin_sq, fin_rt = sem("final_squares"), sem("final_root")
        parts_free = sem("ring_a_free")

        tiles = ([("small", i) for i in range(3)] + [("xt", k) for k in range(KC)] + [("proj", CQ + j) for j in range(4)] +
                 [("qs", 0)] + [("proj", CK + j) for j in range(8)] + [("mt", k) for k in range(KC)] +
                 [("proj", CM + j) for j in range(8)] + [("qms", 0)] + [("mkv", j) for j in range(4)] +
                 [("kr", 0), ("kr", 1), ("vr", 0), ("vr", 1), ("ks", 0), ("vs", 0), ("mr", 0), ("mr", 1)])
        tile_no = {t: i for i, t in enumerate(tiles)}
        SPREAD_AFTER = {("qs", 0): (0, 1), ("proj", CK + 3): (2,), ("mkv", 3): (3,)}
        units = [(False, h, c) for h in range(HEADS) for c in range(2)] + [(True, h, c) for h in range(MHEADS)
                                                                         for c in range(2)]
        NU = len(units)
        SPREAD_BEFORE_UNIT = {0: 4, 6: 5, 12: 6, 18: 7}
        UNITS_BEFORE_BATCH = {5: 6, 6: 12, 7: 18}

        block = ctx.enter_context(nc.Block())

        def k_src(cache, page):
            return cache[0, bass.ds(page, 1)].rearrange("a t h d -> (a t) (h d)")

        def ring_total(b):
            if b % 2 == 0:
                return 16 * PAGES * (4 + b // 2 + 1)
            return 16 * (PAGES * (4 + b // 2 + 1) + 2 * NS)

        def columns_of(pe, b):
            pe.wait_ge(om_ready, b + 1)
            for j in range(4):
                last = pe.matmul(bank[5][:, 320 + j * NS + b:321 + j * NS + b], o_masked[:, b % 2, j * PARTS:(j + 1) * PARTS],
                                 ones[:, 0:1], start=True, stop=True)
            last.then_inc(oc_ready, 1)

        def ln_square(c):
            return gate_up_w[:, 0, 0:D]

        @block.sync
        def _(sp):
            sp.dma_start(pages[:, :], page_table.rearrange("b p -> (b p)")[None, :]).then_inc(pages_in, 16)
            sp.dma_start(x_rows[:, 0:2, :], x_prompt[0].rearrange("(c p) d -> p c d", p=PARTS)).then_inc(x_in, 16)
            sp.dma_start(x_rows[0:NS, 2, :], x_sample[:, 0, :]).then_inc(x_in, 16)
            w_in_k = w_in[0].rearrange("(k p) n -> p k n", p=PARTS)
            sp.dma_start(w_in_a[:, :, 0:512], w_in_k[:, :, 0:512]).then_inc(w_q_in, 16)
            sp.dma_start(w_in_a[:, :, 512:1536], w_in_k[:, :, 512:1536]).then_inc(w_kv_in, 16)
            sp.dma_start(mem_rows, mem_prompt[0].rearrange("(c p) d -> p c d", p=PARTS)).then_inc(mem_in, 16)
            sp.dma_start(w_in_a[:, :, 1536:2048], w_in_k[:, :, 1536:2048]).then_inc(w_m_in, 16)
            sp.dma_start(w_in_b, w_in_k[:, :, 2048:2560]).then_inc(w_ch_in, 16)
            sp.dma_start(w_mem, w_mem_kv[0].rearrange("(k p) n -> p k n", p=PARTS)).then_inc(w_mem_in, 16)
            sp.wait_ge(pages_in, 16)

            def load_pages(cache, batch, half):
                with sp.Fori(0, PAGES) as g:
                    page = sp.value_load(pages[0:1, bass.ds(g + batch * PAGES, 1)], min_val=0, max_val=NPHYS - 1)
                    sp.dma_start(ring[half][:, bass.ds(g * AW, AW)], k_src(cache, page)).then_inc(ring_in[half], 16)

            load_pages(cache_k, 0, 1)
            sp.wait_ge(tile_ready, tile_no[("mkv", 3)] + 1)
            load_pages(cache_k, 1, 0)
            sp.wait_ge(tile_ready, tile_no[("mkv", 3)] + 1)
            sp.dma_start(w_o, w_out[0].rearrange("(j p) n -> p j n", p=PARTS)).then_inc(w_out_in, 16)
            sp.dma_start(ln1_gain, ln1_g[0][None, :].broadcast_to([PARTS, D])).then_inc(ln1_in, 16)
            sp.dma_start(ln1_bias, ln1_b[0][None, :].broadcast_to([PARTS, D])).then_inc(ln1_in, 16)
            for b in range(2, NS):
                sp.wait_ge(k_scored, b - 1)
                load_pages(cache_k, b, (b + 1) % 2)
            sp.wait_ge(k_scored, NS - 1)
            for i, cache in enumerate((cache_mem_k, cache_mem_v)):
                for b in range(NS):
                    sp.dma_start(RB[:, i * 4096 + b * 512:i * 4096 + (b + 1) * 512].rearrange("p (g c) -> p g c", g=2),
                                 cache[0, b].rearrange("(g p) h d -> p g (h d)", p=PARTS)).then_inc(ring_in[1], 16)
            for b in range(NS):
                if b == 0:
                    sp.wait_ge(k_scored, NS)
                elif b == 1:
                    sp.wait_ge(mpv_done, 1)
                else:
                    sp.wait_ge(unit_read, b - 1)
                load_pages(cache_v, b, b % 2)
            sp.wait_ge(unit_read, NS - 1)
            for r in range(3):
                sp.dma_start(bias_f32[r * E:(r + 1) * E, 0:2 * FF], b_gate_up[0]).then_inc(bias_in, 16)
                sp.dma_start(bias_f32[r * E:(r + 1) * E, 2 * FF:2 * FF + D], b_down[0]).then_inc(bias_in, 16)
            gu_k = w_gate_up[0].rearrange("e (k p) n -> e p k n", p=PARTS)
            dn_k = w_down[0].rearrange("e (k p) n -> e p k n", p=PARTS)
            sp.wait_ge(proj_ready, 3)
            sp.wait_ge(x1_ready, 3)
            for k in range(KC):
                sp.dma_start(gate_up_w[:, k, :], gu_k[0, :, k, :]).then_inc(gu_in[k], 16)
            sp.wait_ge(conv_stored, 16 * 4)
            for k in range(KC):
                sp.dma_start(down_w[:, k, :], dn_k[0, :, k, :]).then_inc(dn_in[k], 16)
            sp.wait_ge(unit_read, NS)
            sp.dma_start(ln2_gain, ln2_g[0][None, :].broadcast_to([PARTS, D])).then_inc(ln2_in, 16)
            sp.dma_start(ln2_bias, ln2_b[0][None, :].broadcast_to([PARTS, D])).then_inc(ln2_in, 16)
            sp.wait_ge(table_ready, 1)
            count = sp.value_load(n_blocks[0:1, 0:1], min_val=E, max_val=MAX_BLOCKS)
            with sp.Fori(1, MAX_BLOCKS) as b:
                with sp.If(b < count):
                    e = sp.value_load(block_expert[0:1, bass.ds(b, 1)], min_val=0, max_val=E - 1)
                    for k in range(KC):
                        sp.wait_ge(gu_used, (b - 1) * KC + (k + 1))
                        sp.dma_start(gate_up_w[:, k, :],
                                     gu_k[bass.ds(e, 1), :, k, :].rearrange("a p n -> (a p) n")).then_inc(gu_in[k], 16)
                    for k in range(KC):
                        sp.wait_ge(dn_used, (b - 1) * KC + (k + 1))
                        sp.dma_start(down_w[:, k, :],
                                     dn_k[bass.ds(e, 1), :, k, :].rearrange("a p n -> (a p) n")).then_inc(dn_in[k], 16)
                with sp.Else():
                    pass
            sp.wait_ge(y_ready, 2)
            sp.dma_start(y_prompt[0].rearrange("(c p) d -> p c d", p=PARTS), x_rows[:, 0:2, :]).then_inc(out_done, 16)
            sp.wait_ge(y_ready, 3)
            sp.dma_start(y_sample[:, 0, :], x_rows[0:NS, 2, :]).then_inc(out_done, 16)
            sp.wait_ge(out_done, 16 * 3)
            sp.wait_ge(rows_stored, 16 * 6)
            sp.wait_ge(conv_stored, 16 * 4)

        @block.tensor
        def _(pe):
            def tile_wait(i):
                if i >= 4:
                    pe.wait_ge(tile_copied, i - 3)

            def copied(t):
                pe.wait_ge(tile_copied, tile_no[t] + 1)

            def spread(b):
                if b >= 2:
                    pe.wait_ge(k_scored, b - 1)
                pe.wait_ge(sel_ready, 1)
                pe.matmul(bank[6 + b % 2][:, :], row_pick(b), q_new, start=True, stop=True).then_inc(qb_ready, 1)

            def row_pick(b):
                return ident[0:NS, b:b + 1].broadcast_to([NS, PARTS])

            pe.wait_ge(eye_ready, 1)
            for i, (kind, n) in enumerate(tiles):
                out = bank[i % 4]
                tile_wait(i)
                if kind == "small":
                    if n == 0:
                        pe.wait_ge(smalls_in, 48)
                        last = pe.transpose(out[:, 0:KC], stage[0:KC, 0:PARTS], ident[0:KC, 0:KC])
                    elif n == 1:
                        for j in range(2):
                            last = pe.transpose(out[:, j * 3:j * 3 + 3], stage[0:3, 256 + j * 128:384 + j * 128], ident[0:3, 0:3])
                    else:
                        for j in range(2):
                            last = pe.transpose(out[:, j * 16:j * 16 + 16], stage[0:16, 512 + j * 128:640 + j * 128],
                                                ident[0:16, 0:16])
                elif kind == "xt":
                    pe.wait_ge(x_in, 32)
                    for c in range(3):
                        rows = PARTS if c < 2 else NS
                        last = pe.transpose(out[:, c * PARTS:c * PARTS + rows],
                                            x_rows[0:rows, c, n * PARTS:(n + 1) * PARTS], ident[0:rows, 0:rows])
                elif kind == "proj":
                    pe.wait_ge(w_q_in if n < CK else w_kv_in if n < CM else w_m_in if n < CC else w_ch_in, 16)
                    copied(("xt", KC - 1))
                    for k in range(KC):
                        w = w_in_a[:, k, n * PARTS:(n + 1) * PARTS] if n < 16 else \
                            w_in_b[:, k, (n - 16) * PARTS:(n - 15) * PARTS]
                        last = pe.matmul(out[:, 0:T], w, x_cols[:, k, :], start=(k == 0), stop=(k == KC - 1))
                elif kind == "mt":
                    pe.wait_ge(mem_in, 16)
                    for c in range(2):
                        last = pe.transpose(out[:, c * PARTS:(c + 1) * PARTS],
                                            mem_rows[:, c, n * PARTS:(n + 1) * PARTS], ident[:, :])
                elif kind == "mkv":
                    pe.wait_ge(w_mem_in, 16)
                    copied(("mt", KC - 1))
                    for k in range(KC):
                        last = pe.matmul(out[:, 0:NMEM], w_mem[:, k, n * PARTS:(n + 1) * PARTS], mem_x[:, k, :],
                                         start=(k == 0), stop=(k == KC - 1))
                elif kind in ("qs", "ks", "vs", "qms"):
                    first, chunks = {"qs": (CQ, 4), "ks": (CK, 4), "vs": (CV, 4), "qms": (CM, 2)}[kind]
                    copied(("proj", first + chunks - 1))
                    for j in range(chunks):
                        last = pe.transpose(out[0:NS, j * PARTS:(j + 1) * PARTS], p_cols[:, first + j, NP:T], ident[:, :])
                else:
                    copied(("mkv", 3))
                    for j in range(4):
                        src = mem_cols[:, j, n * PARTS:(n + 1) * PARTS] if kind == "mr" else \
                            p_cols[:, (CK if kind == "kr" else CV) + j, n * PARTS:(n + 1) * PARTS]
                        last = pe.transpose(out[:, j * PARTS:(j + 1) * PARTS], src, ident[:, :])
                last.then_inc(tile_ready, 1)
                for b in SPREAD_AFTER.get((kind, n), ()):
                    copied(("qs", 0))
                    spread(b)

            pe.wait_ge(tile_copied, len(tiles))
            for i in range(NU + 2):
                if i in SPREAD_BEFORE_UNIT:
                    spread(SPREAD_BEFORE_UNIT[i])
                if i < NU:
                    mem, h, c = units[i]
                    p = HD * (h % 2)
                    keys = NMEM if mem else PARTS * (c + 1)
                    out = bank[i % 2][:, 0:keys]
                    if i >= 2:
                        pe.wait_ge(exp_done, i - 1)
                    q = p_cols[p:p + HD, (CM if mem else CQ) + h // 2, c * PARTS:(c + 1) * PARTS]
                    k = mem_cols[p:p + HD, h // 2, :] if mem else p_cols[p:p + HD, CK + h // 2, 0:keys]
                    last = pe.matmul(out, q, k, start=True, stop=mem)
                    if not mem:
                        if i == 0:
                            pe.wait_ge(eyes_ready, 1)
                        last = pe.matmul(out, head_slope_eye[:, h, :], dist[:, PARTS * (1 - c):], start=False, stop=True)
                    last.then_inc(sc_ready, 1)
                if 1 <= i <= NU:
                    n = i - 1
                    mem, h, c = units[n]
                    pe.wait_ge(norm_done, n + 1)
                    if n >= 2:
                        pe.wait_ge(pt_copied, n - 1)
                    for g in range(2 if mem else c + 1):
                        last = pe.transpose(bank[2 + n % 2][:, g * PARTS:(g + 1) * PARTS],
                                            probs[:, n % 2, g * PARTS:(g + 1) * PARTS], ident[:, :])
                    last.then_inc(pt_ready, 1)
                if 2 <= i:
                    n = i - 2
                    mem, h, c = units[n]
                    p = HD * (h % 2)
                    pe.wait_ge(pt_copied, n + 1)
                    if n >= 2:
                        pe.wait_ge(o_copied, n - 1)
                    groups = 2 if mem else c + 1
                    for g in range(groups):
                        v = mkv_rows[:, g, MW + h * HD:MW + (h + 1) * HD] if mem else v_rows[:, g, h * HD:(h + 1) * HD]
                        last = pe.matmul(bank[4 + n % 2][p:p + HD, 0:PARTS], v, probs_t[:, n % 2, g * PARTS:(g + 1) * PARTS],
                                         start=(g == 0), stop=(g == groups - 1))
                    last.then_inc(pv_ready, 1)

            copied(("qms", 0))
            for b in range(NS):
                if b >= 4 and b % 2 == 0:
                    pe.wait_ge(k_scored, NS + b // 2 - 1)
                elif b == 0:
                    pe.wait_ge(k_scored, NS - 1)
                elif b == 2:
                    pe.wait_ge(k_scored, NS)
                last = pe.matmul(bank[6 + (b // 2) % 2][:, (b % 2) * MW:(b % 2 + 1) * MW], row_pick(b), qm_new,
                                 start=True, stop=True)
                if b % 2:
                    last.then_inc(qb_ready, 1)

            pe.wait_ge(o_copied, NU)
            pe.wait_ge(sq_ready, 1)
            sections = ((OATT, 4, bank[4][:, 0:NP]), (OCONV, 2, bank[4][:, NP:2 * NP]), (OMEM, 2, bank[5][:, 0:NP]))
            for first, n, out in sections:
                for j in range(n):
                    last = pe.matmul(out, ones, squares[:, first + j, :], start=(j == 0), stop=(j == n - 1))
            last.then_inc(ss_ready, 1)

            def out_proj(c, banks):
                rows = PARTS if c < 2 else NS
                for half in range(2):
                    for j in range(KC):
                        last = pe.matmul(banks[half][0:rows, :], o_cols[:, j, c * PARTS:c * PARTS + rows],
                                         w_o[:, j, half * HALF:(half + 1) * HALF], start=(j == 0), stop=(j == KC - 1))
                last.then_inc(proj_ready, 1)

            pe.wait_ge(mix_ready, 1)
            pe.wait_ge(w_out_in, 16)
            out_proj(0, bank[0:2])
            out_proj(1, bank[2:4])

            pe.wait_ge(k_scored, NS + 4)
            pe.wait_ge(ri_ready, 1)
            for g in range(2):
                last = pe.transpose(bank[5][0:MROWS, g * PARTS:(g + 1) * PARTS], mem_scores[:, g, :], ident[:, :])
            last.then_inc(mm_ready, 1)
            pe.wait_ge(so_ready, 1)
            pe.matmul(bank[4][0:ROWS, 0:1], so_spread, ones[0:NS, 0:1], start=True, stop=True).then_inc(own_ready, 1)
            pe.wait_ge(res_ready, 2)
            for g in range(PAGES):
                last = pe.transpose(bank[g // 4][0:ROWS, (g % 4) * PARTS:(g % 4 + 1) * PARTS], scores[:, g, :], ident[:, :])
            last.then_inc(l_ready, 1)
            pe.wait_ge(mm_norm, 1)
            for g in range(2):
                last = pe.transpose(bank[6][:, g * MROWS:(g + 1) * MROWS], probs[0:MROWS, 0, g * PARTS:(g + 1) * PARTS],
                                    ident[0:MROWS, 0:MROWS])
            last.then_inc(mmt_ready, 1)
            pe.wait_ge(mmt_copied, 1)
            pe.wait_ge(ring_in[1], 16 * (4 * PAGES + 2 * NS))
            for b in range(NS):
                grp, q = b % 4, b // 4
                for g in range(2):
                    last = pe.matmul(bank[7][32 * grp:32 * grp + 32, q * MW:(q + 1) * MW], mem_pt[:, g, :],
                                     RB[:, 4096 + b * 512 + g * MW:4096 + b * 512 + (g + 1) * MW],
                                     start=(g == 0), stop=(g == 1))
            last.then_inc(mpv_done, 1)
            pe.wait_ge(mom_ready, 1)
            for q in range(2):
                for j in range(2):
                    last = pe.matmul(bank[5][:, 256 + j * NS + 4 * q:256 + j * NS + 4 * q + 4],
                                     mem_masked[:, q, j * PARTS:(j + 1) * PARTS], grp_sel, start=True, stop=True)
            pe.wait_ge(sm_p, 1)
            for g in range(PAGES):
                last = pe.transpose(bank[2 + g // 8][:, (g % 8) * ROWS:(g % 8 + 1) * ROWS],
                                    logits[:, g * PARTS:(g + 1) * PARTS], ident[0:ROWS, 0:ROWS])
            last.then_inc(ptt_ready, 1)
            pe.matmul(bank[4][0:NS, 0:ROWS], po_spread, ident[0:ROWS, 0:ROWS], start=True, stop=True).then_inc(po_ready, 1)
            pe.wait_ge(ptt_copied, 2)
            pe.wait_ge(po_copied, 1)
            for b in range(NS):
                out = bank[6 + b % 2]
                cols = slice(32 * (b // 4), 32 * (b // 4) + 32)
                if b >= 2:
                    pe.wait_ge(om_ready, b - 1)
                pe.wait_ge(ring_in[b % 2], ring_total(b))
                for g in range(PAGES):
                    grp = g % 4
                    last = pe.matmul(out[32 * grp:32 * grp + 32, :], scores[:, g, cols],
                                     ring[b % 2][:, g * AW:(g + 1) * AW], start=(g < 4), stop=(g >= PAGES - 4 and grp > 0))
                last.then_inc(unit_read, 1)
                pe.matmul(out[0:32, :], po_new[:, cols], v_new, start=False, stop=True).then_inc(pv_done, 1)
                if b >= 1:
                    columns_of(pe, b - 1)
            columns_of(pe, NS - 1)

            pe.wait_ge(sq_ready, 2)
            for s, (first, n) in enumerate(((OATT, 4), (OCONV, 2), (OMEM, 2))):
                for j in range(n):
                    last = pe.matmul(bank[4][:, 256 + s * NS:256 + (s + 1) * NS], ones, sq_s[:, first + j, :],
                                     start=(j == 0), stop=(j == n - 1))
            last.then_inc(ss_ready, 1)
            pe.wait_ge(mix_ready, 2)
            out_proj(2, bank[0:2])

            for c in range(3):
                rows = PARTS if c < 2 else NS
                pe.wait_ge(x1_ready, c + 1)
                for k in range(KC):
                    last = pe.transpose(bank[2 + k // 4][:, (k % 4) * PARTS:(k % 4) * PARTS + rows],
                                        x_rows[0:rows, c, k * PARTS:(k + 1) * PARTS], ident[0:rows, 0:rows])
                    if k % 4 == 3:
                        last.then_inc(x1t_ready, 1)
                pe.wait_ge(x1t_copied, 2 * (c + 1))
                if c == 0:
                    pe.wait_ge(router_in, 32)
                for k in range(KC):
                    last = pe.matmul(bank[5][0:rows, c * E:(c + 1) * E], o_cols[:, k, c * PARTS:c * PARTS + rows],
                                     w_r[:, k, :], start=(k == 0), stop=(k == KC - 1))
                last.then_inc(lg_ready, 1)
            pe.wait_ge(ch_ready, 1)
            c0, c1, c2 = chosen[:, 0, :], chosen[:, 1, :], chosen[0:NS, 2, :]
            ranks, counts = bank[6], bank[6][:, 3 * E:4 * E]
            pe.matmul(ranks[:, 0:E], tri, c0, start=True, stop=True)
            pe.matmul(ranks[:, E:2 * E], ones, c0, start=True, stop=False)
            pe.matmul(ranks[:, E:2 * E], tri, c1, start=False, stop=True)
            pe.matmul(ranks[0:NS, 2 * E:3 * E], ones[:, 0:NS], c0, start=True, stop=False)
            pe.matmul(ranks[0:NS, 2 * E:3 * E], ones[:, 0:NS], c1, start=False, stop=False)
            pe.matmul(ranks[0:NS, 2 * E:3 * E], tri[0:NS, 0:NS], c2, start=False, stop=True)
            pe.matmul(counts, ones, c0, start=True, stop=False)
            pe.matmul(counts, ones, c1, start=False, stop=False)
            pe.matmul(counts, ones[0:NS, :], c2, start=False, stop=True).then_inc(cnt_ready, 1)
            pe.wait_ge(rp_ready, 1)
            for a in range(2):
                last = pe.transpose(bank[7][0:3 * E, a * PARTS:(a + 1) * PARTS],
                                    rep3[:, a].rearrange("p r e -> p (r e)"), ident[:, :])
            last.then_inc(rg_ready, 1)

            p_gate, p_up, p_gather, p_hid_t, p_x_t, p_down = bank[0:6]

            def gather(b_next):
                pe.wait_ge(hot_ready, b_next)
                for half in range(2):
                    for c in range(3):
                        rows = PARTS if c < 2 else NS
                        last = pe.matmul(p_gather[half * SLOTS:(half + 1) * SLOTS, :], slot_hot[0:rows, c, :],
                                         x_rows[0:rows, c, half * HALF:(half + 1) * HALF], start=(c == 0), stop=(c == 2))
                last.then_inc(gat_ready, 1)

            def turn_gathered(b_next):
                pe.wait_ge(gat_copied, b_next)
                for j in range(4):
                    last = pe.transpose(p_x_t[:, j * PARTS:(j + 1) * PARTS], xg[:, j * PARTS:(j + 1) * PARTS], ident[:, :])
                last.then_inc(xgt_ready, 1)

            gather(1)
            turn_gathered(1)
            pe.wait_ge(table_ready, 1)
            pe.wait_ge(parts_ready, 1)
            count = pe.value_load(n_blocks[0:1, 0:1], min_val=E, max_val=MAX_BLOCKS)
            with pe.Fori(0, MAX_BLOCKS) as b:
                with pe.If(b < count):
                    pe.wait_ge(xgt_copied, b + 1)
                    pe.wait_ge(bias_hot_ready, b + 1)
                    for half in range(2):
                        rows = slice(half * SLOTS, (half + 1) * SLOTS)
                        for out, at_col in ((p_gate, half * HALF), (p_up, FF + half * HALF)):
                            pe.matmul(out[rows, :], bias_hot, bias_parts[:, at_col:at_col + HALF], start=True, stop=False)
                    for k in range(KC):
                        pe.wait_ge(gu_in[k], 16 * b + 16)
                        for half in range(2):
                            rows = slice(half * SLOTS, (half + 1) * SLOTS)
                            for out, at_col in ((p_gate, half * HALF), (p_up, FF + half * HALF)):
                                last = pe.matmul(out[rows, :], xg_t[:, k % 4, k // 4, :],
                                                 gate_up_w[:, k, at_col:at_col + HALF], start=False, stop=(k == KC - 1))
                        last.then_inc(gu_used, 1)
                    pe.wait_ge(dn_copied, b + 1)
                    for half in range(2):
                        last = pe.matmul(p_down[half * SLOTS:(half + 1) * SLOTS, :], bias_hot,
                                         bias_parts[:, 2 * FF + half * HALF:2 * FF + (half + 1) * HALF],
                                         start=True, stop=False)
                    last.then_inc(hot_used, 1)
                    gather(b + 2)
                    pe.wait_ge(hd_ready, b + 1)
                    for j in range(4):
                        last = pe.transpose(p_hid_t[:, j * PARTS:(j + 1) * PARTS], hid[:, j * PARTS:(j + 1) * PARTS],
                                            ident[:, :])
                    last.then_inc(hdt_ready, 1)
                    turn_gathered(b + 2)
                    pe.wait_ge(hdt_copied, b + 1)
                    for k in range(KC):
                        pe.wait_ge(dn_in[k], 16 * b + 16)
                        for half in range(2):
                            last = pe.matmul(p_down[half * SLOTS:(half + 1) * SLOTS, :], hid_t[:, k % 4, k // 4, :],
                                             down_w[:, k, half * HALF:(half + 1) * HALF], start=False, stop=(k == KC - 1))
                        last.then_inc(dn_used, 1)
                with pe.Else():
                    pass
            pe.sem_inc(experts_done, 1)

        @block.scalar
        def _(act):
            def step(instruction):
                act.wait_ge(act_n.sem, act_n.on(instruction))

            act.dma_start(stage[0:KC, 0:PARTS], g_mix[0].rearrange("(j p) -> j p", p=PARTS)).then_inc(smalls_in, 16)
            act.dma_start(stage[0:3, 256:512], w_conv[0]).then_inc(smalls_in, 16)
            act.dma_start(stage[0:2 * NS, 512:768], state_conv[0].rearrange("b r c -> (b r) c")).then_inc(smalls_in, 16)
            act.dma_start(conv_sample[0, :, 0, :], state_conv[0, :, 1, :]).then_inc(out_done, 16)
            for i, (kind, n) in enumerate(tiles):
                src = bank[i % 4]
                act.wait_ge(tile_ready, i + 1)
                scale = 1.0
                if kind == "small":
                    dst, src = ((g_cols, src[:, 0:KC]), (w_cols, src[:, 0:6].rearrange("p (j i) -> p j i", j=2)),
                                (s_cols, src[:, 0:32].rearrange("p (j b r) -> p j b r", j=2, b=NS)))[n]
                elif kind == "xt":
                    dst, src = x_cols[:, n, :], src[:, 0:T]
                elif kind == "proj":
                    dst, src = p_cols[:, n, :], src[:, 0:T]
                    if n < CK or CM <= n < CB:
                        scale = QSCALE
                elif kind == "mt":
                    dst, src = mem_x[:, n, :], src[:, 0:NMEM]
                elif kind == "mkv":
                    dst, src = mem_cols[:, n, :], src[:, 0:NMEM]
                elif kind in ("qs", "ks", "vs"):
                    dst, src = {"qs": q_new, "ks": k_new, "vs": v_new}[kind], src[0:NS, :]
                elif kind == "qms":
                    dst, src = qm_new, src[0:NS, 0:MW]
                else:
                    dst = {"kr": k_rows, "vr": v_rows, "mr": mkv_rows}[kind][:, n, :]
                act.activation(dst, src, ACT.Copy, scale=scale).then_inc(tile_copied, 1)

            act.wait_ge(tile_copied, len(tiles))
            rows_of = lambda t: t.rearrange("(c p) h d -> p c (h d)", p=PARTS)
            act.dma_start(rows_of(k_prompt[0, 0]), k_rows).then_inc(rows_stored, 16)
            act.dma_start(rows_of(v_prompt[0, 0]), v_rows).then_inc(rows_stored, 16)
            act.dma_start(rows_of(mem_k_prompt[0, 0]), mkv_rows[:, :, 0:MW]).then_inc(rows_stored, 16)
            act.dma_start(rows_of(mem_v_prompt[0, 0]), mkv_rows[:, :, MW:2 * MW]).then_inc(rows_stored, 16)
            act.dma_start(k_sample[0, :, 0].rearrange("b h d -> b (h d)"), k_new).then_inc(rows_stored, 16)
            act.dma_start(v_sample[0, :, 0].rearrange("b h d -> b (h d)"), v_new).then_inc(rows_stored, 16)

            for i in range(NU + 3):
                if i < NU:
                    mem, h, c = units[i]
                    keys = NMEM if mem else PARTS * (c + 1)
                    act.wait_ge(mx_ready, i + 1)
                    if i >= 2:
                        act.wait_ge(pt_ready, i - 1)
                    act.activation(probs[:, i % 2, 0:keys], bank[i % 2][:, 0:keys], ACT.Exp, bias=neg_max[:, i % 2:i % 2 + 1],
                                   accum_out=row_sum[:, i % 2:i % 2 + 1]).then_inc(exp_done, 1)
                if 1 <= i <= NU:
                    n = i - 1
                    mem, h, c = units[n]
                    keys = NMEM if mem else PARTS * (c + 1)
                    act.wait_ge(inv_ready, n + 1)
                    act.activation(probs[:, n % 2, 0:keys], probs[:, n % 2, 0:keys], ACT.Copy,
                                   scale=row_inv[:, n % 2:n % 2 + 1]).then_inc(norm_done, 1)
                if 2 <= i <= NU + 1:
                    n = i - 2
                    mem, h, c = units[n]
                    keys = NMEM if mem else PARTS * (c + 1)
                    act.wait_ge(pt_ready, n + 1)
                    if n >= 2:
                        act.wait_ge(pv_ready, n - 1)
                    act.activation(probs_t[:, n % 2, 0:keys], bank[2 + n % 2][:, 0:keys], ACT.Copy).then_inc(pt_copied, 1)
                if 3 <= i:
                    n = i - 3
                    mem, h, c = units[n]
                    p = HD * (h % 2)
                    act.wait_ge(pv_ready, n + 1)
                    act.activation(o_cols[p:p + HD, (OMEM if mem else OATT) + h // 2, c * PARTS:(c + 1) * PARTS],
                                   bank[4 + n % 2][p:p + HD, 0:PARTS], ACT.Copy).then_inc(o_copied, 1)

            act.wait_ge(ss_ready, 1)
            act.wait_ge(const_ready, 1)
            act.activation(rms_p[:, 0, :], bank[4][:, 0:NP], ACT.Sqrt, bias=eps, scale=1.0 / AW)
            act.activation(rms_p[:, 1, :], bank[4][:, NP:2 * NP], ACT.Sqrt, bias=eps, scale=1.0 / MW)
            act.activation(probs_t[:, 0, :], bank[5][:, 0:NP], ACT.Sqrt, bias=eps, scale=1.0 / MW).then_inc(rt_ready, 1)

            def layernorm_root(n, rows, c):
                act.wait_ge(res_ready, n)
                act.activation(ln_square(c)[0:rows], x_rows[0:rows, c, :], ACT.Square,
                               accum_out=ln_s[0:rows, c, 3:4]).then_inc(var_ready, 1)
                act.wait_ge(var_ready, n)
                act.activation(ln_s[0:rows, c, 4:5], ln_s[0:rows, c, 3:4], ACT.Sqrt, bias=eps[0:rows], scale=1.0 / D)\
                   .then_inc(root_ready, 1)

            layernorm_root(1, PARTS, 0)
            layernorm_root(2, PARTS, 1)
            act.wait_ge(mm_max, 1)
            act.activation(probs[0:MROWS, 0, :], bank[5][0:MROWS, 0:NMEM], ACT.Exp, bias=mstat[:, 0:1],
                           accum_out=mstat[:, 1:2]).then_inc(mm_exp, 1)
            act.wait_ge(mmt_ready, 1)
            act.activation(mem_pt, bank[6][:, 0:2 * MROWS].rearrange("p (g r) -> p g r", g=2), ACT.Copy)\
               .then_inc(mmt_copied, 1)
            act.wait_ge(sm_max, 1)
            act.activation(logits, logits, ACT.Exp, bias=stat[:, 2:3], accum_out=stat[:, 3:4]).then_inc(sm_exp, 1)
            act.activation(stat[:, 4:5], own, ACT.Exp, bias=stat[:, 2:3]).then_inc(sm_exp, 1)
            act.wait_ge(ptt_ready, 1)
            for i in range(2):
                act.activation(scores[:, 8 * i:8 * i + 8, :], bank[2 + i][:, :].rearrange("p (g r) -> p g r", g=8), ACT.Copy)\
                   .then_inc(ptt_copied, 1)
            act.wait_ge(po_ready, 1)
            act.activation(po_new, bank[4][0:NS, 0:ROWS], ACT.Copy).then_inc(po_copied, 1)
            act.wait_ge(oc_ready, NS)
            act.activation(o_cols[:, OATT:OATT + 4, NP:T], bank[5][:, 320:320 + 4 * NS].rearrange("p (j b) -> p j b", j=4),
                           ACT.Copy).then_inc(oc_copied, 1)
            act.activation(o_cols[:, OMEM:OMEM + 2, NP:T], bank[5][:, 256:256 + 2 * NS].rearrange("p (j b) -> p j b", j=2),
                           ACT.Copy).then_inc(oc_copied, 1)
            act.wait_ge(ss_ready, 2)
            act.activation(rms_s[:, 0:NS], bank[4][:, 256:256 + NS], ACT.Sqrt, bias=eps, scale=1.0 / AW)
            act.activation(rms_s[:, NS:3 * NS], bank[4][:, 256 + NS:256 + 3 * NS], ACT.Sqrt, bias=eps, scale=1.0 / MW)\
               .then_inc(rt_ready, 1)
            for c in range(2):
                for i in range(2):
                    act.wait_ge(x1t_ready, 2 * c + i + 1)
                    act.activation(o_cols[:, 4 * i:4 * i + 4, c * PARTS:(c + 1) * PARTS],
                                   bank[2 + i][:, :].rearrange("p (k t) -> p k t", k=4), ACT.Copy).then_inc(x1t_copied, 1)
            layernorm_root(3, NS, 2)
            for i in range(2):
                act.wait_ge(x1t_ready, 5 + i)
                act.activation(o_cols[:, 4 * i:4 * i + 4, NP:T],
                               bank[2 + i][:, :].rearrange("p (k t) -> p k t", k=4)[:, :, 0:NS], ACT.Copy)\
                   .then_inc(x1t_copied, 1)
            act.wait_ge(xm_ready, 1)
            act.activation(w4, w4, ACT.Exp).then_inc(xe_ready, 1)
            act.wait_ge(rg_ready, 1)
            act.activation(range96[:, 0:1], bank[7][0:3 * E, 0:1], ACT.Copy)
            act.activation(range96[:, 1:2], bank[7][0:3 * E, PARTS:PARTS + 1], ACT.Copy).then_inc(rg_copied, 1)

            def copy_gathered(n):
                act.wait_ge(gat_ready, n)
                act.activation(xg, bank[2][:, :], ACT.Copy).then_inc(gat_copied, 1)

            def copy_turned(n):
                act.wait_ge(xgt_ready, n)
                act.activation(xg_t.rearrange("p j h s -> p (j h s)"), bank[4][:, :], ACT.Copy).then_inc(xgt_copied, 1)

            copy_gathered(1)
            copy_turned(1)
            act.wait_ge(table_ready, 1)
            count = act.value_load(n_blocks[0:1, 0:1], min_val=E, max_val=MAX_BLOCKS)
            act.sem_inc(dn_copied, 1)
            rows_dst = expert_rows.rearrange("(b s) d -> b s d", s=SLOTS)
            act.wait_ge(spare_zeroed, 16)
            with act.Fori(0, MAX_BLOCKS) as b:
                with act.If(b < count):
                    act.wait_ge(g_ready, b + 1)
                    act.activation(sig_v, gate_v, ACT.Sigmoid, scale=SW_ALPHA).then_inc(sg_ready, 1)
                    copy_gathered(b + 2)
                    act.wait_ge(hdt_ready, b + 1)
                    act.activation(hid_t.rearrange("p j h s -> p (j h s)"), bank[3][:, :], ACT.Copy).then_inc(hdt_copied, 1)
                    copy_turned(b + 2)
                    act.wait_ge(dn_used, b * KC + KC)
                    act.activation(out_rows, bank[5][:, :], ACT.Copy).then_inc(dn_copied, 1)
                    act.wait_ge(dn_copied, b + 2)
                    for half in range(2):
                        act.dma_start(rows_dst[bass.ds(b, 1), :, half * HALF:(half + 1) * HALF].rearrange("a s d -> (a s) d"),
                                      out_rows[half * SLOTS:(half + 1) * SLOTS, :]).then_inc(rows_out, 16)
                    act.wait_ge(rows_out, b * 32 + 32)
                    act.sem_inc(block_stored, 1)
                with act.Else():
                    pass
            act.sem_inc(all_stored, 1)
            for c in range(3):
                rows = PARTS if c < 2 else NS
                act.wait_ge(fin_sq, c + 1)
                act.activation(gathered[0:rows, 12 + c, :], x_rows[0:rows, c, :], ACT.Square,
                               accum_out=ln_s[0:rows, c, 3:4]).then_inc(fin_rt, 1)
                act.wait_ge(fin_rt, 2 * c + 1)
                act.activation(ln_s[0:rows, c, 4:5], ln_s[0:rows, c, 3:4], ACT.Sqrt, bias=eps[0:rows], scale=1.0 / D)\
                   .then_inc(fin_rt, 1)

        @block.gpsimd
        def _(pool):
            def step(instruction):
                pool.wait_ge(pool_n.sem, pool_n.on(instruction))

            def iota(dst, pattern, base=0, cm=0):
                return pool.iota(dst, pattern, base=base, channel_multiplier=cm, allow_small_or_imprecise_dtypes=True)

            step(pool.memset(ident, 0.0))
            pool.affine_select(ident, ident, [[-1, PARTS]], ALU.not_equal, 1.0, base=0, channel_multiplier=1)\
                .then_inc(eye_ready, 1)
            pool.iota(rowi[:, 0:1], [[1, 1]], base=0, channel_multiplier=1).then_inc(rowi_ready, 1)
            pool.memset(ones, 1.0)
            step(pool.memset(tri, 1.0))
            step(pool.affine_select(tri, tri, [[1, PARTS]], ALU.is_ge, 0.0, base=-1, channel_multiplier=-1))
            pool.memset(eps, EPS)
            iota(iota8, [[1, 8]])
            iota(head_mask, [[1, HEADS], [0, HD]])
            for h in range(HEADS):
                pool.memset(slope8[:, h:h + 1], 2.0 ** (-8.0 * (h + 1) / HEADS))
            step(iota(dist, [[-1, 2 * PARTS]], base=PARTS, cm=1))
            step(pool.affine_select(dist, dist, [[-1, 2 * PARTS]], ALU.is_ge, BIG, base=PARTS, channel_multiplier=1))
            step(pool.memset(delta8, 1.0))
            step(pool.affine_select(delta8, delta8, [[1, NS], [0, HEADS]], ALU.is_equal, 0.0, base=0, channel_multiplier=-1))
            pool.memset(lg.rearrange("p c e -> p (c e)"), 0.0)
            iota(iota32, [[1, E]])
            iota(slot_id, [[1, SLOTS]]).then_inc(const_ready, 1)
            pool.wait_ge(const_ready, 1)

            pool.wait_ge(tile_copied, len(tiles))
            for h in range(HEADS):
                last = pool.tensor_scalar(head_slope_eye[:, h, :], ident, -2.0 ** (-8.0 * (h + 1) / HEADS), None, ALU.mult)
            last.then_inc(eyes_ready, 1)
            iota(logits, [[1, PAST]], base=-PAST).then_inc(logits_iota, 1)

            u = p_cols[:, CC:CC + 2, :]
            step(pool.tensor_tensor(u, u, p_cols[:, CH:CH + 2, :], ALU.mult))
            pool.sem_inc(conv_u, 1)
            for j in range(2):
                o = o_cols[:, OCONV + j, 0:NP]
                t = p_cols[:, CH + j, 0:NP]
                step(pool.tensor_scalar(o, u[:, j, 0:NP], w_cols[:, j, 2:3], None, ALU.mult))
                for back in (1, 2):
                    step(pool.tensor_scalar(t[:, 0:NP - back], u[:, j, 0:NP - back], w_cols[:, j, 2 - back:3 - back], None,
                                            ALU.mult))
                    step(pool.tensor_tensor(o[:, back:NP], o[:, back:NP], t[:, 0:NP - back], ALU.add))
                step(pool.tensor_tensor(o, o, p_cols[:, CB + j, 0:NP], ALU.mult))
                so_, ts = o_cols[:, OCONV + j, NP:T], c_s[:, 0, j, :]
                step(pool.tensor_scalar(so_, u[:, j, NP:T], w_cols[:, j, 2:3], None, ALU.mult))
                for back in (1, 2):
                    step(pool.tensor_scalar(ts, s_cols[:, j, :, 2 - back], w_cols[:, j, 2 - back:3 - back], None, ALU.mult))
                    step(pool.tensor_tensor(so_, so_, ts, ALU.add))
                step(pool.tensor_tensor(so_, so_, p_cols[:, CB + j, NP:T], ALU.mult))
            for j in range(2):
                cols = slice(j * PARTS, (j + 1) * PARTS)
                with nc.allow_non_contiguous_dma(reason="two rows of the convolution state"):
                    pool.dma_start(conv_prompt[0, 0][:, cols].rearrange("r p -> p r"), u[:, j, NP - 2:NP]).then_inc(conv_stored, 16)
                    pool.dma_start(conv_sample[0, :, 1, cols].rearrange("b p -> p b"), u[:, j, NP:T]).then_inc(conv_stored, 16)

            pool.wait_ge(o_copied, NU)
            pool.wait_ge(pv_ready, NU)
            pool.tensor_tensor(squares, o_cols[:, :, 0:NP], o_cols[:, :, 0:NP], ALU.mult).then_inc(sq_ready, 1)
            pool.wait_ge(sq_ready, 1)
            for j in range(KC):
                step(pool.tensor_scalar(o_cols[:, j, 0:NP], o_cols[:, j, 0:NP], g_cols[:, j:j + 1], None, ALU.mult))
            pool.wait_ge(ri_ready, 1)
            for first, n, r in ((OATT, 4, rms_p[:, 0, :]), (OCONV, 2, rms_p[:, 1, :]), (OMEM, 2, probs_t[:, 0, :])):
                for j in range(first, first + n):
                    last = pool.tensor_tensor(o_cols[:, j, 0:NP], o_cols[:, j, 0:NP], r, ALU.mult)
            last.then_inc(mix_ready, 1)
            pool.wait_ge(oc_copied, 2)
            pool.tensor_tensor(sq_s, o_cols[:, :, NP:T], o_cols[:, :, NP:T], ALU.mult).then_inc(sq_ready, 1)
            pool.wait_ge(sq_ready, 2)
            for j in range(KC):
                step(pool.tensor_scalar(o_cols[:, j, NP:T], o_cols[:, j, NP:T], g_cols[:, j:j + 1], None, ALU.mult))
            pool.wait_ge(ri_ready, 2)
            for first, n, s in ((OATT, 4, 0), (OCONV, 2, 1), (OMEM, 2, 2)):
                for j in range(first, first + n):
                    last = pool.tensor_tensor(o_cols[:, j, NP:T], o_cols[:, j, NP:T], rms_s[:, s * NS:(s + 1) * NS], ALU.mult)
            last.then_inc(mix_ready, 1)

            pool.wait_ge(unit_read, NS - 1)
            step(pool.memset(zero_rows, 0.0))
            spare = MAX_BLOCKS - E
            pool.dma_start(expert_rows[E * SLOTS:, :].rearrange("(c p) d -> p c d", p=PARTS),
                           zero_rows.unsqueeze(1).broadcast_to([PARTS, spare * SLOTS // PARTS, D])).then_inc(spare_zeroed, 16)
            pool.wait_ge(rows_stored, 16 * 6)
            iota(block_iota, [[1, MAX_BLOCKS + 1]]).then_inc(table_iota, 1)
            with nc.allow_non_contiguous_dma(reason="rows of 128 bytes"):
                pool.dma_start(w_r, w_router[0].rearrange("(k p) e -> p k e", p=PARTS)).then_inc(router_in, 16)
            pool.dma_start(br_row, b_router[0][None, :].broadcast_to([PARTS, E])).then_inc(router_in, 16)
            pool.wait_ge(bias_in, 16 * 6)
            W = 2 * FF + D
            for part in range(3):
                rows = slice(part * E, (part + 1) * E)
                left, piece = bias_f32[rows], bias_parts[rows]
                for i in range(part):
                    step(pool.tensor_copy(piece, left))
                    step(pool.tensor_tensor(left, left, piece, ALU.subtract))
                step(pool.tensor_copy(piece, left))
            pool.sem_inc(parts_ready, 1)

            pool.wait_ge(table_ready, 1)
            pool.wait_ge(slot_rows_ready, 1)
            pool.wait_ge(all_stored, 1)
            for c in range(3):
                rows = PARTS if c < 2 else NS
                for k in range(TOPK):
                    pool.indirect_dma_start(gathered[0:rows, c * TOPK + k, :], None, expert_rows,
                                            bass.IndirectOffsetOnAxis(ap=slot_rows[0:rows, c, k:k + 1], axis=0),
                                            bounds_check=MAX_BLOCKS * SLOTS - 1).then_inc(row_in_sems[c], 16)

        @block.vector
        def _(dve):
            def step(instruction):
                dve.wait_ge(dve_n.sem, dve_n.on(instruction))

            dve.wait_ge(rowi_ready, 1)
            step(dve.tensor_scalar(rowi[:, 1:2], rowi[:, 0:1], HEADS - 1, None, ALU.bitwise_and))
            step(dve.tensor_scalar(rowi[:, 2:3], rowi[:, 0:1], 3, 3, ALU.logical_shift_right, ALU.bitwise_and))
            step(dve.tensor_scalar(rowi[:, 3:4], rowi[:, 0:1], 5, None, ALU.logical_shift_right))
            step(dve.tensor_scalar(rowi[:, 4:5], rowi[:, 0:1], 3, None, ALU.bitwise_and))
            step(dve.tensor_scalar(rowi[:, 5:6], rowi[:, 0:1], 2, 7, ALU.logical_shift_right, ALU.bitwise_and))
            step(dve.tensor_scalar(rowi[:, 6:7], rowi[:, 0:1], 3, None, ALU.logical_shift_right))
            step(dve.tensor_copy(row_f[:, 0:7], rowi[:, 0:7]))
            dve.wait_ge(const_ready, 1)
            step(dve.tensor_scalar(head_mask, head_mask, row_f[:, 1:2], None, ALU.is_equal))
            step(dve.tensor_scalar(hot8, iota8, row_f[:, 1:2], None, ALU.is_equal))
            step(dve.tensor_tensor(slope8, slope8, hot8, ALU.mult))
            step(dve.tensor_reduce(slope, slope8, AX.X, ALU.add))
            step(dve.tensor_scalar(row_sel, iota8[:, 0:4], row_f[:, 2:3], None, ALU.is_equal))
            step(dve.tensor_scalar(grp_sel, iota8[:, 0:4], row_f[:, 3:4], None, ALU.is_equal))
            step(dve.tensor_scalar(q_sel, iota8[:, 0:2], 4.0, row_f[:, 3:4], ALU.mult, ALU.add))
            step(dve.tensor_scalar(q_sel, q_sel, row_f[:, 5:6], None, ALU.is_equal))
            step(dve.tensor_scalar(dsel, iota8[0:ROWS], row_f[0:ROWS, 6:7], None, ALU.is_equal))
            dve.sem_inc(sel_ready, 1)

            def key_batch(b):
                half = (b + 1) % 2
                r = ring[half][:, :].rearrange("p (g n) -> p g n", g=PAGES)
                dve.wait_ge(ring_in[half], 16 * PAGES * (b // 2 + 1))
                dve.wait_ge(qb_ready, b + 1)
                q = bank[6 + b % 2][:, :].unsqueeze(1).broadcast_to([PARTS, PAGES, AW])
                step(dve.tensor_tensor(r, r, q, ALU.mult))
                dve.tensor_reduce(scores[:, :, b * HEADS:(b + 1) * HEADS],
                                  ring[half][:, :].rearrange("p (g h d) -> p g h d", g=PAGES, h=HEADS),
                                  AX.X, ALU.add).then_inc(k_scored, 1)

            def unit_steps(a, z):
                for i in range(a, z):
                    if i < NU:
                        mem, h, c = units[i]
                        keys = NMEM if mem else PARTS * (c + 1)
                        dve.wait_ge(sc_ready, i + 1)
                        if i >= 2:
                            dve.wait_ge(exp_done, i - 1)
                        dve.tensor_reduce(neg_max[:, i % 2:i % 2 + 1], bank[i % 2][:, 0:keys], AX.X, ALU.max, negate=True)\
                           .then_inc(mx_ready, 1)
                    if i >= 1:
                        n = i - 1
                        dve.wait_ge(exp_done, n + 1)
                        if n >= 2:
                            dve.wait_ge(norm_done, n - 1)
                        dve.reciprocal(row_inv[:, n % 2:n % 2 + 1], row_sum[:, n % 2:n % 2 + 1]).then_inc(inv_ready, 1)

            for b in range(5):
                key_batch(b)
            unit_steps(0, 6)
            key_batch(5)
            unit_steps(6, 12)
            key_batch(6)
            unit_steps(12, 18)
            key_batch(7)
            unit_steps(18, NU + 1)

            dve.wait_ge(ring_in[1], 16 * (4 * PAGES + 2 * NS))
            for i in range(4):
                dve.wait_ge(qb_ready, NS + i + 1)
                r = RB[:, i * 1024:(i + 1) * 1024].rearrange("p (b g n) -> p b g n", b=2, g=2)
                q = bank[6 + i % 2][:, :].rearrange("p (b n) -> p b n", b=2).unsqueeze(2).broadcast_to([PARTS, 2, 2, MW])
                step(dve.tensor_tensor(r, r, q, ALU.mult))
                for j in range(2):
                    b = 2 * i + j
                    last = dve.tensor_reduce(mem_scores[:, :, b * MHEADS:(b + 1) * MHEADS],
                                             RB[:, b * 512:(b + 1) * 512].rearrange("p (g h d) -> p g h d", g=2, h=MHEADS),
                                             AX.X, ALU.add)
                last.then_inc(k_scored, 1)
            dve.wait_ge(tile_copied, len(tiles))
            own_prod = stage[0:NS, 0:AW]
            dve.wait_ge(pv_ready, NU)
            step(dve.tensor_tensor(own_prod, q_new, k_new, ALU.mult))
            step(dve.tensor_reduce(so, own_prod.rearrange("p (h d) -> p h d", h=HEADS), AX.X, ALU.add))
            dve.tensor_tensor(so_spread.rearrange("p (b h) -> p b h", b=NS), delta8.rearrange("p (b h) -> p b h", b=NS),
                              so.unsqueeze(1).broadcast_to([NS, NS, HEADS]), ALU.mult).then_inc(so_ready, 1)
            for q in range(2):
                step(dve.tensor_scalar(mem_mask[:, q, :].rearrange("p (h d) -> p h d", h=MHEADS),
                                       iota8[:, 0:MHEADS].unsqueeze(2).broadcast_to([PARTS, MHEADS, HD]), row_f[:, 4:5],
                                       q_sel[:, q:q + 1], ALU.is_equal, ALU.mult))
            dve.wait_ge(rt_ready, 1)
            step(dve.reciprocal(rms_p, rms_p))
            dve.reciprocal(probs_t[:, 0, :], probs_t[:, 0, :]).then_inc(ri_ready, 1)

            def layernorm_center(c, banks, order):
                rows = PARTS if c < 2 else NS
                x, s = x_rows[0:rows, c, :], ln_s[0:rows, c]
                dve.wait_ge(proj_ready, order)
                for half in range(2):
                    cols = slice(half * HALF, (half + 1) * HALF)
                    step(dve.scalar_tensor_tensor(x[:, cols], x[:, cols], ALPHA, banks[half][0:rows, :], ALU.mult, ALU.add,
                                                  accum_out=s[:, half:half + 1]))
                step(dve.tensor_scalar(s[:, 2:3], s[:, 0:1], s[:, 1:2], -1.0 / D, ALU.add, ALU.mult))
                dve.tensor_scalar(x, x, s[:, 2:3], None, ALU.add).then_inc(res_ready, 1)

            def layernorm_scale(c, order):
                rows = PARTS if c < 2 else NS
                x, s = x_rows[0:rows, c, :], ln_s[0:rows, c]
                dve.wait_ge(root_ready, order)
                step(dve.reciprocal(s[:, 5:6], s[:, 4:5]))
                step(dve.scalar_tensor_tensor(x, x, s[:, 5:6], ln1_gain[0:rows], ALU.mult, ALU.mult))
                dve.tensor_tensor(x, x, ln1_bias[0:rows], ALU.add).then_inc(x1_ready, 1)

            layernorm_center(0, bank[0:2], 1)
            layernorm_center(1, bank[2:4], 2)

            dve.wait_ge(rows_stored, 16 * 6)
            dve.wait_ge(mm_ready, 1)
            dve.tensor_reduce(mstat[:, 0:1], bank[5][0:MROWS, 0:NMEM], AX.X, ALU.max, negate=True).then_inc(mm_max, 1)
            dve.wait_ge(mm_exp, 1)
            step(dve.reciprocal(mstat[:, 2:3], mstat[:, 1:2]))
            dve.tensor_scalar(probs[0:MROWS, 0, :], probs[0:MROWS, 0, :], mstat[:, 2:3], None, ALU.mult).then_inc(mm_norm, 1)

            dve.wait_ge(own_ready, 1)
            step(dve.tensor_copy(own, bank[4][0:ROWS, 0:1]))
            dve.wait_ge(l_ready, 1)
            for i in range(4):
                step(dve.tensor_reduce(gate8[:, 2 * i:2 * i + 2], bank[i][0:ROWS, :].rearrange("p (n k) -> p n k", n=2),
                                       AX.X, ALU.add))
            step(dve.max(top8, gate8))
            step(dve.max_index(seli[:, :], top8, gate8))
            step(dve.tensor_copy(seli_f, seli[:, :]))
            step(dve.tensor_scalar(pen, iota8[0:ROWS], seli_f[:, 0:1], None, ALU.is_equal))
            for i in (1, 2):
                step(dve.scalar_tensor_tensor(pen, iota8[0:ROWS], seli_f[:, i:i + 1], pen, ALU.is_equal, ALU.add))
            step(dve.tensor_scalar(pen, pen, -1.0, BIG, ALU.add, ALU.mult))
            dve.wait_ge(logits_iota, 1)
            for i in range(4):
                l = logits[:, i * 512:(i + 1) * 512]
                step(dve.scalar_tensor_tensor(l, l, slope[0:ROWS], bank[i][0:ROWS, :], ALU.mult, ALU.add))
            lb = logits.rearrange("p (n k) -> p n k", n=NBLK)
            step(dve.tensor_tensor(lb, lb, pen.unsqueeze(2).broadcast_to([ROWS, NBLK, BLK]), ALU.add))
            step(dve.tensor_reduce(stat[:, 0:1], logits, AX.X, ALU.max))
            step(dve.tensor_tensor(stat[:, 1:2], stat[:, 0:1], own, ALU.max))
            dve.tensor_scalar(stat[:, 2:3], stat[:, 1:2], -1.0, None, ALU.mult).then_inc(sm_max, 1)
            dve.wait_ge(sm_exp, 2)
            step(dve.tensor_tensor(stat[:, 5:6], stat[:, 3:4], stat[:, 4:5], ALU.add))
            step(dve.reciprocal(stat[:, 6:7], stat[:, 5:6]))
            step(dve.tensor_tensor(stat[:, 7:8], stat[:, 4:5], stat[:, 6:7], ALU.mult))
            step(dve.tensor_scalar(po_spread, dsel, stat[:, 7:8], None, ALU.mult))
            dve.tensor_scalar(logits, logits, stat[:, 6:7], None, ALU.mult).then_inc(sm_p, 1)

            dve.wait_ge(ln1_in, 32)
            layernorm_scale(0, 1)
            layernorm_scale(1, 2)
            dve.wait_ge(mpv_done, 1)
            dve.tensor_tensor(mem_masked, bank[7][:, :].rearrange("p (q c) -> p q c", q=2), mem_mask, ALU.mult)\
               .then_inc(mom_ready, 1)
            for b in range(NS):
                dve.wait_ge(pv_done, b + 1)
                if b >= 2:
                    dve.wait_ge(oc_ready, b - 1)
                dve.scalar_tensor_tensor(o_masked[:, b % 2, :], bank[6 + b % 2][:, :], row_sel[:, b % 4:b % 4 + 1], head_mask,
                                         ALU.mult, ALU.mult).then_inc(om_ready, 1)
            dve.wait_ge(rt_ready, 2)
            dve.reciprocal(rms_s, rms_s).then_inc(ri_ready, 1)
            layernorm_center(2, bank[0:2], 3)
            layernorm_scale(2, 3)

            dve.wait_ge(lg_ready, 3)
            dve.wait_ge(router_in, 32)
            pl = bank[5][:, 0:3 * E].rearrange("p (c e) -> p c e", c=3)
            step(dve.tensor_tensor(lg[:, 0:2, :], pl[:, 0:2, :], br_row.unsqueeze(1).broadcast_to([PARTS, 2, E]), ALU.add))
            step(dve.tensor_tensor(lg[0:NS, 2, :], pl[0:NS, 2, :], br_row[0:NS], ALU.add))
            for c in range(3):
                step(dve.max(max8[:, c, :], lg[:, c, :]))
                step(dve.max_index(topi[:, c, :], max8[:, c, :], lg[:, c, :]))
            step(dve.tensor_copy(topf, topi[:, :, :]))
            dve.tensor_tensor(w4, max8[:, :, 0:TOPK], max8[:, :, 0:1].broadcast_to([PARTS, 3, TOPK]), ALU.subtract)\
               .then_inc(xm_ready, 1)
            step(dve.tensor_tensor(onehot, iota32.unsqueeze(1).unsqueeze(1).broadcast_to([PARTS, 3, TOPK, E]),
                                   topf[:, :, 0:TOPK].unsqueeze(3).broadcast_to([PARTS, 3, TOPK, E]), ALU.is_equal))
            dve.tensor_reduce(chosen, onehot.rearrange("p c k e -> p c e k"), AX.X, ALU.add).then_inc(ch_ready, 1)
            dve.wait_ge(cnt_ready, 1)
            cnt = bank[6][:, 3 * E:4 * E]
            step(dve.tensor_scalar(nb, cnt, float(SLOTS), 1.0, ALU.is_gt, ALU.add))
            for m in range(2, -(-T // SLOTS)):
                step(dve.scalar_tensor_tensor(nb, cnt, float(m * SLOTS), nb, ALU.is_gt, ALU.add))
            step(dve.tensor_tensor_scan(ends, ones[:, 0:E], nb, 0.0, ALU.mult, ALU.add))
            step(dve.tensor_tensor(starts, ends, nb, ALU.subtract))
            step(dve.tensor_copy(rep3[:, 0], starts.unsqueeze(1).broadcast_to([PARTS, 3, E])))
            dve.tensor_copy(rep3[:, 1], ends.unsqueeze(1).broadcast_to([PARTS, 3, E])).then_inc(rp_ready, 1)
            step(dve.memset(slots_g.rearrange("p c e -> p (c e)"), 0.0))
            st = starts.unsqueeze(1).broadcast_to([PARTS, 2, E])
            step(dve.scalar_tensor_tensor(slots_g[:, 0:2, :], st, float(SLOTS),
                                          bank[6][:, 0:2 * E].rearrange("p (c e) -> p c e", c=2), ALU.mult, ALU.add))
            step(dve.scalar_tensor_tensor(slots_g[0:NS, 2, :], starts[0:NS], float(SLOTS), bank[6][0:NS, 2 * E:3 * E],
                                          ALU.mult, ALU.add))
            step(dve.tensor_tensor(oh_g, onehot, slots_g.unsqueeze(2).broadcast_to([PARTS, 3, TOPK, E]), ALU.mult))
            step(dve.tensor_reduce(slot4, oh_g, AX.X, ALU.add))

            def slots(wait_used, n):
                if wait_used is not None:
                    dve.wait_ge(gat_ready, wait_used)
                    dve.wait_ge(step_b, wait_used)
                dve.tensor_tensor(slot_eq, slot_id.unsqueeze(1).unsqueeze(1).broadcast_to([PARTS, 3, TOPK, SLOTS]),
                                  slot4.unsqueeze(3).broadcast_to([PARTS, 3, TOPK, SLOTS]), ALU.is_equal).then_inc(step_a, 1)
                dve.wait_ge(step_a, n)
                dve.tensor_scalar(slot_id, slot_id, float(SLOTS), None, ALU.add).then_inc(step_b, 1)
                dve.tensor_reduce(slot_hot, slot_eq.rearrange("p c k s -> p c s k"), AX.X, ALU.add).then_inc(hot_ready, 1)

            def bias_rows(n):
                dve.wait_ge(step_c, n)
                dve.tensor_scalar(block_ge, block_id, range96[:, 0:1], None, ALU.is_ge).then_inc(step_d, 1)
                dve.wait_ge(step_d, n)
                dve.scalar_tensor_tensor(bias_hot, block_id, range96[:, 1:2], block_ge, ALU.is_lt, ALU.mult)\
                   .then_inc(bias_hot_ready, 1)
                dve.wait_ge(bias_hot_ready, n)
                dve.tensor_scalar(block_id, block_id, 1.0, None, ALU.add).then_inc(step_c, 1)

            slots(None, 1)
            step(dve.memset(block_id, 0.0))
            bi = MAX_BLOCKS + 1
            dve.wait_ge(table_iota, 1)
            step(dve.tensor_tensor(ends_cmp, block_iota.unsqueeze(2).broadcast_to([1, bi, E]),
                                   ends[0:1].unsqueeze(1).broadcast_to([1, bi, E]), ALU.is_ge))
            step(dve.tensor_reduce(block_ef, ends_cmp, AX.X, ALU.add))
            step(dve.tensor_scalar(block_ef, block_ef, float(E - 1), None, ALU.min))
            step(dve.tensor_copy(block_expert[:, :], block_ef))
            dve.tensor_copy(n_blocks[:, :], ends[0:1, E - 1:E]).then_inc(table_ready, 1)
            dve.tensor_copy(slot_rows[:, :, :], slot4).then_inc(slot_rows_ready, 1)
            dve.wait_ge(xe_ready, 1)
            step(dve.tensor_reduce(w4s, w4, AX.X, ALU.add))
            step(dve.reciprocal(w4s, w4s))
            step(dve.tensor_tensor(w4, w4, w4s.unsqueeze(2).broadcast_to([PARTS, 3, TOPK]), ALU.mult))
            dve.wait_ge(rg_copied, 1)
            dve.sem_inc(step_c, 1)
            bias_rows(1)
            dve.wait_ge(table_ready, 1)
            count = dve.value_load(n_blocks[0:1, 0:1], min_val=E, max_val=MAX_BLOCKS)
            with dve.Fori(0, MAX_BLOCKS) as b:
                with dve.If(b < count):
                    slots(b + 1, b + 2)
                    dve.wait_ge(gu_used, b * KC + KC)
                    dve.tensor_scalar(gate_v, bank[0][:, :], LIMIT, None, ALU.min).then_inc(g_ready, 1)
                    dve.tensor_scalar(up_v, bank[1][:, :], -LIMIT, LIMIT, ALU.max, ALU.min).then_inc(gu_read, 1)
                    dve.wait_ge(g_ready, b + 1)
                    dve.wait_ge(gu_read, b + 1)
                    dve.scalar_tensor_tensor(up_v, up_v, 1.0, gate_v, ALU.add, ALU.mult).then_inc(up_ready, 1)
                    dve.wait_ge(up_ready, b + 1)
                    dve.wait_ge(sg_ready, b + 1)
                    dve.tensor_tensor(hid, up_v, sig_v, ALU.mult).then_inc(hd_ready, 1)
                    dve.wait_ge(hot_used, b + 1)
                    bias_rows(b + 2)
                with dve.Else():
                    pass

            dve.wait_ge(ln2_in, 32)
            dve.wait_ge(experts_done, 1)
            for c in range(3):
                rows = PARTS if c < 2 else NS
                x, s = x_rows[0:rows, c, :], ln_s[0:rows, c]
                step(dve.tensor_scalar(x, x, ALPHA, None, ALU.mult))
                dve.wait_ge(row_in_sems[c], 16 * TOPK)
                for k in range(TOPK):
                    more = {"accum_out": s[:, 0:1]} if k == TOPK - 1 else {}
                    step(dve.scalar_tensor_tensor(x, gathered[0:rows, c * TOPK + k, :], w4[0:rows, c, k:k + 1], x,
                                                  ALU.mult, ALU.add, **more))
                step(dve.tensor_scalar(s[:, 2:3], s[:, 0:1], -1.0 / D, None, ALU.mult))
                dve.tensor_scalar(x, x, s[:, 2:3], None, ALU.add).then_inc(fin_sq, 1)
                dve.wait_ge(fin_rt, 2 * c + 2)
                step(dve.reciprocal(s[:, 5:6], s[:, 4:5]))
                step(dve.scalar_tensor_tensor(x, x, s[:, 5:6], ln2_gain[0:rows], ALU.mult, ALU.mult))
                dve.tensor_tensor(x, x, ln2_bias[0:rows], ALU.add).then_inc(y_ready, 1)


_INS = ['x_prompt', 'x_sample', 'cache_k', 'cache_v', 'cache_mem_k', 'cache_mem_v', 'state_conv', 'page_table',
        'mem_prompt', 'w_in', 'w_mem_kv', 'w_conv', 'g_mix', 'w_out', 'ln1_g', 'ln1_b', 'w_router', 'b_router',
        'w_gate_up', 'b_gate_up', 'w_down', 'b_down', 'ln2_g', 'ln2_b']


def kernel(**inputs):
    import numpy as np
    import concourse.bacc as bacc
    from concourse.bass_utils import run_bass_kernel_spmd

    nc = bacc.Bacc("TRN2", target_bir_lowering=False, num_devices=1)
    arrays, args = {}, []
    for name in _INS:
        a = np.ascontiguousarray(inputs[name])
        arrays[f"in_{name}"] = a
        args.append(nc.dram_tensor(f"in_{name}", a.shape, mybir.dt.from_np(a.dtype), kind="ExternalInput").ap())
    xp, xs, ck, mk, st = (inputs[n].shape for n in ('x_prompt', 'x_sample', 'cache_k', 'cache_mem_k', 'state_conv'))
    heads = (ck[3], ck[4])
    outs = [xp, xs, (1, 1, xp[1], *heads), (1, 1, xp[1], *heads), (1, 1, *st[2:]), (1, 1, *mk[2:]), (1, 1, *mk[2:]),
            (1, xs[0], 1, *heads), (1, xs[0], 1, *heads), tuple(st)]
    for i, shape in enumerate(outs):
        args.append(nc.dram_tensor(f"out_{i}", shape, F32, kind="ExternalOutput").ap())
    blocks = 32 + (xp[1] + xs[0]) * 4 // 65
    args.append(nc.dram_tensor("expert_rows", (blocks * 64, xp[2]), F32, kind="Internal").ap())
    layer_kernel(nc, *args)
    r = run_bass_kernel_spmd(nc, [arrays], core_ids=[0])
    return tuple(r.results[0][f"out_{i}"] for i in range(len(outs)))
```

```python
from contextlib import ExitStack

import concourse.bass as bass
from concourse import mybir

ALU = mybir.AluOpType
ACT = mybir.ActivationFunctionType
AX = mybir.AxisListType
F32 = mybir.dt.float32
I32 = mybir.dt.int32
U32 = mybir.dt.uint32

BIG = 1.0e30
PARTS = 128


class Counter:

    def __init__(self, sem):
        self.sem, self.n = sem, 0

    def on(self, instruction):
        instruction.then_inc(self.sem, 1)
        self.n += 1
        return self.n


def layer_kernel(nc, x_prompt, x_sample, cache_k, cache_v, cache_mem_k, cache_mem_v, state_conv, page_table,
                 mem_prompt, w_in, w_mem_kv, w_conv, g_mix, w_out, ln1_g, ln1_b, w_router, b_router,
                 w_gate_up, b_gate_up, w_down, b_down, ln2_g, ln2_b,
                 y_prompt, y_sample, k_prompt, v_prompt, conv_prompt, mem_k_prompt, mem_v_prompt,
                 k_sample, v_sample, conv_sample, expert_rows):
    D = x_prompt.shape[2]
    NP = x_prompt.shape[1]
    NS = x_sample.shape[0]
    T = NP + NS
    KC = D // PARTS
    HD = 64
    HEADS = cache_k.shape[3]
    MHEADS = cache_mem_k.shape[3]
    AW = HEADS * HD
    MW = MHEADS * HD
    NMEM = mem_prompt.shape[1]
    PAGES = page_table.shape[1]
    NPHYS = cache_k.shape[1]
    PAST = PAGES * PARTS
    BLK = 256
    NBLK = PAST // BLK
    PC = w_in.shape[2] // PARTS
    E = w_router.shape[2]
    FF = w_down.shape[2]
    TOPK = 4
    SLOTS = 64
    MAX_BLOCKS = E + (T * TOPK) // (SLOTS + 1)
    HALF = D // 2
    QSCALE = HD ** -0.5
    ALPHA = 2.0 ** 0.25
    EPS = 1e-5
    LIMIT = 7.0
    SW_ALPHA = 1.702
    ROWS = NS * HEADS
    MROWS = NS * MHEADS
    assert ROWS == 64 and NP == 256 and PARTS == page_table.shape[1] * NS and PC == 20
    CQ, CK, CV, CM, CB, CC, CH = 0, 4, 8, 12, 14, 16, 18
    OATT, OCONV, OMEM = 0, 4, 6

    ctx = ExitStack()
    with ctx:
        def sb(name, shape, dt=F32):
            return ctx.enter_context(nc.sbuf_tensor(name, shape, dt))

        def sem(name):
            return ctx.enter_context(nc.semaphore(name))

        gate_up_w = sb("gate_up_w", [PARTS, KC, 2 * FF])
        down_w = sb("down_w", [PARTS, KC, D])
        ring = [sb("ring_a", [PARTS, PAGES * AW]), sb("ring_b", [PARTS, PAGES * AW])]
        x_rows = sb("x_rows", [PARTS, 3, D])
        x_cols = sb("x_cols", [PARTS, KC, T])
        work = sb("work", [PARTS, 2 * KC * NMEM])
        consts = sb("consts", [PARTS, 1280])
        small = sb("small", [PARTS, 1280])
        page_of = sb("page_of", [PARTS, NS], I32)
        page_row = sb("page_row", [PARTS, NS], I32)
        topi = sb("topi", [PARTS, 3, 8], U32)
        seli = sb("seli", [ROWS, 8], U32)
        rowi = sb("rowi", [PARTS, 8], I32)
        slot_rows = sb("slot_rows", [PARTS, 3, TOPK], I32)
        block_expert = sb("block_expert", [1, MAX_BLOCKS + 1], I32)
        last_block = sb("last_block", [1, E], I32)
        n_blocks = sb("n_blocks", [1, 1], I32)
        bank = [ctx.enter_context(nc.psum_tensor(f"bank{i}", [PARTS, 512], F32))[:, :] for i in range(8)]

        used = {"c": 0, "s": 0}

        def const(n, rows=PARTS):
            a = used["c"]
            used["c"] += n
            assert used["c"] <= 1280
            return consts[0:rows, a:a + n]

        def scratch(n, rows=PARTS):
            a = used["s"]
            used["s"] += n
            assert used["s"] <= 1280
            return small[0:rows, a:a + n]

        w_in_a = gate_up_w
        RA, RB = ring
        w_in_b = RA[:, 0:KC * 512].rearrange("p (k n) -> p k n", k=KC)
        w_mem = RA[:, KC * 512:2 * KC * 512].rearrange("p (k n) -> p k n", k=KC)
        down_flat = down_w[:, :, :].rearrange("p k n -> p (k n)")
        p_cols = down_flat[:, 0:PC * T].rearrange("p (j t) -> p j t", j=PC)
        at = PC * T
        scores = down_flat[:, at:at + PAGES * ROWS].rearrange("p (g r) -> p g r", g=PAGES)
        at += PAGES * ROWS
        mem_cols = down_flat[:, at:at + 4 * NMEM].rearrange("p (j t) -> p j t", j=4)
        stage = down_flat[:, at:at + 4 * NMEM]
        at += 4 * NMEM
        q_new = down_flat[0:NS, at:at + AW]
        at += AW
        qm_new = down_flat[0:NS, at:at + MW]
        at += MW
        assert at <= KC * D
        head_slope_eye = gate_up_w[:, 0, 0:HEADS * PARTS].rearrange("p (h c) -> p h c", h=HEADS)
        squares = gate_up_w[:, 0, :].rearrange("p (j t) -> p j t", j=KC)
        ln1_gain, ln1_bias = gate_up_w[:, 1, 0:D], gate_up_w[:, 1, D:2 * D]
        k_new, v_new = gate_up_w[0:NS, 2, 0:AW], gate_up_w[0:NS, 2, AW:2 * AW]
        mem_v = gate_up_w[:, 4:6, :].rearrange("p s (b g c) -> p (s b) g c", b=4, g=2)
        mem_k = gate_up_w[:, 6:8, :].rearrange("p s (b g c) -> p (s b) g c", b=4, g=2)
        mem_masked = gate_up_w[:, 2, 3 * AW:4 * AW].rearrange("p (q c) -> p q c", q=2)
        logits = gate_up_w[0:ROWS, 3, 0:PAST]
        w_o = gate_up_w[:, 4:8, :].rearrange("p s (u n) -> p (s u) n", u=2)
        mem_rows = work[:, 0:2 * D].rearrange("p (c d) -> p c d", c=2)
        mem_x = work[:, 2 * D:2 * D + KC * NMEM].rearrange("p (k t) -> p k t", k=KC)
        k_rows = work[:, 0:2 * AW].rearrange("p (c d) -> p c d", c=2)
        v_rows = work[:, 2 * AW:4 * AW].rearrange("p (c d) -> p c d", c=2)
        mkv_rows = work[:, 4 * AW:6 * AW].rearrange("p (c d) -> p c d", c=2)
        probs = work[:, 6 * AW:8 * AW].rearrange("p (b k) -> p b k", b=2)
        probs_t = k_rows
        o_masked = v_rows
        mem_probs = probs[0:MROWS, 1, NMEM:2 * NMEM]
        o_cols = x_cols
        bias_rows_w = RA[0:E, 0:2 * FF + D]
        zero_rows = RA[:, 2 * FF + D:2 * FF + 2 * D]
        rb = {"n": 0}

        def part_b(n, rows=PARTS):
            a = rb["n"]
            rb["n"] += n
            assert rb["n"] <= PAGES * AW
            return RB[0:rows, a:a + n]

        xg = part_b(HALF)
        xg_t = part_b(HALF).rearrange("p (j h s) -> p j h s", j=4, h=2)
        gate_v, up_v, sig_v, hid = part_b(HALF), part_b(HALF), part_b(HALF), part_b(HALF)
        ends_cmp = RB[0:1, rb["n"] - 4 * HALF:rb["n"] - 4 * HALF + (MAX_BLOCKS + 1) * E].rearrange("p (b e) -> p b e", e=E)
        oh_g = RB[:, rb["n"] - 3 * TOPK * E:rb["n"]].rearrange("p (c k e) -> p c k e", c=3, k=TOPK)
        assert (MAX_BLOCKS + 1) * E + 3 * TOPK * E <= 4 * HALF
        hid_t = part_b(HALF).rearrange("p (j h s) -> p j h s", j=4, h=2)
        out_rows = part_b(HALF)
        slot_eq = part_b(3 * TOPK * SLOTS).rearrange("p (c k s) -> p c k s", c=3, k=TOPK)
        slot_hot = part_b(3 * SLOTS).rearrange("p (c s) -> p c s", c=3)
        onehot = part_b(3 * TOPK * E).rearrange("p (c k e) -> p c k e", c=3, k=TOPK)
        ln2_gain, ln2_bias = part_b(D), part_b(D)
        gathered = gate_up_w[:, :, :].rearrange("p k (u n) -> p (k u) n", u=2)

        ident = const(PARTS)
        ones = const(PARTS)
        tri = const(PARTS)
        dist = const(3 * PARTS)
        eps = const(1)
        row_f = const(8)
        iota8 = const(8)
        hot8 = const(8)
        slope8 = const(8)
        slope = const(1)
        row_sel = const(4)
        grp_sel = const(4)
        q_sel = const(2)
        hot4 = const(2 * MHEADS).rearrange("p (q h) -> p q h", q=2)
        delta8 = const(ROWS, NS)
        dsel = const(8, ROWS)
        g_cols = scratch(KC)
        page_f = scratch(NS)
        w_cols = scratch(6).rearrange("p (j i) -> p j i", j=2)
        s_cols = scratch(4 * NS).rearrange("p (j b r) -> p j b r", j=2, b=NS)
        mem_scores = scratch(2 * MROWS).rearrange("p (g r) -> p g r", g=2)
        mem_pt = scratch(2 * MROWS).rearrange("p (g r) -> p g r", g=2)
        so = scratch(8, NS)
        so_spread = scratch(ROWS, NS)
        po_new = scratch(ROWS, NS)
        po_spread = scratch(8, ROWS)
        own = scratch(1, ROWS)
        stat = scratch(16, ROWS)
        gate8 = scratch(8, ROWS)
        gate_part = scratch(4 * NBLK, ROWS).rearrange("p (n i) -> p n i", n=NBLK)
        top8 = scratch(8, ROWS)
        seli_f = scratch(8, ROWS)
        pen = scratch(8, ROWS)
        mstat = scratch(4, MROWS)
        neg_max = scratch(4).rearrange("p (b c) -> p b c", b=2)
        row_sum = scratch(4).rearrange("p (b c) -> p b c", b=2)
        row_inv = scratch(4).rearrange("p (b c) -> p b c", b=2)
        u_s = scratch(2 * NS).rearrange("p (j b) -> p j b", j=2)
        c_s = scratch(4 * NS).rearrange("p (a j b) -> p a j b", a=2, j=2)
        sq_s = scratch(KC * NS).rearrange("p (j t) -> p j t", j=KC)
        rms_s = scratch(3 * NS)
        ln_s = scratch(3 * 8).rearrange("p (c i) -> p c i", c=3)
        lg = scratch(3 * E).rearrange("p (c e) -> p c e", c=3)
        br_row = scratch(E)
        max8 = scratch(24).rearrange("p (c k) -> p c k", c=3)
        topf = scratch(24).rearrange("p (c k) -> p c k", c=3)
        w4 = scratch(3 * TOPK).rearrange("p (c k) -> p c k", c=3)
        w4s = scratch(3)
        chosen = scratch(3 * E).rearrange("p (c e) -> p c e", c=3)
        iota32 = scratch(E)
        nb = scratch(E)
        ends = scratch(E)
        starts = scratch(E)
        slots_g = scratch(3 * E).rearrange("p (c e) -> p c e", c=3)
        slot4 = scratch(3 * TOPK).rearrange("p (c k) -> p c k", c=3)
        slot_id = scratch(SLOTS)
        rms_p = work[:, 6 * AW:6 * AW + 3 * NP].rearrange("p (s t) -> p s t", s=3)
        w_r = work[:, 4 * AW:4 * AW + KC * E].rearrange("p (k e) -> p k e", k=KC)
        expert_range = work[0:E, 5 * AW:5 * AW + 2]
        block_id = work[0:E, 5 * AW + 200:5 * AW + 200 + SLOTS]
        block_ge = work[0:E, 5 * AW + 264:5 * AW + 264 + SLOTS]
        bias_hot = work[0:E, 5 * AW + 100:5 * AW + 100 + SLOTS]
        block_iota = work[0:1, 5 * AW + 360:5 * AW + 360 + MAX_BLOCKS + 1]
        block_ef = work[0:1, 5 * AW + 410:5 * AW + 410 + MAX_BLOCKS + 1]
        assert 410 + MAX_BLOCKS + 1 <= 512

        x_in, mem_in, pages_in, smalls_in = sem("x_in"), sem("mem_in"), sem("pages_in"), sem("smalls_in")
        w_q_in, w_kv_in, w_m_in, w_ch_in, w_mem_in = (sem("w_q_in"), sem("w_kv_in"), sem("w_m_in"),
                                                      sem("w_ch_in"), sem("w_mem_in"))
        ring_in = [sem("ring_a_in"), sem("ring_b_in")]
        w_out_in, ln1_in, router_in, ln2_in, bias_in = (sem("w_out_in"), sem("ln1_in"), sem("router_in"),
                                                        sem("ln2_in"), sem("bias_in"))
        gu_in = [sem(f"gate_up_in{k}") for k in range(KC)]
        dn_in = [sem(f"down_in{k}") for k in range(KC)]
        mem_scored = sem("mem_keys_scored")
        mem_kv_in, page_rows_ready = sem("mem_kv_in"), sem("page_rows_ready")
        eye_ready, const_ready, rowi_ready, sel_ready = (sem("eye_ready"), sem("const_ready"), sem("rowi_ready"),
                                                         sem("sel_ready"))
        tile_ready, tile_copied = sem("tile_ready"), sem("tile_copied")
        qb_ready, k_scored = sem("query_spread"), sem("keys_scored")
        eyes_ready, logits_iota = sem("slope_eyes_ready"), sem("logits_iota_ready")
        sc_ready, mx_ready, exp_done, inv_ready = (sem("unit_scores"), sem("unit_max"), sem("unit_exp"),
                                                   sem("unit_inverse"))
        norm_done, pt_ready, pt_copied, pv_ready, o_copied = (sem("unit_norm"), sem("unit_turned"),
                                                              sem("unit_turned_copied"), sem("unit_pv"),
                                                              sem("unit_out_copied"))
        conv_done, conv_u = sem("conv_done"), sem("conv_u_ready")
        sq_ready, ss_ready, rt_ready, ri_ready, mix_ready = (sem("squares_ready"), sem("square_sums"),
                                                             sem("rms_root"), sem("rms_inverse"), sem("mix_ready"))
        proj_ready, res_ready, var_ready, root_ready, x1_ready = (sem("out_proj"), sem("centered_ready"),
                                                                  sem("variance_ready"), sem("root_ready"),
                                                                  sem("x1_ready"))
        x1t_ready, x1t_copied, lg_ready = sem("x1_turned"), sem("x1_turned_copied"), sem("router_logits")
        so_ready, own_ready, l_ready, sm_max, sm_exp, sm_p = (sem("own_spread"), sem("own_score"),
                                                              sem("score_rows"), sem("softmax_max"),
                                                              sem("softmax_exp"), sem("softmax_done"))
        ptt_ready, ptt_copied, po_ready, po_copied = (sem("probs_turned"), sem("probs_turned_copied"),
                                                      sem("own_prob_spread"), sem("own_prob_copied"))
        pv_done, om_ready, oc_ready, oc_copied = sem("page_values"), sem("o_masked"), sem("o_cols"), sem("o_cols_copied")
        unit_read = sem("values_read")
        mm_ready, mm_max, mm_exp, mm_norm, mmt_ready, mmt_copied = (sem("mem_rows"), sem("mem_max"), sem("mem_exp"),
                                                                   sem("mem_norm"), sem("mem_turned"),
                                                                   sem("mem_turned_copied"))
        mpv_done, mom_ready = sem("mem_values"), sem("mem_masked")
        xm_ready, xe_ready, ch_ready, cnt_ready, rp_ready, rg_ready, rg_copied = (
            sem("router_shift"), sem("router_exp"), sem("chosen_ready"), sem("counts_ready"), sem("ranges_spread"),
            sem("ranges_turned"), sem("ranges_copied"))
        table_ready, parts_ready = sem("block_table"), sem("bias_parts_ready")
        hot_ready, hot_used, gat_ready, gat_copied = (sem("slots_hot"), sem("slots_used"), sem("gathered"),
                                                      sem("gathered_copied"))
        xgt_ready, xgt_copied, gu_ready, gu_used = (sem("gathered_turned"), sem("gathered_turned_copied"),
                                                    sem("gate_up_done"), sem("gate_up_tiles_used"))
        g_ready, sg_ready, hd_ready, hdt_ready, hdt_copied = (sem("gate_clamped"), sem("sigmoid"), sem("hidden"),
                                                              sem("hidden_turned"), sem("hidden_turned_copied"))
        gu_read = sem("gate_up_read")
        dn_ready, dn_used, dn_copied, rows_out = (sem("down_done"), sem("down_tiles_used"), sem("down_copied"),
                                                  sem("expert_rows_out"))
        step_a, step_b, step_c, step_d = sem("slot_equal"), sem("slot_id_next"), sem("block_id_next"), sem("block_at_start")
        up_ready, bias_hot_ready, table_iota = sem("up_times_gate"), sem("bias_row_hot"), sem("block_numbers")
        spare_zeroed = sem("spare_rows_zeroed")
        experts_done = sem("experts_done")
        block_stored, all_stored = sem("block_rows_stored"), sem("all_blocks_stored")
        rows_stored, conv_stored, slot_rows_ready = sem("key_value_rows_stored"), sem("conv_stored"), sem("slot_rows_ready")
        row_in_sems = [sem(f"rows_in{c}") for c in range(3)]
        row_in = sem("rows_gathered")
        y_ready, out_done = sem("y_ready"), sem("outputs_stored")
        dve_n, act_n, pool_n = Counter(sem("dve_step")), Counter(sem("act_step")), Counter(sem("pool_step"))
        fin_sq, fin_rt = sem("final_squares"), sem("final_root")
        parts_free = sem("ring_a_free")

        tiles = ([("small", i) for i in range(3)] + [("xt", k) for k in range(KC)] + [("proj", CQ + j) for j in range(4)] +
                 [("qs", 0)] + [("proj", CC + j) for j in range(4)] + [("mt", k) for k in range(KC)] +
                 [("mkv", j) for j in range(4)] + [("proj", CK + j) for j in range(8)] +
                 [("proj", CM + j) for j in range(4)] + [("qms", 0)] +
                 [("kr", 0), ("kr", 1), ("vr", 0), ("vr", 1), ("ks", 0), ("vs", 0), ("mr", 0), ("mr", 1)])
        tile_no = {t: i for i, t in enumerate(tiles)}
        SPREAD_AFTER = {("qs", 0): (0, 1), ("proj", CK + 1): (2,), ("proj", CB + 1): (3,)}
        units = [(False, h) for h in range(HEADS)] + [(True, h) for h in range(MHEADS)]
        NU = len(units)
        SCORE_SLOTS = 2 * NS
        FIRST_SLOT = 6
        SPREAD_BEFORE_UNIT = {2 * b - 1 - FIRST_SLOT: b for b in range(4, NS)}
        K_HALF = [1, 1] + [b % 2 for b in range(2, NS)]
        PROMPT_AFTER = {1: "project 0", 2: "project 1", 4: "turn 0", 5: "turn 1"}

        block = ctx.enter_context(nc.Block())

        def ring_total(b):
            return 16 * (K_HALF.count(b % 2) + b // 2 + 1)

        def keys_total(b):
            return 16 * K_HALF[:b + 1].count(K_HALF[b])

        def columns_of(pe, b):
            pe.wait_ge(om_ready, b + 1)
            for j in range(4):
                last = pe.matmul(bank[5][:, 320 + j * NS + b:321 + j * NS + b], o_masked[:, b % 2, j * PARTS:(j + 1) * PARTS],
                                 ones[:, 0:1], start=True, stop=True)
            last.then_inc(oc_ready, 1)

        def ln_square(c):
            return gate_up_w[:, 0, 0:D]

        @block.sync
        def _(sp):
            with nc.allow_non_contiguous_dma(reason="page numbers, one a partition"):
                for b in range(NS):
                    sp.dma_start(page_of[:, b:b + 1],
                                 page_table[b].unsqueeze(1).broadcast_to([PAGES, PARTS // PAGES])).then_inc(pages_in, 16)
            sp.dma_start(x_rows[:, 0:2, :], x_prompt[0].rearrange("(c p) d -> p c d", p=PARTS)).then_inc(x_in, 16)
            sp.dma_start(x_rows[0:NS, 2, :], x_sample[:, 0, :]).then_inc(x_in, 16)
            w_in_k = w_in[0].rearrange("(k p) n -> p k n", p=PARTS)
            sp.dma_start(w_in_a[:, :, 0:512], w_in_k[:, :, 0:512]).then_inc(w_q_in, 16)
            sp.dma_start(w_in_b, w_in_k[:, :, 2048:2560]).then_inc(w_ch_in, 16)
            sp.dma_start(mem_rows, mem_prompt[0].rearrange("(c p) d -> p c d", p=PARTS)).then_inc(mem_in, 16)
            sp.dma_start(w_mem, w_mem_kv[0].rearrange("(k p) n -> p k n", p=PARTS)).then_inc(w_mem_in, 16)
            sp.dma_start(w_in_a[:, :, 512:1536], w_in_k[:, :, 512:1536]).then_inc(w_kv_in, 16)
            sp.dma_start(w_in_a[:, :, 1536:2048], w_in_k[:, :, 1536:2048]).then_inc(w_m_in, 16)
            sp.wait_ge(tile_ready, tile_no[("proj", CB + 1)] + 1)
            for dst, cache in ((mem_k, cache_mem_k), (mem_v, cache_mem_v)):
                sp.dma_start(dst.rearrange("p b g c -> p b (g c)"),
                             cache[0].rearrange("b (p g) h d -> p b (g h d)", p=PARTS)).then_inc(mem_kv_in, 16)
            sp.dma_start(ln1_gain, ln1_g[0][None, :].broadcast_to([PARTS, D])).then_inc(ln1_in, 16)
            sp.dma_start(ln1_bias, ln1_b[0][None, :].broadcast_to([PARTS, D])).then_inc(ln1_in, 16)
            sp.wait_ge(mpv_done, 1)
            sp.dma_start(w_o, w_out[0].rearrange("(j p) n -> p j n", p=PARTS)).then_inc(w_out_in, 16)
            sp.wait_ge(unit_read, NS - 1)
            sp.dma_start(bias_rows_w[:, 0:2 * FF], b_gate_up[0]).then_inc(bias_in, 16)
            sp.dma_start(bias_rows_w[:, 2 * FF:2 * FF + D], b_down[0]).then_inc(bias_in, 16)
            gu_k = w_gate_up[0].rearrange("e (k p) n -> e p k n", p=PARTS)
            dn_k = w_down[0].rearrange("e (k p) n -> e p k n", p=PARTS)
            sp.wait_ge(proj_ready, 3)
            sp.wait_ge(x1_ready, 3)
            for k in range(KC):
                sp.dma_start(gate_up_w[:, k, :], gu_k[0, :, k, :]).then_inc(gu_in[k], 16)
            sp.wait_ge(conv_stored, 16 * 4)
            for k in range(KC):
                sp.dma_start(down_w[:, k, :], dn_k[0, :, k, :]).then_inc(dn_in[k], 16)
            sp.wait_ge(unit_read, NS)
            sp.dma_start(ln2_gain, ln2_g[0][None, :].broadcast_to([PARTS, D])).then_inc(ln2_in, 16)
            sp.dma_start(ln2_bias, ln2_b[0][None, :].broadcast_to([PARTS, D])).then_inc(ln2_in, 16)
            sp.wait_ge(table_ready, 1)
            with sp.Fori(1, E) as e:
                last = sp.value_load(last_block[0:1, bass.ds(e - 1, 1)], min_val=0, max_val=MAX_BLOCKS - 1)
                for k in range(KC):
                    sp.wait_ge(gu_used, last * KC + (k + 1))
                    sp.dma_start(gate_up_w[:, k, :],
                                 gu_k[bass.ds(e, 1), :, k, :].rearrange("a p n -> (a p) n")).then_inc(gu_in[k], 16)
                for k in range(KC):
                    sp.wait_ge(dn_used, last * KC + (k + 1))
                    sp.dma_start(down_w[:, k, :],
                                 dn_k[bass.ds(e, 1), :, k, :].rearrange("a p n -> (a p) n")).then_inc(dn_in[k], 16)
            sp.wait_ge(y_ready, 2)
            sp.dma_start(y_prompt[0].rearrange("(c p) d -> p c d", p=PARTS), x_rows[:, 0:2, :]).then_inc(out_done, 16)
            sp.wait_ge(y_ready, 3)
            sp.dma_start(y_sample[:, 0, :], x_rows[0:NS, 2, :]).then_inc(out_done, 16)
            sp.wait_ge(out_done, 16 * 3)
            sp.wait_ge(rows_stored, 16 * 6)
            sp.wait_ge(conv_stored, 16 * 4)

        @block.tensor
        def _(pe):
            def tile_wait(i):
                if i >= 4:
                    pe.wait_ge(tile_copied, i - 3)

            def copied(t):
                pe.wait_ge(tile_copied, tile_no[t] + 1)

            def spread(b):
                if b >= 2:
                    pe.wait_ge(k_scored, 2 * (b - 1))
                pe.matmul(bank[6 + b % 2][:, :], row_pick(b), q_new, start=True, stop=True).then_inc(qb_ready, 1)

            def row_pick(b):
                return ident[0:NS, b:b + 1].broadcast_to([NS, PARTS])

            pe.wait_ge(eye_ready, 1)
            for i, (kind, n) in enumerate(tiles):
                out = bank[i % 4]
                tile_wait(i)
                if kind == "small":
                    if n == 0:
                        pe.wait_ge(smalls_in, 48)
                        last = pe.transpose(out[:, 0:KC], stage[0:KC, 0:PARTS], ident[0:KC, 0:KC])
                    elif n == 1:
                        for j in range(2):
                            last = pe.transpose(out[:, j * 3:j * 3 + 3], stage[0:3, 256 + j * 128:384 + j * 128], ident[0:3, 0:3])
                    else:
                        for j in range(2):
                            last = pe.transpose(out[:, j * 16:j * 16 + 16], stage[0:16, 512 + j * 128:640 + j * 128],
                                                ident[0:16, 0:16])
                elif kind == "xt":
                    pe.wait_ge(x_in, 32)
                    for c in range(3):
                        rows = PARTS if c < 2 else NS
                        last = pe.transpose(out[:, c * PARTS:c * PARTS + rows],
                                            x_rows[0:rows, c, n * PARTS:(n + 1) * PARTS], ident[0:rows, 0:rows])
                elif kind == "proj":
                    pe.wait_ge(w_q_in if n < CK else w_kv_in if n < CM else w_m_in if n < CC else w_ch_in, 16)
                    copied(("xt", KC - 1))
                    for k in range(KC):
                        w = w_in_a[:, k, n * PARTS:(n + 1) * PARTS] if n < 16 else \
                            w_in_b[:, k, (n - 16) * PARTS:(n - 15) * PARTS]
                        last = pe.matmul(out[:, 0:T], w, x_cols[:, k, :], start=(k == 0), stop=(k == KC - 1))
                elif kind == "mt":
                    pe.wait_ge(mem_in, 16)
                    for c in range(2):
                        last = pe.transpose(out[:, c * PARTS:(c + 1) * PARTS],
                                            mem_rows[:, c, n * PARTS:(n + 1) * PARTS], ident[:, :])
                elif kind == "mkv":
                    pe.wait_ge(w_mem_in, 16)
                    copied(("mt", KC - 1))
                    for k in range(KC):
                        last = pe.matmul(out[:, 0:NMEM], w_mem[:, k, n * PARTS:(n + 1) * PARTS], mem_x[:, k, :],
                                         start=(k == 0), stop=(k == KC - 1))
                elif kind in ("qs", "ks", "vs", "qms"):
                    first, chunks = {"qs": (CQ, 4), "ks": (CK, 4), "vs": (CV, 4), "qms": (CM, 2)}[kind]
                    copied(("proj", first + chunks - 1))
                    for j in range(chunks):
                        last = pe.transpose(out[0:NS, j * PARTS:(j + 1) * PARTS], p_cols[:, first + j, NP:T], ident[:, :])
                else:
                    copied(("mkv", 3))
                    for j in range(4):
                        src = mem_cols[:, j, n * PARTS:(n + 1) * PARTS] if kind == "mr" else \
                            p_cols[:, (CK if kind == "kr" else CV) + j, n * PARTS:(n + 1) * PARTS]
                        last = pe.transpose(out[:, j * PARTS:(j + 1) * PARTS], src, ident[:, :])
                last.then_inc(tile_ready, 1)
                for b in SPREAD_AFTER.get((kind, n), ()):
                    copied(("qs", 0))
                    spread(b)

            pe.wait_ge(tile_copied, len(tiles))
            for i in range(NU + 2):
                if i in SPREAD_BEFORE_UNIT:
                    spread(SPREAD_BEFORE_UNIT[i])
                if i < NU:
                    mem, h = units[i]
                    p = HD * (h % 2)
                    if i >= 2:
                        pe.wait_ge(exp_done, 2 * (i - 1))
                    k = mem_cols[p:p + HD, h // 2, :] if mem else p_cols[p:p + HD, CK + h // 2, 0:NP]
                    for c in range(2):
                        out = bank[i % 2][:, c * NP:(c + 1) * NP]
                        q = p_cols[p:p + HD, (CM if mem else CQ) + h // 2, c * PARTS:(c + 1) * PARTS]
                        last = pe.matmul(out, q, k, start=True, stop=mem)
                        if not mem:
                            if i == 0:
                                pe.wait_ge(eyes_ready, 1)
                            last = pe.matmul(out, head_slope_eye[:, h, :], dist[:, PARTS * (1 - c):PARTS * (3 - c)],
                                             start=False, stop=True)
                    last.then_inc(sc_ready, 1)
                if 1 <= i <= NU:
                    n = i - 1
                    pe.wait_ge(norm_done, n + 1)
                    if n >= 2:
                        pe.wait_ge(pt_copied, n - 1)
                    for g in range(2):
                        for c in range(2):
                            last = pe.transpose(bank[2 + n % 2][:, (2 * g + c) * PARTS:(2 * g + c + 1) * PARTS],
                                                probs[:, n % 2, (2 * c + g) * PARTS:(2 * c + g + 1) * PARTS], ident[:, :])
                    last.then_inc(pt_ready, 1)
                if 2 <= i:
                    n = i - 2
                    mem, h = units[n]
                    p = HD * (h % 2)
                    pe.wait_ge(pt_copied, n + 1)
                    if n >= 2:
                        pe.wait_ge(o_copied, n - 1)
                    for g in range(2):
                        v = mkv_rows[:, g, MW + h * HD:MW + (h + 1) * HD] if mem else v_rows[:, g, h * HD:(h + 1) * HD]
                        last = pe.matmul(bank[4 + n % 2][p:p + HD, 0:NP], v, probs_t[:, n % 2, g * NP:(g + 1) * NP],
                                         start=(g == 0), stop=(g == 1))
                    last.then_inc(pv_ready, 1)

            pe.wait_ge(o_copied, NU)
            pe.wait_ge(so_ready, 1)
            pe.matmul(bank[5][0:ROWS, 511:512], so_spread, ones[0:NS, 0:1], start=True, stop=True).then_inc(own_ready, 1)
            pe.wait_ge(k_scored, SCORE_SLOTS)
            for g in range(PAGES):
                last = pe.transpose(bank[g // 4][0:ROWS, (g % 4) * PARTS:(g % 4 + 1) * PARTS], scores[:, g, :], ident[:, :])
            last.then_inc(l_ready, 1)
            pe.wait_ge(sq_ready, 1)
            sections = ((OATT, 4, bank[4][:, 0:NP]), (OCONV, 2, bank[4][:, NP:2 * NP]), (OMEM, 2, bank[5][:, 0:NP]))
            for first, n, out in sections:
                for j in range(n):
                    last = pe.matmul(out, ones, squares[:, first + j, :], start=(j == 0), stop=(j == n - 1))
            last.then_inc(ss_ready, 1)
            for i in range(NS // 2):
                if i >= 2:
                    pe.wait_ge(mem_scored, i - 1)
                for b in (2 * i, 2 * i + 1):
                    last = pe.matmul(bank[6 + i % 2][:, (b % 2) * MW:(b % 2 + 1) * MW], row_pick(b), qm_new,
                                     start=True, stop=True)
                last.then_inc(qb_ready, 1)

            def out_proj(c, banks):
                rows = PARTS if c < 2 else NS
                for half in range(2):
                    for j in range(KC):
                        last = pe.matmul(banks[half][0:rows, :], o_cols[:, j, c * PARTS:c * PARTS + rows],
                                         w_o[:, j, half * HALF:(half + 1) * HALF], start=(j == 0), stop=(j == KC - 1))
                last.then_inc(proj_ready, 1)

            def turn_x1(c):
                rows = PARTS if c < 2 else NS
                pe.wait_ge(x1_ready, c + 1)
                for k in range(KC):
                    last = pe.transpose(bank[2 + k // 4][:, (k % 4) * PARTS:(k % 4) * PARTS + rows],
                                        x_rows[0:rows, c, k * PARTS:(k + 1) * PARTS], ident[0:rows, 0:rows])
                    if k % 4 == 3:
                        last.then_inc(x1t_ready, 1)
                pe.wait_ge(x1t_copied, 2 * (c + 1))
                if c == 0:
                    pe.wait_ge(router_in, 32)
                for k in range(KC):
                    last = pe.matmul(bank[4][0:rows, c * E:(c + 1) * E], o_cols[:, k, c * PARTS:c * PARTS + rows],
                                     w_r[:, k, :], start=(k == 0), stop=(k == KC - 1))
                last.then_inc(lg_ready, 1)

            pe.wait_ge(mem_scored, NS // 2)
            pe.wait_ge(rt_ready, 1)
            for g in range(2):
                last = pe.transpose(bank[4][0:MROWS, g * PARTS:(g + 1) * PARTS], mem_scores[:, g, :], ident[:, :])
            last.then_inc(mm_ready, 1)
            pe.wait_ge(sm_p, 1)
            for g in range(PAGES):
                last = pe.transpose(bank[2 + g // 8][:, (g % 8) * ROWS:(g % 8 + 1) * ROWS],
                                    logits[:, g * PARTS:(g + 1) * PARTS], ident[0:ROWS, 0:ROWS])
            last.then_inc(ptt_ready, 1)
            pe.wait_ge(mm_norm, 1)
            for g in range(2):
                last = pe.transpose(bank[4][:, 256 + g * MROWS:256 + (g + 1) * MROWS],
                                    mem_probs[:, g * PARTS:(g + 1) * PARTS], ident[0:MROWS, 0:MROWS])
            pe.matmul(bank[4][0:NS, 320:320 + ROWS], po_spread, ident[0:ROWS, 0:ROWS], start=True, stop=True)\
                .then_inc(po_ready, 1)
            pe.wait_ge(mmt_copied, 1)
            for b in range(NS):
                grp, q = b % 4, b // 4
                for g in range(2):
                    last = pe.matmul(bank[1][32 * grp:32 * grp + 32, q * MW:(q + 1) * MW], mem_pt[:, g, :],
                                     mem_v[:, b, g, :], start=(g == 0), stop=(g == 1))
            last.then_inc(mpv_done, 1)
            pe.wait_ge(mom_ready, 1)
            for q in range(2):
                for j in range(2):
                    last = pe.matmul(bank[5][:, 256 + j * NS + 4 * q:256 + j * NS + 4 * q + 4],
                                     mem_masked[:, q, j * PARTS:(j + 1) * PARTS], grp_sel, start=True, stop=True)
            pe.wait_ge(ptt_copied, 2)
            pe.wait_ge(po_copied, 1)
            for b in range(NS):
                out = bank[6 + b % 2]
                cols = slice(32 * (b // 4), 32 * (b // 4) + 32)
                if b >= 2:
                    pe.wait_ge(om_ready, b - 1)
                pe.wait_ge(ring_in[b % 2], ring_total(b))
                for g in range(PAGES):
                    grp = g % 4
                    last = pe.matmul(out[32 * grp:32 * grp + 32, :], scores[:, g, cols],
                                     ring[b % 2][:, g * AW:(g + 1) * AW], start=(g < 4), stop=(g >= PAGES - 4 and grp > 0))
                last.then_inc(unit_read, 1)
                pe.matmul(out[0:32, :], po_new[:, cols], v_new, start=False, stop=True).then_inc(pv_done, 1)
                if b >= 1:
                    columns_of(pe, b - 1)
                what = PROMPT_AFTER.get(b)
                if what == "project 0":
                    pe.wait_ge(mix_ready, 1)
                    pe.wait_ge(w_out_in, 16)
                    out_proj(0, bank[0:2])
                elif what == "project 1":
                    out_proj(1, bank[2:4])
                elif what == "turn 0":
                    turn_x1(0)
                elif what == "turn 1":
                    turn_x1(1)
            columns_of(pe, NS - 1)

            pe.wait_ge(sq_ready, 2)
            for s, (first, n) in enumerate(((OATT, 4), (OCONV, 2), (OMEM, 2))):
                for j in range(n):
                    last = pe.matmul(bank[4][:, 256 + s * NS:256 + (s + 1) * NS], ones, sq_s[:, first + j, :],
                                     start=(j == 0), stop=(j == n - 1))
            last.then_inc(ss_ready, 1)
            pe.wait_ge(mix_ready, 2)
            out_proj(2, bank[0:2])

            turn_x1(2)
            pe.wait_ge(ch_ready, 1)
            c0, c1, c2 = chosen[:, 0, :], chosen[:, 1, :], chosen[0:NS, 2, :]
            ranks, counts = bank[6], bank[6][:, 3 * E:4 * E]
            pe.matmul(ranks[:, 0:E], tri, c0, start=True, stop=True)
            pe.matmul(ranks[:, E:2 * E], ones, c0, start=True, stop=False)
            pe.matmul(ranks[:, E:2 * E], tri, c1, start=False, stop=True)
            pe.matmul(ranks[0:NS, 2 * E:3 * E], ones[:, 0:NS], c0, start=True, stop=False)
            pe.matmul(ranks[0:NS, 2 * E:3 * E], ones[:, 0:NS], c1, start=False, stop=False)
            pe.matmul(ranks[0:NS, 2 * E:3 * E], tri[0:NS, 0:NS], c2, start=False, stop=True)
            pe.matmul(counts, ones, c0, start=True, stop=False)
            pe.matmul(counts, ones, c1, start=False, stop=False)
            pe.matmul(counts, ones[0:NS, :], c2, start=False, stop=True).then_inc(cnt_ready, 1)
            pe.wait_ge(rp_ready, 1)
            for a, row in enumerate((starts, ends)):
                last = pe.transpose(bank[7][0:E, a * PARTS:(a + 1) * PARTS], row, ident[:, :])
            last.then_inc(rg_ready, 1)

            p_gate, p_up, p_gather, p_hid_t, p_x_t, p_down = bank[0:6]

            def gather(b_next):
                pe.wait_ge(hot_ready, b_next)
                for half in range(2):
                    for c in range(3):
                        rows = PARTS if c < 2 else NS
                        last = pe.matmul(p_gather[half * SLOTS:(half + 1) * SLOTS, :], slot_hot[0:rows, c, :],
                                         x_rows[0:rows, c, half * HALF:(half + 1) * HALF], start=(c == 0), stop=(c == 2))
                last.then_inc(gat_ready, 1)

            def turn_gathered(b_next):
                pe.wait_ge(gat_copied, b_next)
                for j in range(4):
                    last = pe.transpose(p_x_t[:, j * PARTS:(j + 1) * PARTS], xg[:, j * PARTS:(j + 1) * PARTS], ident[:, :])
                last.then_inc(xgt_ready, 1)

            gather(1)
            turn_gathered(1)
            pe.wait_ge(table_ready, 1)
            pe.wait_ge(bias_in, 32)
            count = pe.value_load(n_blocks[0:1, 0:1], min_val=E, max_val=MAX_BLOCKS)
            with pe.Fori(0, MAX_BLOCKS) as b:
                with pe.If(b < count):
                    e = pe.value_load(block_expert[0:1, bass.ds(b, 1)], min_val=0, max_val=E - 1)
                    pe.wait_ge(xgt_copied, b + 1)
                    pe.wait_ge(bias_hot_ready, b + 1)
                    for half in range(2):
                        rows = slice(half * SLOTS, (half + 1) * SLOTS)
                        for out, at_col in ((p_gate, half * HALF), (p_up, FF + half * HALF)):
                            pe.matmul(out[rows, :], bias_hot, bias_rows_w[:, at_col:at_col + HALF], start=True, stop=False)
                    for k in range(KC):
                        pe.wait_ge(gu_in[k], e * 16 + 16)
                        for half in range(2):
                            rows = slice(half * SLOTS, (half + 1) * SLOTS)
                            for out, at_col in ((p_gate, half * HALF), (p_up, FF + half * HALF)):
                                last = pe.matmul(out[rows, :], xg_t[:, k % 4, k // 4, :],
                                                 gate_up_w[:, k, at_col:at_col + HALF], start=False, stop=(k == KC - 1))
                        last.then_inc(gu_used, 1)
                    pe.wait_ge(dn_copied, b + 1)
                    for half in range(2):
                        last = pe.matmul(p_down[half * SLOTS:(half + 1) * SLOTS, :], bias_hot,
                                         bias_rows_w[:, 2 * FF + half * HALF:2 * FF + (half + 1) * HALF],
                                         start=True, stop=False)
                    last.then_inc(hot_used, 1)
                    gather(b + 2)
                    pe.wait_ge(hd_ready, b + 1)
                    for j in range(4):
                        last = pe.transpose(p_hid_t[:, j * PARTS:(j + 1) * PARTS], hid[:, j * PARTS:(j + 1) * PARTS],
                                            ident[:, :])
                    last.then_inc(hdt_ready, 1)
                    turn_gathered(b + 2)
                    pe.wait_ge(hdt_copied, b + 1)
                    for k in range(KC):
                        pe.wait_ge(dn_in[k], e * 16 + 16)
                        for half in range(2):
                            last = pe.matmul(p_down[half * SLOTS:(half + 1) * SLOTS, :], hid_t[:, k % 4, k // 4, :],
                                             down_w[:, k, half * HALF:(half + 1) * HALF], start=False, stop=(k == KC - 1))
                        last.then_inc(dn_used, 1)
                with pe.Else():
                    pass
            pe.sem_inc(experts_done, 1)

        @block.scalar
        def _(act):
            def step(instruction):
                act.wait_ge(act_n.sem, act_n.on(instruction))

            act.dma_start(stage[0:KC, 0:PARTS], g_mix[0].rearrange("(j p) -> j p", p=PARTS)).then_inc(smalls_in, 16)
            act.dma_start(stage[0:3, 256:512], w_conv[0]).then_inc(smalls_in, 16)
            act.dma_start(stage[0:2 * NS, 512:768], state_conv[0].rearrange("b r c -> (b r) c")).then_inc(smalls_in, 16)
            act.dma_start(conv_sample[0, :, 0, :], state_conv[0, :, 1, :]).then_inc(out_done, 16)
            for i, (kind, n) in enumerate(tiles):
                src = bank[i % 4]
                act.wait_ge(tile_ready, i + 1)
                scale = 1.0
                if kind == "small":
                    dst, src = ((g_cols, src[:, 0:KC]), (w_cols, src[:, 0:6].rearrange("p (j i) -> p j i", j=2)),
                                (s_cols, src[:, 0:32].rearrange("p (j b r) -> p j b r", j=2, b=NS)))[n]
                elif kind == "xt":
                    dst, src = x_cols[:, n, :], src[:, 0:T]
                elif kind == "proj":
                    dst, src = p_cols[:, n, :], src[:, 0:T]
                    if n < CK or CM <= n < CB:
                        scale = QSCALE
                elif kind == "mt":
                    dst, src = mem_x[:, n, :], src[:, 0:NMEM]
                elif kind == "mkv":
                    dst, src = mem_cols[:, n, :], src[:, 0:NMEM]
                elif kind in ("qs", "ks", "vs"):
                    dst, src = {"qs": q_new, "ks": k_new, "vs": v_new}[kind], src[0:NS, :]
                elif kind == "qms":
                    dst, src = qm_new, src[0:NS, 0:MW]
                else:
                    dst = {"kr": k_rows, "vr": v_rows, "mr": mkv_rows}[kind][:, n, :]
                act.activation(dst, src, ACT.Copy, scale=scale).then_inc(tile_copied, 1)

            act.wait_ge(tile_copied, len(tiles))
            rows_of = lambda t: t.rearrange("(c p) h d -> p c (h d)", p=PARTS)
            act.dma_start(rows_of(k_prompt[0, 0]), k_rows).then_inc(rows_stored, 16)
            act.dma_start(rows_of(v_prompt[0, 0]), v_rows).then_inc(rows_stored, 16)
            act.dma_start(rows_of(mem_k_prompt[0, 0]), mkv_rows[:, :, 0:MW]).then_inc(rows_stored, 16)
            act.dma_start(rows_of(mem_v_prompt[0, 0]), mkv_rows[:, :, MW:2 * MW]).then_inc(rows_stored, 16)
            act.dma_start(k_sample[0, :, 0].rearrange("b h d -> b (h d)"), k_new).then_inc(rows_stored, 16)
            act.dma_start(v_sample[0, :, 0].rearrange("b h d -> b (h d)"), v_new).then_inc(rows_stored, 16)

            for i in range(NU + 2):
                if i < NU:
                    act.wait_ge(mx_ready, i + 1)
                    if i >= 2:
                        act.wait_ge(pt_ready, i - 1)
                    for c in range(2):
                        act.activation(probs[:, i % 2, c * NP:(c + 1) * NP], bank[i % 2][:, c * NP:(c + 1) * NP], ACT.Exp,
                                       bias=neg_max[:, i % 2, c:c + 1],
                                       accum_out=row_sum[:, i % 2, c:c + 1]).then_inc(exp_done, 1)
                if 1 <= i <= NU:
                    n = i - 1
                    act.wait_ge(pt_ready, n + 1)
                    if n == 0:
                        act.wait_ge(rows_stored, 16 * 6)
                    if n >= 2:
                        act.wait_ge(pv_ready, n - 1)
                    act.activation(probs_t[:, n % 2, :], bank[2 + n % 2][:, :], ACT.Copy).then_inc(pt_copied, 1)
                if 2 <= i:
                    n = i - 2
                    mem, h = units[n]
                    p = HD * (h % 2)
                    act.wait_ge(pv_ready, n + 1)
                    act.activation(o_cols[p:p + HD, (OMEM if mem else OATT) + h // 2, 0:NP],
                                   bank[4 + n % 2][p:p + HD, 0:NP], ACT.Copy).then_inc(o_copied, 1)

            act.wait_ge(ss_ready, 1)
            act.activation(rms_p[:, 0, :], bank[4][:, 0:NP], ACT.Sqrt, bias=eps, scale=1.0 / AW)
            act.activation(rms_p[:, 1, :], bank[4][:, NP:2 * NP], ACT.Sqrt, bias=eps, scale=1.0 / MW)
            act.activation(rms_p[:, 2, :], bank[5][:, 0:NP], ACT.Sqrt, bias=eps, scale=1.0 / MW).then_inc(rt_ready, 1)

            def layernorm_root(n, rows, c):
                act.wait_ge(res_ready, n)
                act.activation(ln_square(c)[0:rows], x_rows[0:rows, c, :], ACT.Square,
                               accum_out=ln_s[0:rows, c, 3:4]).then_inc(var_ready, 1)
                act.wait_ge(var_ready, n)
                act.activation(ln_s[0:rows, c, 4:5], ln_s[0:rows, c, 3:4], ACT.Sqrt, bias=eps[0:rows], scale=1.0 / D)\
                   .then_inc(root_ready, 1)

            act.wait_ge(sm_max, 1)
            act.activation(logits, logits, ACT.Exp, bias=stat[:, 2:3], accum_out=stat[:, 3:4]).then_inc(sm_exp, 1)
            act.activation(stat[:, 4:5], own, ACT.Exp, bias=stat[:, 2:3]).then_inc(sm_exp, 1)
            act.wait_ge(mm_max, 1)
            act.activation(mem_probs, bank[4][0:MROWS, 0:NMEM], ACT.Exp, bias=mstat[:, 0:1],
                           accum_out=mstat[:, 1:2]).then_inc(mm_exp, 1)
            act.wait_ge(ptt_ready, 1)
            for i in range(2):
                act.activation(scores[:, 8 * i:8 * i + 8, :], bank[2 + i][:, :].rearrange("p (g r) -> p g r", g=8), ACT.Copy)\
                   .then_inc(ptt_copied, 1)
            act.wait_ge(po_ready, 1)
            act.activation(po_new, bank[4][0:NS, 320:320 + ROWS], ACT.Copy).then_inc(po_copied, 1)
            act.activation(mem_pt, bank[4][:, 256:256 + 2 * MROWS].rearrange("p (g r) -> p g r", g=2), ACT.Copy)\
               .then_inc(mmt_copied, 1)
            layernorm_root(1, PARTS, 0)
            layernorm_root(2, PARTS, 1)
            for c in range(2):
                for i in range(2):
                    act.wait_ge(x1t_ready, 2 * c + i + 1)
                    act.activation(o_cols[:, 4 * i:4 * i + 4, c * PARTS:(c + 1) * PARTS],
                                   bank[2 + i][:, :].rearrange("p (k t) -> p k t", k=4), ACT.Copy).then_inc(x1t_copied, 1)
            act.wait_ge(oc_ready, NS)
            act.activation(o_cols[:, OATT:OATT + 4, NP:T], bank[5][:, 320:320 + 4 * NS].rearrange("p (j b) -> p j b", j=4),
                           ACT.Copy).then_inc(oc_copied, 1)
            act.activation(o_cols[:, OMEM:OMEM + 2, NP:T], bank[5][:, 256:256 + 2 * NS].rearrange("p (j b) -> p j b", j=2),
                           ACT.Copy).then_inc(oc_copied, 1)
            act.wait_ge(ss_ready, 2)
            act.activation(rms_s[:, 0:NS], bank[4][:, 256:256 + NS], ACT.Sqrt, bias=eps, scale=1.0 / AW)
            act.activation(rms_s[:, NS:3 * NS], bank[4][:, 256 + NS:256 + 3 * NS], ACT.Sqrt, bias=eps, scale=1.0 / MW)\
               .then_inc(rt_ready, 1)
            layernorm_root(3, NS, 2)
            for i in range(2):
                act.wait_ge(x1t_ready, 5 + i)
                act.activation(o_cols[:, 4 * i:4 * i + 4, NP:T],
                               bank[2 + i][:, :].rearrange("p (k t) -> p k t", k=4)[:, :, 0:NS], ACT.Copy)\
                   .then_inc(x1t_copied, 1)
            act.wait_ge(xm_ready, 1)
            act.activation(w4, w4, ACT.Exp).then_inc(xe_ready, 1)
            act.wait_ge(rg_ready, 1)
            act.activation(expert_range[:, 0:1], bank[7][0:E, 0:1], ACT.Copy)
            act.activation(expert_range[:, 1:2], bank[7][0:E, PARTS:PARTS + 1], ACT.Copy).then_inc(rg_copied, 1)

            def copy_gathered(n):
                act.wait_ge(gat_ready, n)
                act.activation(xg, bank[2][:, :], ACT.Copy).then_inc(gat_copied, 1)

            def copy_turned(n):
                act.wait_ge(xgt_ready, n)
                act.activation(xg_t.rearrange("p j h s -> p (j h s)"), bank[4][:, :], ACT.Copy).then_inc(xgt_copied, 1)

            copy_gathered(1)
            copy_turned(1)
            act.wait_ge(table_ready, 1)
            count = act.value_load(n_blocks[0:1, 0:1], min_val=E, max_val=MAX_BLOCKS)
            act.sem_inc(dn_copied, 1)
            rows_dst = expert_rows.rearrange("(b s) d -> b s d", s=SLOTS)
            act.wait_ge(spare_zeroed, 16)
            with act.Fori(0, MAX_BLOCKS) as b:
                with act.If(b < count):
                    act.wait_ge(g_ready, b + 1)
                    act.activation(sig_v, gate_v, ACT.Sigmoid, scale=SW_ALPHA).then_inc(sg_ready, 1)
                    copy_gathered(b + 2)
                    act.wait_ge(hdt_ready, b + 1)
                    act.activation(hid_t.rearrange("p j h s -> p (j h s)"), bank[3][:, :], ACT.Copy).then_inc(hdt_copied, 1)
                    copy_turned(b + 2)
                    act.wait_ge(dn_used, b * KC + KC)
                    act.activation(out_rows, bank[5][:, :], ACT.Copy).then_inc(dn_copied, 1)
                    act.wait_ge(dn_copied, b + 2)
                    for half in range(2):
                        act.dma_start(rows_dst[bass.ds(b, 1), :, half * HALF:(half + 1) * HALF].rearrange("a s d -> (a s) d"),
                                      out_rows[half * SLOTS:(half + 1) * SLOTS, :]).then_inc(rows_out, 16)
                    act.wait_ge(rows_out, b * 32 + 32)
                    act.sem_inc(block_stored, 1)
                with act.Else():
                    pass
            act.sem_inc(all_stored, 1)
            for c in range(3):
                rows = PARTS if c < 2 else NS
                act.wait_ge(fin_sq, c + 1)
                act.activation(gathered[0:rows, 12 + c, :], x_rows[0:rows, c, :], ACT.Square,
                               accum_out=ln_s[0:rows, c, 3:4]).then_inc(fin_rt, 1)
                act.wait_ge(fin_rt, 2 * c + 1)
                act.activation(ln_s[0:rows, c, 4:5], ln_s[0:rows, c, 3:4], ACT.Sqrt, bias=eps[0:rows], scale=1.0 / D)\
                   .then_inc(fin_rt, 1)

        @block.gpsimd
        def _(pool):
            def step(instruction):
                pool.wait_ge(pool_n.sem, pool_n.on(instruction))

            def iota(dst, pattern, base=0, cm=0):
                return pool.iota(dst, pattern, base=base, channel_multiplier=cm, allow_small_or_imprecise_dtypes=True)

            step(pool.memset(ident, 0.0))
            pool.affine_select(ident, ident, [[-1, PARTS]], ALU.not_equal, 1.0, base=0, channel_multiplier=1)\
                .then_inc(eye_ready, 1)
            pool.iota(rowi[:, 0:1], [[1, 1]], base=0, channel_multiplier=1).then_inc(rowi_ready, 1)
            pool.memset(ones, 1.0)
            step(pool.memset(tri, 1.0))
            step(pool.affine_select(tri, tri, [[1, PARTS]], ALU.is_ge, 0.0, base=-1, channel_multiplier=-1))
            pool.memset(eps, EPS)
            iota(iota8, [[1, 8]])
            for h in range(HEADS):
                pool.memset(slope8[:, h:h + 1], 2.0 ** (-8.0 * (h + 1) / HEADS))
            step(iota(dist, [[-1, 3 * PARTS]], base=PARTS, cm=1))
            step(pool.affine_select(dist, dist, [[-1, 3 * PARTS]], ALU.is_ge, BIG, base=PARTS, channel_multiplier=1))
            step(pool.memset(delta8, 1.0))
            step(pool.affine_select(delta8, delta8, [[1, NS], [0, HEADS]], ALU.is_equal, 0.0, base=0, channel_multiplier=-1))
            pool.memset(lg.rearrange("p c e -> p (c e)"), 0.0)
            iota(iota32, [[1, E]])
            iota(slot_id, [[1, SLOTS]]).then_inc(const_ready, 1)
            pool.wait_ge(const_ready, 1)

            cache_row = "n (r t) h d -> (n r) (t h d)"
            rows_k = cache_k[0].rearrange(cache_row, r=PARTS // PAGES)
            rows_v = cache_v[0].rearrange(cache_row, r=PARTS // PAGES)

            def load_batch(rows, b, half):
                pool.indirect_dma_start(ring[half][:, :], None, rows,
                                        bass.IndirectOffsetOnAxis(ap=page_row[:, b:b + 1], axis=0),
                                        bounds_check=NPHYS * (PARTS // PAGES) - 1).then_inc(ring_in[half], 16)

            def load_keys(b):
                if b == 2:
                    pool.wait_ge(tile_ready, tile_no[("mkv", 3)] + 1)
                else:
                    before = max(i for i in range(b) if K_HALF[i] == K_HALF[b])
                    pool.wait_ge(k_scored, 2 * (before + 1))
                load_batch(rows_k, b, K_HALF[b])

            pool.wait_ge(page_rows_ready, 1)
            load_batch(rows_k, 0, K_HALF[0])
            for b in range(1, 5):
                load_keys(b)
            pool.wait_ge(tile_copied, len(tiles))
            for h in range(HEADS):
                last = pool.tensor_scalar(head_slope_eye[:, h, :], ident, -2.0 ** (-8.0 * (h + 1) / HEADS), None, ALU.mult)
            last.then_inc(eyes_ready, 1)
            iota(logits, [[1, PAGES], [PAGES, PARTS]], base=-PAST).then_inc(logits_iota, 1)
            load_keys(5)

            u = p_cols[:, CC:CC + 2, :]
            step(pool.tensor_tensor(u, u, p_cols[:, CH:CH + 2, :], ALU.mult))
            pool.sem_inc(conv_u, 1)
            for j in range(2):
                o = o_cols[:, OCONV + j, 0:NP]
                t = p_cols[:, CH + j, 0:NP]
                step(pool.tensor_scalar(o, u[:, j, 0:NP], w_cols[:, j, 2:3], None, ALU.mult))
                for back in (1, 2):
                    step(pool.tensor_scalar(t[:, 0:NP - back], u[:, j, 0:NP - back], w_cols[:, j, 2 - back:3 - back], None,
                                            ALU.mult))
                    step(pool.tensor_tensor(o[:, back:NP], o[:, back:NP], t[:, 0:NP - back], ALU.add))
                step(pool.tensor_tensor(o, o, p_cols[:, CB + j, 0:NP], ALU.mult))
                so_, ts = o_cols[:, OCONV + j, NP:T], c_s[:, 0, j, :]
                step(pool.tensor_scalar(so_, u[:, j, NP:T], w_cols[:, j, 2:3], None, ALU.mult))
                for back in (1, 2):
                    step(pool.tensor_scalar(ts, s_cols[:, j, :, 2 - back], w_cols[:, j, 2 - back:3 - back], None, ALU.mult))
                    step(pool.tensor_tensor(so_, so_, ts, ALU.add))
                step(pool.tensor_tensor(so_, so_, p_cols[:, CB + j, NP:T], ALU.mult))
                load_keys(6 + j)
            pool.sem_inc(conv_done, 1)
            for j in range(2):
                cols = slice(j * PARTS, (j + 1) * PARTS)
                with nc.allow_non_contiguous_dma(reason="two rows of the convolution state"):
                    pool.dma_start(conv_prompt[0, 0][:, cols].rearrange("r p -> p r"), u[:, j, NP - 2:NP]).then_inc(conv_stored, 16)
                    pool.dma_start(conv_sample[0, :, 1, cols].rearrange("b p -> p b"), u[:, j, NP:T]).then_inc(conv_stored, 16)

            def load_router():
                pool.wait_ge(pv_ready, NU)
                iota(block_iota, [[1, MAX_BLOCKS + 1]]).then_inc(table_iota, 1)
                with nc.allow_non_contiguous_dma(reason="rows of 128 bytes"):
                    pool.dma_start(w_r, w_router[0].rearrange("(k p) e -> p k e", p=PARTS)).then_inc(router_in, 16)
                pool.dma_start(br_row, b_router[0][None, :].broadcast_to([PARTS, E])).then_inc(router_in, 16)

            for b in range(NS):
                if b == 3:
                    load_router()
                if b < 2:
                    pool.wait_ge(k_scored, 2 * (NS - 1 + b))
                else:
                    pool.wait_ge(unit_read, b - 1)
                load_batch(rows_v, b, b % 2)

            pool.wait_ge(unit_read, NS - 1)
            step(pool.memset(zero_rows, 0.0))
            spare = MAX_BLOCKS - E
            pool.dma_start(expert_rows[E * SLOTS:, :].rearrange("(c p) d -> p c d", p=PARTS),
                           zero_rows.unsqueeze(1).broadcast_to([PARTS, spare * SLOTS // PARTS, D])).then_inc(spare_zeroed, 16)
            pool.wait_ge(table_ready, 1)
            pool.wait_ge(slot_rows_ready, 1)
            pool.wait_ge(all_stored, 1)
            for c in range(3):
                rows = PARTS if c < 2 else NS
                for k in range(TOPK):
                    pool.indirect_dma_start(gathered[0:rows, c * TOPK + k, :], None, expert_rows,
                                            bass.IndirectOffsetOnAxis(ap=slot_rows[0:rows, c, k:k + 1], axis=0),
                                            bounds_check=MAX_BLOCKS * SLOTS - 1).then_inc(row_in_sems[c], 16)

        @block.vector
        def _(dve):
            def step(instruction):
                dve.wait_ge(dve_n.sem, dve_n.on(instruction))

            dve.wait_ge(rowi_ready, 1)
            step(dve.tensor_scalar(rowi[:, 1:2], rowi[:, 0:1], HEADS - 1, None, ALU.bitwise_and))
            step(dve.tensor_scalar(rowi[:, 2:3], rowi[:, 0:1], 3, 3, ALU.logical_shift_right, ALU.bitwise_and))
            step(dve.tensor_scalar(rowi[:, 3:4], rowi[:, 0:1], 5, None, ALU.logical_shift_right))
            step(dve.tensor_scalar(rowi[:, 4:5], rowi[:, 0:1], 3, None, ALU.bitwise_and))
            step(dve.tensor_scalar(rowi[:, 5:6], rowi[:, 0:1], 2, 7, ALU.logical_shift_right, ALU.bitwise_and))
            step(dve.tensor_scalar(rowi[:, 6:7], rowi[:, 0:1], 3, None, ALU.logical_shift_right))
            step(dve.tensor_copy(row_f[:, 0:7], rowi[:, 0:7]))
            dve.wait_ge(pages_in, 16 * NS)
            step(dve.tensor_copy(page_f, page_of[:, :]))
            step(dve.tensor_scalar(page_f, page_f, float(PARTS // PAGES), row_f[:, 1:2], ALU.mult, ALU.add))
            dve.tensor_copy(page_row[:, :], page_f).then_inc(page_rows_ready, 1)
            dve.wait_ge(const_ready, 1)
            step(dve.tensor_scalar(hot8, iota8, row_f[:, 1:2], None, ALU.is_equal))
            step(dve.tensor_tensor(slope8, slope8, hot8, ALU.mult))
            step(dve.tensor_reduce(slope, slope8, AX.X, ALU.add))
            step(dve.tensor_scalar(row_sel, iota8[:, 0:4], row_f[:, 2:3], None, ALU.is_equal))
            step(dve.tensor_scalar(grp_sel, iota8[:, 0:4], row_f[:, 3:4], None, ALU.is_equal))
            step(dve.tensor_scalar(q_sel, iota8[:, 0:2], 4.0, row_f[:, 3:4], ALU.mult, ALU.add))
            step(dve.tensor_scalar(q_sel, q_sel, row_f[:, 5:6], None, ALU.is_equal))
            for q in range(2):
                step(dve.tensor_scalar(hot4[:, q, :], iota8[:, 0:MHEADS], row_f[:, 4:5], q_sel[:, q:q + 1],
                                       ALU.is_equal, ALU.mult))
            step(dve.tensor_scalar(dsel, iota8[0:ROWS], row_f[0:ROWS, 6:7], None, ALU.is_equal))
            dve.sem_inc(sel_ready, 1)

            def score_keys(slot):
                b, part = slot // 2, slot % 2
                half, at_j = K_HALF[b], part * PAGES // 2
                r = ring[half][:, part * PAGES * AW // 2:(part + 1) * PAGES * AW // 2]
                if part == 0:
                    dve.wait_ge(ring_in[half], keys_total(b))
                    dve.wait_ge(qb_ready, b + 1)
                pages_r = r.rearrange("p (g n) -> p g n", g=PAGES // 2)
                q = bank[6 + b % 2][:, :].unsqueeze(1).broadcast_to([PARTS, PAGES // 2, AW])
                step(dve.tensor_tensor(pages_r, pages_r, q, ALU.mult))
                dve.tensor_reduce(scores[:, at_j:at_j + PAGES // 2, b * HEADS:(b + 1) * HEADS],
                                  r.rearrange("p (g h d) -> p g h d", g=PAGES // 2, h=HEADS),
                                  AX.X, ALU.add).then_inc(k_scored, 1)

            for slot in range(FIRST_SLOT + NU + 1):
                n = slot - FIRST_SLOT - 1
                if n >= 0:
                    dve.wait_ge(exp_done, 2 * (n + 1))
                    if n >= 2:
                        dve.wait_ge(norm_done, n - 1)
                    step(dve.reciprocal(row_inv[:, n % 2, :], row_sum[:, n % 2, :]))
                    pn = probs[:, n % 2, :].rearrange("p (c k) -> p c k", c=2)
                    dve.tensor_tensor(pn, pn, row_inv[:, n % 2, :].unsqueeze(2).broadcast_to([PARTS, 2, NP]), ALU.mult)\
                       .then_inc(norm_done, 1)
                n = slot - FIRST_SLOT
                if 0 <= n < NU:
                    dve.wait_ge(sc_ready, n + 1)
                    dve.tensor_reduce(neg_max[:, n % 2, :], bank[n % 2][:, :].rearrange("p (c k) -> p c k", c=2), AX.X,
                                      ALU.max, negate=True).then_inc(mx_ready, 1)
                if slot < SCORE_SLOTS:
                    score_keys(slot)

            dve.wait_ge(tile_copied, len(tiles))
            own_prod = gate_up_w[0:NS, 2, 2 * AW:3 * AW]
            step(dve.tensor_tensor(own_prod, q_new, k_new, ALU.mult))
            step(dve.tensor_reduce(so, own_prod.rearrange("p (h d) -> p h d", h=HEADS), AX.X, ALU.add))
            dve.tensor_tensor(so_spread.rearrange("p (b h) -> p b h", b=NS), delta8.rearrange("p (b h) -> p b h", b=NS),
                              so.unsqueeze(1).broadcast_to([NS, NS, HEADS]), ALU.mult).then_inc(so_ready, 1)
            def layernorm_center(c, banks, order):
                rows = PARTS if c < 2 else NS
                x, s = x_rows[0:rows, c, :], ln_s[0:rows, c]
                dve.wait_ge(proj_ready, order)
                for half in range(2):
                    cols = slice(half * HALF, (half + 1) * HALF)
                    step(dve.scalar_tensor_tensor(x[:, cols], x[:, cols], ALPHA, banks[half][0:rows, :], ALU.mult, ALU.add,
                                                  accum_out=s[:, half:half + 1]))
                step(dve.tensor_scalar(s[:, 2:3], s[:, 0:1], s[:, 1:2], -1.0 / D, ALU.add, ALU.mult))
                dve.tensor_scalar(x, x, s[:, 2:3], None, ALU.add).then_inc(res_ready, 1)

            def layernorm_scale(c, order):
                rows = PARTS if c < 2 else NS
                x, s = x_rows[0:rows, c, :], ln_s[0:rows, c]
                dve.wait_ge(root_ready, order)
                step(dve.reciprocal(s[:, 5:6], s[:, 4:5]))
                step(dve.scalar_tensor_tensor(x, x, s[:, 5:6], ln1_gain[0:rows], ALU.mult, ALU.mult))
                dve.tensor_tensor(x, x, ln1_bias[0:rows], ALU.add).then_inc(x1_ready, 1)

            dve.wait_ge(own_ready, 1)
            step(dve.tensor_copy(own, bank[5][0:ROWS, 511:512]))
            dve.wait_ge(l_ready, 1)
            for i in range(4):
                step(dve.tensor_reduce(gate_part[:, :, i], bank[i][0:ROWS, :].rearrange("p (j n q) -> p n j q", j=4, n=NBLK),
                                       AX.XY, ALU.add))
            step(dve.tensor_reduce(gate8, gate_part, AX.X, ALU.add))
            step(dve.max(top8, gate8))
            step(dve.max_index(seli[:, :], top8, gate8))
            step(dve.tensor_copy(seli_f, seli[:, :]))
            step(dve.tensor_scalar(pen, iota8[0:ROWS], seli_f[:, 0:1], None, ALU.is_equal))
            for i in (1, 2):
                step(dve.scalar_tensor_tensor(pen, iota8[0:ROWS], seli_f[:, i:i + 1], pen, ALU.is_equal, ALU.add))
            step(dve.tensor_scalar(pen, pen, -1.0, BIG, ALU.add, ALU.mult))
            dve.wait_ge(logits_iota, 1)
            for i in range(4):
                l = logits[:, i * 512:(i + 1) * 512]
                step(dve.scalar_tensor_tensor(l, l, slope[0:ROWS], bank[i][0:ROWS, :], ALU.mult, ALU.add))
            lb = logits.rearrange("p (j n q) -> p j n q", j=PAGES, n=NBLK)
            step(dve.tensor_tensor(lb, lb, pen.unsqueeze(1).unsqueeze(3).broadcast_to([ROWS, PAGES, NBLK, BLK // PAGES]),
                                   ALU.add))
            step(dve.tensor_reduce(stat[:, 0:1], logits, AX.X, ALU.max))
            step(dve.tensor_tensor(stat[:, 1:2], stat[:, 0:1], own, ALU.max))
            dve.tensor_scalar(stat[:, 2:3], stat[:, 1:2], -1.0, None, ALU.mult).then_inc(sm_max, 1)
            dve.wait_ge(o_copied, NU)
            dve.wait_ge(conv_done, 1)
            dve.tensor_tensor(squares, o_cols[:, :, 0:NP], o_cols[:, :, 0:NP], ALU.mult).then_inc(sq_ready, 1)
            dve.wait_ge(mem_kv_in, 32)
            for i in range(NS // 2):
                dve.wait_ge(qb_ready, NS + i + 1)
                r = mem_k[:, 2 * i:2 * i + 2]
                q = bank[6 + i % 2][:, :].rearrange("p (b n) -> p b n", b=2).unsqueeze(2).broadcast_to([PARTS, 2, 2, MW])
                step(dve.tensor_tensor(r, r, q, ALU.mult))
                for b in (2 * i, 2 * i + 1):
                    last = dve.tensor_reduce(mem_scores[:, :, b * MHEADS:(b + 1) * MHEADS],
                                             mem_k[:, b].rearrange("p g (h d) -> p g h d", h=MHEADS), AX.X, ALU.add)
                last.then_inc(mem_scored, 1)
            dve.wait_ge(sm_exp, 2)
            step(dve.tensor_tensor(stat[:, 5:6], stat[:, 3:4], stat[:, 4:5], ALU.add))
            step(dve.reciprocal(stat[:, 6:7], stat[:, 5:6]))
            step(dve.tensor_tensor(stat[:, 7:8], stat[:, 4:5], stat[:, 6:7], ALU.mult))
            step(dve.tensor_scalar(po_spread, dsel, stat[:, 7:8], None, ALU.mult))
            dve.tensor_scalar(logits, logits, stat[:, 6:7], None, ALU.mult).then_inc(sm_p, 1)

            dve.wait_ge(mm_ready, 1)
            dve.tensor_reduce(mstat[:, 0:1], bank[4][0:MROWS, 0:NMEM], AX.X, ALU.max, negate=True).then_inc(mm_max, 1)
            dve.wait_ge(mm_exp, 1)
            step(dve.reciprocal(mstat[:, 2:3], mstat[:, 1:2]))
            dve.tensor_scalar(mem_probs, mem_probs, mstat[:, 2:3], None, ALU.mult).then_inc(mm_norm, 1)
            dve.wait_ge(rt_ready, 1)
            step(dve.reciprocal(rms_p, rms_p))
            for s, (first, n) in enumerate(((OATT, 4), (OCONV, 2), (OMEM, 2))):
                for j in range(first, first + n):
                    last = dve.scalar_tensor_tensor(o_cols[:, j, 0:NP], o_cols[:, j, 0:NP], g_cols[:, j:j + 1],
                                                    rms_p[:, s, :], ALU.mult, ALU.mult)
            last.then_inc(mix_ready, 1)
            dve.wait_ge(mpv_done, 1)
            dve.tensor_tensor(mem_masked.rearrange("p q (h d) -> p (q h) d", h=MHEADS),
                              bank[1][:, :].rearrange("p (q d) -> p q d", d=HD),
                              hot4.rearrange("p q h -> p (q h)").unsqueeze(2).broadcast_to([PARTS, 2 * MHEADS, HD]),
                              ALU.mult).then_inc(mom_ready, 1)
            hot_head = hot8.unsqueeze(2).broadcast_to([PARTS, HEADS, HD])
            for b in range(NS):
                dve.wait_ge(pv_done, b + 1)
                if b >= 2:
                    dve.wait_ge(oc_ready, b - 1)
                dve.scalar_tensor_tensor(o_masked[:, b % 2, :].rearrange("p (h d) -> p h d", h=HEADS),
                                         bank[6 + b % 2][:, :].rearrange("p (h d) -> p h d", h=HEADS),
                                         row_sel[:, b % 4:b % 4 + 1], hot_head, ALU.mult, ALU.mult).then_inc(om_ready, 1)
                if b == 2:
                    layernorm_center(0, bank[0:2], 1)
                elif b == 3:
                    layernorm_center(1, bank[2:4], 2)
                    dve.wait_ge(ln1_in, 32)
                    layernorm_scale(0, 1)
                    layernorm_scale(1, 2)
            dve.wait_ge(oc_copied, 2)
            step(dve.tensor_tensor(sq_s, o_cols[:, :, NP:T], o_cols[:, :, NP:T], ALU.mult))
            dve.sem_inc(sq_ready, 1)
            dve.wait_ge(rt_ready, 2)
            step(dve.reciprocal(rms_s, rms_s))
            for first, n, s in ((OATT, 4, 0), (OCONV, 2, 1), (OMEM, 2, 2)):
                for j in range(first, first + n):
                    last = dve.scalar_tensor_tensor(o_cols[:, j, NP:T], o_cols[:, j, NP:T], g_cols[:, j:j + 1],
                                                    rms_s[:, s * NS:(s + 1) * NS], ALU.mult, ALU.mult)
            last.then_inc(mix_ready, 1)
            layernorm_center(2, bank[0:2], 3)
            layernorm_scale(2, 3)

            dve.wait_ge(lg_ready, 3)
            dve.wait_ge(router_in, 32)
            pl = bank[4][:, 0:3 * E].rearrange("p (c e) -> p c e", c=3)
            step(dve.tensor_tensor(lg[:, 0:2, :], pl[:, 0:2, :], br_row.unsqueeze(1).broadcast_to([PARTS, 2, E]), ALU.add))
            step(dve.tensor_tensor(lg[0:NS, 2, :], pl[0:NS, 2, :], br_row[0:NS], ALU.add))
            for c in range(3):
                step(dve.max(max8[:, c, :], lg[:, c, :]))
                step(dve.max_index(topi[:, c, :], max8[:, c, :], lg[:, c, :]))
            step(dve.tensor_copy(topf, topi[:, :, :]))
            dve.tensor_tensor(w4, max8[:, :, 0:TOPK], max8[:, :, 0:1].broadcast_to([PARTS, 3, TOPK]), ALU.subtract)\
               .then_inc(xm_ready, 1)
            step(dve.tensor_tensor(onehot, iota32.unsqueeze(1).unsqueeze(1).broadcast_to([PARTS, 3, TOPK, E]),
                                   topf[:, :, 0:TOPK].unsqueeze(3).broadcast_to([PARTS, 3, TOPK, E]), ALU.is_equal))
            dve.tensor_reduce(chosen, onehot.rearrange("p c k e -> p c e k"), AX.X, ALU.add).then_inc(ch_ready, 1)
            dve.wait_ge(cnt_ready, 1)
            cnt = bank[6][:, 3 * E:4 * E]
            step(dve.tensor_scalar(nb, cnt, float(SLOTS), 1.0, ALU.is_gt, ALU.add))
            for m in range(2, -(-T // SLOTS)):
                step(dve.scalar_tensor_tensor(nb, cnt, float(m * SLOTS), nb, ALU.is_gt, ALU.add))
            step(dve.tensor_tensor_scan(ends, ones[:, 0:E], nb, 0.0, ALU.mult, ALU.add))
            step(dve.tensor_tensor(starts, ends, nb, ALU.subtract))
            dve.sem_inc(rp_ready, 1)
            step(dve.memset(slots_g.rearrange("p c e -> p (c e)"), 0.0))
            st = starts.unsqueeze(1).broadcast_to([PARTS, 2, E])
            step(dve.scalar_tensor_tensor(slots_g[:, 0:2, :], st, float(SLOTS),
                                          bank[6][:, 0:2 * E].rearrange("p (c e) -> p c e", c=2), ALU.mult, ALU.add))
            step(dve.scalar_tensor_tensor(slots_g[0:NS, 2, :], starts[0:NS], float(SLOTS), bank[6][0:NS, 2 * E:3 * E],
                                          ALU.mult, ALU.add))
            step(dve.tensor_tensor(oh_g, onehot, slots_g.unsqueeze(2).broadcast_to([PARTS, 3, TOPK, E]), ALU.mult))
            step(dve.tensor_reduce(slot4, oh_g, AX.X, ALU.add))

            def slots(wait_used, n):
                if wait_used is not None:
                    dve.wait_ge(gat_ready, wait_used)
                    dve.wait_ge(step_b, wait_used)
                dve.tensor_tensor(slot_eq, slot_id.unsqueeze(1).unsqueeze(1).broadcast_to([PARTS, 3, TOPK, SLOTS]),
                                  slot4.unsqueeze(3).broadcast_to([PARTS, 3, TOPK, SLOTS]), ALU.is_equal).then_inc(step_a, 1)
                dve.wait_ge(step_a, n)
                dve.tensor_scalar(slot_id, slot_id, float(SLOTS), None, ALU.add).then_inc(step_b, 1)
                dve.tensor_reduce(slot_hot, slot_eq.rearrange("p c k s -> p c s k"), AX.X, ALU.add).then_inc(hot_ready, 1)

            def bias_rows(n):
                dve.wait_ge(step_c, n)
                dve.tensor_scalar(block_ge, block_id, expert_range[:, 0:1], None, ALU.is_ge).then_inc(step_d, 1)
                dve.wait_ge(step_d, n)
                dve.scalar_tensor_tensor(bias_hot, block_id, expert_range[:, 1:2], block_ge, ALU.is_lt, ALU.mult)\
                   .then_inc(bias_hot_ready, 1)
                dve.wait_ge(bias_hot_ready, n)
                dve.tensor_scalar(block_id, block_id, 1.0, None, ALU.add).then_inc(step_c, 1)

            slots(None, 1)
            step(dve.memset(block_id, 0.0))
            bi = MAX_BLOCKS + 1
            dve.wait_ge(table_iota, 1)
            step(dve.tensor_tensor(ends_cmp, block_iota.unsqueeze(2).broadcast_to([1, bi, E]),
                                   ends[0:1].unsqueeze(1).broadcast_to([1, bi, E]), ALU.is_ge))
            step(dve.tensor_reduce(block_ef, ends_cmp, AX.X, ALU.add))
            step(dve.tensor_scalar(block_ef, block_ef, float(E - 1), None, ALU.min))
            step(dve.tensor_copy(block_expert[:, :], block_ef))
            step(dve.tensor_scalar(block_ef[:, 0:E], ends[0:1], -1.0, None, ALU.add))
            step(dve.tensor_copy(last_block[:, :], block_ef[:, 0:E]))
            dve.tensor_copy(n_blocks[:, :], ends[0:1, E - 1:E]).then_inc(table_ready, 1)
            dve.tensor_copy(slot_rows[:, :, :], slot4).then_inc(slot_rows_ready, 1)
            dve.wait_ge(xe_ready, 1)
            step(dve.tensor_reduce(w4s, w4, AX.X, ALU.add))
            step(dve.reciprocal(w4s, w4s))
            step(dve.tensor_tensor(w4, w4, w4s.unsqueeze(2).broadcast_to([PARTS, 3, TOPK]), ALU.mult))
            dve.wait_ge(rg_copied, 1)
            dve.sem_inc(step_c, 1)
            bias_rows(1)
            dve.wait_ge(table_ready, 1)
            count = dve.value_load(n_blocks[0:1, 0:1], min_val=E, max_val=MAX_BLOCKS)
            with dve.Fori(0, MAX_BLOCKS) as b:
                with dve.If(b < count):
                    slots(b + 1, b + 2)
                    dve.wait_ge(gu_used, b * KC + KC)
                    dve.tensor_scalar(gate_v, bank[0][:, :], LIMIT, None, ALU.min).then_inc(g_ready, 1)
                    dve.tensor_scalar(up_v, bank[1][:, :], -LIMIT, LIMIT, ALU.max, ALU.min).then_inc(gu_read, 1)
                    dve.wait_ge(g_ready, b + 1)
                    dve.wait_ge(gu_read, b + 1)
                    dve.scalar_tensor_tensor(up_v, up_v, 1.0, gate_v, ALU.add, ALU.mult).then_inc(up_ready, 1)
                    dve.wait_ge(up_ready, b + 1)
                    dve.wait_ge(sg_ready, b + 1)
                    dve.tensor_tensor(hid, up_v, sig_v, ALU.mult).then_inc(hd_ready, 1)
                    dve.wait_ge(hot_used, b + 1)
                    bias_rows(b + 2)
                with dve.Else():
                    pass

            dve.wait_ge(ln2_in, 32)
            dve.wait_ge(experts_done, 1)
            for c in range(3):
                rows = PARTS if c < 2 else NS
                x, s = x_rows[0:rows, c, :], ln_s[0:rows, c]
                step(dve.tensor_scalar(x, x, ALPHA, None, ALU.mult))
                dve.wait_ge(row_in_sems[c], 16 * TOPK)
                for k in range(TOPK):
                    more = {"accum_out": s[:, 0:1]} if k == TOPK - 1 else {}
                    step(dve.scalar_tensor_tensor(x, gathered[0:rows, c * TOPK + k, :], w4[0:rows, c, k:k + 1], x,
                                                  ALU.mult, ALU.add, **more))
                step(dve.tensor_scalar(s[:, 2:3], s[:, 0:1], -1.0 / D, None, ALU.mult))
                dve.tensor_scalar(x, x, s[:, 2:3], None, ALU.add).then_inc(fin_sq, 1)
                dve.wait_ge(fin_rt, 2 * c + 2)
                step(dve.reciprocal(s[:, 5:6], s[:, 4:5]))
                step(dve.scalar_tensor_tensor(x, x, s[:, 5:6], ln2_gain[0:rows], ALU.mult, ALU.mult))
                dve.tensor_tensor(x, x, ln2_bias[0:rows], ALU.add).then_inc(y_ready, 1)


_INS = ['x_prompt', 'x_sample', 'cache_k', 'cache_v', 'cache_mem_k', 'cache_mem_v', 'state_conv', 'page_table',
        'mem_prompt', 'w_in', 'w_mem_kv', 'w_conv', 'g_mix', 'w_out', 'ln1_g', 'ln1_b', 'w_router', 'b_router',
        'w_gate_up', 'b_gate_up', 'w_down', 'b_down', 'ln2_g', 'ln2_b']


def kernel(**inputs):
    import numpy as np
    import concourse.bacc as bacc
    from concourse.bass_utils import run_bass_kernel_spmd

    nc = bacc.Bacc("TRN2", target_bir_lowering=False, num_devices=1)
    arrays, args = {}, []
    for name in _INS:
        a = np.ascontiguousarray(inputs[name])
        arrays[f"in_{name}"] = a
        args.append(nc.dram_tensor(f"in_{name}", a.shape, mybir.dt.from_np(a.dtype), kind="ExternalInput").ap())
    xp, xs, ck, mk, st = (inputs[n].shape for n in ('x_prompt', 'x_sample', 'cache_k', 'cache_mem_k', 'state_conv'))
    heads = (ck[3], ck[4])
    outs = [xp, xs, (1, 1, xp[1], *heads), (1, 1, xp[1], *heads), (1, 1, *st[2:]), (1, 1, *mk[2:]), (1, 1, *mk[2:]),
            (1, xs[0], 1, *heads), (1, xs[0], 1, *heads), tuple(st)]
    for i, shape in enumerate(outs):
        args.append(nc.dram_tensor(f"out_{i}", shape, F32, kind="ExternalOutput").ap())
    blocks = 32 + (xp[1] + xs[0]) * 4 // 65
    args.append(nc.dram_tensor("expert_rows", (blocks * 64, xp[2]), F32, kind="Internal").ap())
    layer_kernel(nc, *args)
    r = run_bass_kernel_spmd(nc, [arrays], core_ids=[0])
    return tuple(r.results[0][f"out_{i}"] for i in range(len(outs)))
```

```python
from contextlib import ExitStack

import concourse.bass as bass
from concourse import mybir

ALU = mybir.AluOpType
ACT = mybir.ActivationFunctionType
AX = mybir.AxisListType
F32 = mybir.dt.float32
BF16 = mybir.dt.bfloat16
I32 = mybir.dt.int32
U32 = mybir.dt.uint32

BIG = 1.0e30
PARTS = 128


class Counter:

    def __init__(self, sem):
        self.sem, self.n = sem, 0

    def on(self, instruction):
        instruction.then_inc(self.sem, 1)
        self.n += 1
        return self.n


def layer_kernel(nc, x_prompt, x_sample, cache_k, cache_v, cache_mem_k, cache_mem_v, state_conv, page_table,
                 mem_prompt, w_in, w_mem_kv, w_conv, g_mix, w_out, ln1_g, ln1_b, w_router, b_router,
                 w_gate_up, b_gate_up, w_down, b_down, ln2_g, ln2_b,
                 y_prompt, y_sample, k_prompt, v_prompt, conv_prompt, mem_k_prompt, mem_v_prompt,
                 k_sample, v_sample, conv_sample):
    D = x_prompt.shape[2]
    NP = x_prompt.shape[1]
    NS = x_sample.shape[0]
    T = NP + NS
    KC = D // PARTS
    HD = 64
    HEADS = cache_k.shape[3]
    MHEADS = cache_mem_k.shape[3]
    AW = HEADS * HD
    MW = MHEADS * HD
    NMEM = mem_prompt.shape[1]
    PAGES = page_table.shape[1]
    NPHYS = cache_k.shape[1]
    PAST = PAGES * PARTS
    BLK = 256
    NBLK = PAST // BLK
    PC = w_in.shape[2] // PARTS
    E = w_router.shape[2]
    FF = w_down.shape[2]
    TOPK = 4
    SLOTS = 64
    MAX_BLOCKS = E + (T * TOPK) // (SLOTS + 1)
    HALF = D // 2
    QSCALE = HD ** -0.5
    ALPHA = 2.0 ** 0.25
    EPS = 1e-5
    LIMIT = 7.0
    SW_ALPHA = 1.702
    ROWS = NS * HEADS
    MROWS = NS * MHEADS
    assert ROWS == 64 and NP == 256 and PARTS == page_table.shape[1] * NS and PC == 20
    CQ, CK, CV, CM, CB, CC, CH = 0, 4, 8, 12, 14, 16, 18
    OATT, OCONV, OMEM = 0, 4, 6

    ctx = ExitStack()
    with ctx:
        def sb(name, shape, dt=F32):
            return ctx.enter_context(nc.sbuf_tensor(name, shape, dt))

        def sem(name):
            return ctx.enter_context(nc.semaphore(name))

        CONSTS, SMALLS = 1320, 912
        gate_up_w = sb("gate_up_w", [PARTS, KC, 2 * FF])
        down_w = sb("down_w", [PARTS, KC, D])
        ring = [sb("ring_a", [PARTS, PAGES * AW]), sb("ring_b", [PARTS, PAGES * AW])]
        x_rows = sb("x_rows", [PARTS, 3, D])
        x_cols = sb("x_cols", [PARTS, KC, T])
        work = sb("work", [PARTS, 2 * KC * NMEM])
        consts = sb("consts", [PARTS, CONSTS])
        small = sb("small", [PARTS, SMALLS])
        page_of = sb("page_of", [PARTS, NS], I32)
        page_row = sb("page_row", [PARTS, 2 * NS], I32)
        topi = sb("topi", [PARTS, 3, 8], U32)
        seli = sb("seli", [ROWS, 8], U32)
        rowi = sb("rowi", [PARTS, 9], I32)
        k_turned_b = sb("k_turned_b", [PARTS, AW])
        block_expert = sb("block_expert", [1, MAX_BLOCKS + 1], I32)
        last_block = sb("last_block", [1, E], I32)
        n_blocks = sb("n_blocks", [1, 1], I32)
        bank = [ctx.enter_context(nc.psum_tensor(f"bank{i}", [PARTS, 512], F32))[:, :] for i in range(8)]

        used = {"c": 0, "s": 0}

        def const(n, rows=PARTS):
            a = used["c"]
            used["c"] += n
            assert used["c"] <= CONSTS
            return consts[0:rows, a:a + n]

        def scratch(n, rows=PARTS):
            a = used["s"]
            used["s"] += n
            assert used["s"] <= SMALLS
            return small[0:rows, a:a + n]

        w_in_a = gate_up_w
        RA, RB = ring
        w_in_b = RA[:, 0:KC * 512].rearrange("p (k n) -> p k n", k=KC)
        w_mem = RA[:, KC * 512:2 * KC * 512].rearrange("p (k n) -> p k n", k=KC)
        down_flat = down_w[:, :, :].rearrange("p k n -> p (k n)")
        p_cols = down_flat[:, 0:PC * T].rearrange("p (j t) -> p j t", j=PC)
        at = PC * T
        at_scores = at
        scores = down_flat[:, at:at + PAGES * ROWS].rearrange("p (g r) -> p g r", g=PAGES)
        at += PAGES * ROWS
        mem_cols = down_flat[:, at:at + 4 * NMEM].rearrange("p (j t) -> p j t", j=4)
        stage = down_flat[:, at:at + 4 * NMEM]
        at += 4 * NMEM
        q_new = down_flat[0:NS, at:at + AW]
        at += AW
        qm_new = down_flat[0:NS, at:at + MW]
        at += MW
        assert at <= KC * D
        head_slope_eye = gate_up_w[:, 0, 0:HEADS * PARTS].rearrange("p (h c) -> p h c", h=HEADS)
        squares = gate_up_w[:, 0, :].rearrange("p (j t) -> p j t", j=KC)
        ln_gained = gate_up_w[:, 0, D:2 * D]
        ln1_gain, ln1_bias = gate_up_w[:, 1, 0:D], gate_up_w[:, 1, D:2 * D]
        k_new, v_new = gate_up_w[0:NS, 2, 0:AW], gate_up_w[0:NS, 2, AW:2 * AW]
        mem_v = gate_up_w[:, 4:6, :].rearrange("p s (b g c) -> p (s b) g c", b=4, g=2)
        mem_k = gate_up_w[:, 6:8, :].rearrange("p s (b g c) -> p (s b) g c", b=4, g=2)
        mem_masked = gate_up_w[:, 2, 3 * AW:4 * AW].rearrange("p (q c) -> p q c", q=2)
        logits = gate_up_w[0:ROWS, 3, 0:PAST]
        w_o = gate_up_w[:, 4:8, :].rearrange("p s (u n) -> p (s u) n", u=2)
        mem_rows = work[:, 0:2 * D].rearrange("p (c d) -> p c d", c=2)
        mem_x = work[:, 2 * D:2 * D + KC * NMEM].rearrange("p (k t) -> p k t", k=KC)
        k_rows = work[:, 0:2 * AW].rearrange("p (c d) -> p c d", c=2)
        v_rows = work[:, 2 * AW:4 * AW].rearrange("p (c d) -> p c d", c=2)
        mkv_rows = work[:, 4 * AW:6 * AW].rearrange("p (c d) -> p c d", c=2)
        probs = work[:, 6 * AW:8 * AW].rearrange("p (b k) -> p b k", b=2)
        probs_t = work[:, 0:AW]
        k_turned = [work[:, AW:2 * AW], k_turned_b]
        o_masked = v_rows
        sample_parts = v_rows
        mem_probs = probs[0:MROWS, 1, NMEM:2 * NMEM]
        o_cols = x_cols
        bias_left = down_flat[0:3 * E, 0:2 * FF + D]
        bias_up = work[0:3 * E, 0:FF].bitcast(BF16)
        bias_down = work[0:3 * E, 6 * AW:6 * AW + D // 2].bitcast(BF16)
        expert_sum = RA[:, 2 * FF + D:2 * FF + D + KC * T].rearrange("p (j t) -> p j t", j=KC)
        ln2_gain, ln2_bias = RA[:, 6 * D:7 * D], RA[:, 7 * D:8 * D]
        rb = {"n": 0}

        def part_b(n, rows=PARTS):
            a = rb["n"]
            rb["n"] += n
            assert rb["n"] <= PAGES * AW
            return RB[0:rows, a:a + n]

        xg = part_b(HALF)
        xg_t = part_b(HALF).rearrange("p (j h s) -> p j h s", j=4, h=2)
        gate_v, up_v, sig_v, hid = part_b(HALF), part_b(HALF), part_b(HALF), part_b(HALF)
        ends_cmp = RB[0:1, rb["n"] - 4 * HALF:rb["n"] - 4 * HALF + (MAX_BLOCKS + 1) * E].rearrange("p (b e) -> p b e", e=E)
        oh_g = RB[:, rb["n"] - 3 * TOPK * E:rb["n"]].rearrange("p (c k e) -> p c k e", c=3, k=TOPK)
        assert (MAX_BLOCKS + 1) * E + 3 * TOPK * E <= 4 * HALF
        hid_t = part_b(HALF).rearrange("p (j h s) -> p j h s", j=4, h=2)
        out_rows = part_b(HALF)
        slot_eq = part_b(3 * TOPK * SLOTS).rearrange("p (c k s) -> p c k s", c=3, k=TOPK)
        slot_hot = part_b(3 * SLOTS).rearrange("p (c s) -> p c s", c=3)
        onehot = part_b(3 * TOPK * E).rearrange("p (c k e) -> p c k e", c=3, k=TOPK)
        slot_weight = part_b(3 * PARTS).rearrange("p (c s) -> p c s", c=3)
        slot_weight_t = part_b(3 * PARTS)

        ident = const(PARTS)
        ones = const(PARTS)
        tri = const(PARTS)
        ones_b, tri_b = const(PARTS // 2).bitcast(BF16), const(PARTS // 2).bitcast(BF16)
        dist = const(3 * PARTS)
        eps = const(1)
        row_f = const(9)
        hot_chunk = const(4 * HEADS).rearrange("p (j h) -> p j h", j=4)
        q_head_cols = const(4 * NS * HEADS).rearrange("p (j b h) -> p j b h", j=4, b=NS)
        iota8 = const(8)
        hot8 = const(8)
        slope8 = const(8)
        slope = const(1)
        row_sel = const(4)
        sum_groups = const(NS)
        sum_logits = part_b(E)
        grp_sel = const(4)
        q_sel = const(2)
        hot4 = const(2 * MHEADS).rearrange("p (q h) -> p q h", q=2)
        delta8 = const(ROWS, NS)
        dsel = const(8, ROWS)
        g_cols = scratch(KC)
        page_f = scratch(NS)
        page_rows_f = scratch(2 * NS).rearrange("p (b i) -> p b i", b=NS)
        w_cols = scratch(6).rearrange("p (j i) -> p j i", j=2)
        s_cols = scratch(4 * NS).rearrange("p (j b r) -> p j b r", j=2, b=NS)
        mem_scores = scratch(2 * MROWS).rearrange("p (g r) -> p g r", g=2)
        mem_pt = scratch(2 * MROWS).rearrange("p (g r) -> p g r", g=2)
        so = scratch(8, NS)
        so_spread = scratch(ROWS, NS)
        po_new = scratch(ROWS, NS)
        po_spread = scratch(8, ROWS)
        own = scratch(1, ROWS)
        stat = scratch(16, ROWS)
        gate8 = scratch(8, ROWS)
        gate_part = scratch(4 * NBLK, ROWS).rearrange("p (n i) -> p n i", n=NBLK)
        top8 = scratch(8, ROWS)
        seli_f = scratch(8, ROWS)
        pen = scratch(8, ROWS)
        mstat = scratch(4, MROWS)
        neg_max = scratch(4).rearrange("p (b c) -> p b c", b=2)
        row_sum = scratch(4).rearrange("p (b c) -> p b c", b=2)
        row_inv = scratch(4).rearrange("p (b c) -> p b c", b=2)
        c_s = scratch(2 * NS).rearrange("p (j b) -> p j b", j=2)
        sq_s = part_b(KC * 32).rearrange("p (j t) -> p j t", j=KC)
        rms_s = scratch(1)
        ln_s = scratch(3 * 8).rearrange("p (c i) -> p c i", c=3)
        lg = scratch(3 * E).rearrange("p (c e) -> p c e", c=3)
        br_row = scratch(E)
        max8 = scratch(24).rearrange("p (c k) -> p c k", c=3)
        topf = scratch(24).rearrange("p (c k) -> p c k", c=3)
        w4 = scratch(3 * TOPK).rearrange("p (c k) -> p c k", c=3)
        w4s = scratch(3)
        chosen = part_b(3 * E // 2).bitcast(BF16).rearrange("p (c e) -> p c e", c=3)
        iota32 = scratch(E)
        nb = scratch(E)
        ends = scratch(E)
        starts = scratch(E)
        slots_g = part_b(3 * E).rearrange("p (c e) -> p c e", c=3)
        slot4 = scratch(3 * TOPK).rearrange("p (c k) -> p c k", c=3)
        slot_id = scratch(SLOTS)
        logit_parts = work[:, 7 * AW:7 * AW + NP]
        rms_p = work[:, 6 * AW:6 * AW + 3 * NP].rearrange("p (s t) -> p s t", s=3)
        w_r = work[:, 4 * AW:4 * AW + KC * E].rearrange("p (k e) -> p k e", k=KC)
        expert_range = work[0:3 * E, 5 * AW:5 * AW + 2]
        block_id = work[0:3 * E, 5 * AW + 200:5 * AW + 200 + SLOTS]
        block_ge = work[0:3 * E, 5 * AW + 264:5 * AW + 264 + SLOTS]
        bias_hot = work[0:3 * E, 5 * AW + 100:5 * AW + 100 + SLOTS // 2].bitcast(BF16)
        block_iota = work[0:1, 5 * AW + 360:5 * AW + 360 + MAX_BLOCKS + 1]
        block_ef = work[0:1, 5 * AW + 410:5 * AW + 410 + MAX_BLOCKS + 1]
        assert 410 + MAX_BLOCKS + 1 <= 512

        x_in, mem_in, pages_in, smalls_in = sem("x_in"), sem("mem_in"), sem("pages_in"), sem("smalls_in")
        w_q_in, w_k_in, w_v_in, w_m_in = sem("w_q_in"), sem("w_k_in"), sem("w_v_in"), sem("w_m_in")
        w_ch_in, w_mem_in, w_out_in, ln1_in = sem("w_ch_in"), sem("w_mem_in"), sem("w_out_in"), sem("ln1_in")
        router_in, ln2_in, bias_in = sem("router_in"), sem("ln2_in"), sem("bias_in")
        sum_ready, sum_added = sem("token_columns_ready"), sem("token_columns_added")
        sums_zeroed, moe_ready, pieces_ready = sem("sums_zeroed"), sem("moe_rows_ready"), sem("bias_pieces")
        left_ready, weighted, weight_ready = sem("bias_left"), sem("slots_weighted"), sem("slot_weights")
        weight_turned, weight_copied = sem("slot_weights_turned"), sem("slot_weights_copied")
        mem_scored, mem_kv_in, page_rows_ready = sem("mem_keys_scored"), sem("mem_kv_in"), sem("page_rows_ready")
        eye_ready, const_ready, rowi_ready = sem("eye_ready"), sem("const_ready"), sem("rowi_ready")
        tile_ready, tile_copied = sem("tile_ready"), sem("tile_copied")
        qb_ready, k_scored, eyes_ready = sem("query_spread"), sem("keys_scored"), sem("slope_eyes_ready")
        logits_iota, sc_ready, mx_ready = sem("logits_iota_ready"), sem("unit_scores"), sem("unit_max")
        exp_done, norm_done, pt_ready = sem("unit_exp"), sem("unit_norm"), sem("unit_turned")
        pt_copied, pv_ready, o_copied = sem("unit_turned_copied"), sem("unit_pv"), sem("unit_out_copied")
        conv_done, sq_ready, ss_ready = sem("conv_done"), sem("squares_ready"), sem("square_sums")
        rt_ready, mix_ready, proj_ready = sem("rms_root"), sem("mix_ready"), sem("out_proj")
        res_ready, var_ready, root_ready = sem("centered_ready"), sem("variance_ready"), sem("root_ready")
        x1_ready, x1t_ready, x1t_copied = sem("x1_ready"), sem("x1_turned"), sem("x1_turned_copied")
        lg_ready, so_ready, own_ready = sem("router_logits"), sem("own_spread"), sem("own_score")
        l_ready, sm_max, sm_exp = sem("score_rows"), sem("softmax_max"), sem("softmax_exp")
        sm_p, ptt_ready, ptt_copied = sem("softmax_done"), sem("probs_turned"), sem("probs_turned_copied")
        po_ready, po_copied, pv_done = sem("own_prob_spread"), sem("own_prob_copied"), sem("page_values")
        om_ready, oc_ready, oc_copied = sem("o_masked"), sem("o_cols"), sem("o_cols_copied")
        unit_read, mm_ready, mm_max, mm_exp = sem("values_read"), sem("mem_rows"), sem("mem_max"), sem("mem_exp")
        mm_norm, mmt_ready, mmt_copied = sem("mem_norm"), sem("mem_turned"), sem("mem_turned_copied")
        mpv_done, mom_ready, xm_ready = sem("mem_values"), sem("mem_masked"), sem("router_shift")
        xe_ready, ch_ready, cnt_ready = sem("router_exp"), sem("chosen_ready"), sem("counts_ready")
        rp_ready, rg_ready, rg_copied = sem("ranges_spread"), sem("ranges_turned"), sem("ranges_copied")
        table_ready, parts_ready = sem("block_table"), sem("sample_parts")
        parts_copied, hot_ready, hot_used = sem("sample_parts_copied"), sem("slots_hot"), sem("slots_used")
        gat_ready, gat_copied, xgt_ready = sem("gathered"), sem("gathered_copied"), sem("gathered_turned")
        xgt_copied, gu_used = sem("gathered_turned_copied"), sem("gate_up_tiles_used")
        g_ready, sg_ready, hd_ready = sem("gate_clamped"), sem("sigmoid"), sem("hidden")
        hdt_ready, hdt_copied, gu_read = sem("hidden_turned"), sem("hidden_turned_copied"), sem("gate_up_read")
        dn_used, dn_copied, step_a = sem("down_tiles_used"), sem("down_copied"), sem("slot_equal")
        step_b, step_c, step_d = sem("slot_id_next"), sem("block_id_next"), sem("block_at_start")
        up_ready, bias_hot_ready, table_iota = sem("up_times_gate"), sem("bias_row_hot"), sem("block_numbers")
        rows_stored, conv_stored, y_ready = sem("key_value_rows_stored"), sem("conv_stored"), sem("y_ready")
        out_done, fin_sq, fin_rt = sem("outputs_stored"), sem("final_squares"), sem("final_root")
        gained, page_turned, page_copied = sem("final_rows_gained"), sem("page_turned"), sem("page_copied")
        page_scored, page_kept, q_cols_ready = sem("page_scored"), sem("page_scores_kept"), sem("query_columns")
        lgt_ready, lgt_copied, lgt_ones = sem("logit_parts"), sem("logit_parts_copied"), sem("logit_selector")
        inverse_ready, prompt_logits_read = sem("sample_rms_inverse"), sem("prompt_logits_read")
        ring_in = [[sem("ring_a_low_in"), sem("ring_a_high_in")], [sem("ring_b_low_in"), sem("ring_b_high_in")]]
        gu_in = [sem(f"gate_up_in{k}") for k in range(KC)]
        dn_in = [sem(f"down_in{k}") for k in range(KC)]
        dve_n, pool_n = Counter(sem("dve_step")), Counter(sem("pool_step"))

        tiles = ([("small", i) for i in range(3)] + [("xt", k) for k in range(KC)] + [("proj", CQ + j) for j in range(4)] +
                 [("qs", 0)] + [("proj", CC + j) for j in range(4)] + [("mt", k) for k in range(KC)] +
                 [("mkv", j) for j in range(4)] + [("proj", CK + j) for j in range(8)] +
                 [("proj", CM + j) for j in range(4)] + [("qms", 0)] +
                 [("kr", 0), ("kr", 1), ("vr", 0), ("vr", 1), ("ks", 0), ("vs", 0), ("mr", 0), ("mr", 1)])
        tile_no = {t: i for i, t in enumerate(tiles)}
        SPREAD_AFTER = {("qs", 0): (0, 1), ("mkv", 3): (2,), ("proj", CK + 4): (3,), ("proj", CM + 1): (4,)}
        units = [(True, h) for h in range(MHEADS)] + [(False, h) for h in range(HEADS)]
        NU = len(units)
        SCORE_SLOTS = 2 * NS
        FIRST_SLOT = 9
        TURN_FROM, TURN_PAGES = 5, 2
        TURNED = (NS - TURN_FROM) * 2 * TURN_PAGES
        assert 2 * TURN_FROM > FIRST_SLOT and TURN_PAGES == 2

        def pages_beside(i):
            m = i - 2 * (2 * TURN_FROM - FIRST_SLOT)
            return (m,) if 0 <= m < TURNED else ()

        SPREAD_BEFORE_UNIT = {max(0, 4 * b - 3 - 2 * FIRST_SLOT): b for b in range(5, NS)}
        K_HALF = [1, 1] + [b % 2 for b in range(2, NS)]

        def ring_total(b):
            return 16 * (K_HALF.count(b % 2) + b // 2 + 1)

        def turned_total(b, part):
            return TURN_PAGES * (2 * (b - TURN_FROM) + part + 1) if b >= TURN_FROM else 0

        MEM_BANK = [bank[4], bank[1], bank[0], bank[1]]
        MEMORY_AFTER = 1

        def keys_total(b):
            return 16 * K_HALF[:b + 1].count(K_HALF[b])

        def columns_of(pe, b):
            pe.wait_ge(om_ready, b + 1)
            for j in range(4):
                last = pe.matmul(bank[5][:, 320 + j * NS + b:321 + j * NS + b], o_masked[:, b % 2, j * PARTS:(j + 1) * PARTS],
                                 ones[:, 0:1], start=True, stop=True)
            last.then_inc(oc_ready, 1)

        def ln_square(c):
            return gate_up_w[:, 0, 0:D]

        block = ctx.enter_context(nc.Block())

        @block.sync
        def _(sp):
            sp.dma_start(x_rows[:, 0:2, :], x_prompt[0].rearrange("(c p) d -> p c d", p=PARTS)).then_inc(x_in, 16)
            sp.dma_start(x_rows[0:NS, 2, :], x_sample[:, 0, :]).then_inc(x_in, 16)
            with nc.allow_non_contiguous_dma(reason="page numbers, one a partition"):
                for b in range(NS):
                    sp.dma_start(page_of[:, b:b + 1],
                                 page_table[b].unsqueeze(1).broadcast_to([PAGES, PARTS // PAGES])).then_inc(pages_in, 16)
            w_in_k = w_in[0].rearrange("(k p) n -> p k n", p=PARTS)
            sp.dma_start(w_in_a[:, :, 0:512], w_in_k[:, :, 0:512]).then_inc(w_q_in, 16)
            sp.dma_start(w_in_b, w_in_k[:, :, 2048:2560]).then_inc(w_ch_in, 16)
            sp.dma_start(mem_rows, mem_prompt[0].rearrange("(c p) d -> p c d", p=PARTS)).then_inc(mem_in, 16)
            sp.dma_start(w_mem, w_mem_kv[0].rearrange("(k p) n -> p k n", p=PARTS)).then_inc(w_mem_in, 16)
            sp.wait_ge(ring_in[1][1], 16)
            sp.dma_start(w_in_a[:, :, 512:1024], w_in_k[:, :, 512:1024]).then_inc(w_k_in, 16)
            sp.wait_ge(ring_in[1][1], 32)
            sp.dma_start(w_in_a[:, :, 1024:1536], w_in_k[:, :, 1024:1536]).then_inc(w_v_in, 16)
            sp.dma_start(w_in_a[:, :, 1536:2048], w_in_k[:, :, 1536:2048]).then_inc(w_m_in, 16)
            sp.wait_ge(tile_ready, tile_no[("proj", CB + 1)] + 1)
            sp.wait_ge(k_scored, 2 * NS - 5)
            for dst, cache in ((mem_k, cache_mem_k), (mem_v, cache_mem_v)):
                sp.dma_start(dst.rearrange("p b g c -> p b (g c)"),
                             cache[0].rearrange("b (p g) h d -> p b (g h d)", p=PARTS)).then_inc(mem_kv_in, 16)
            sp.dma_start(ln1_gain, ln1_g[0][None, :].broadcast_to([PARTS, D])).then_inc(ln1_in, 16)
            sp.dma_start(ln1_bias, ln1_b[0][None, :].broadcast_to([PARTS, D])).then_inc(ln1_in, 16)
            sp.wait_ge(pv_ready, NU)
            sp.wait_ge(conv_stored, 16 * 4)
            for r in range(3):
                sp.dma_start(bias_left[r * E:(r + 1) * E, 0:2 * FF], b_gate_up[0]).then_inc(bias_in, 16)
                sp.dma_start(bias_left[r * E:(r + 1) * E, 2 * FF:2 * FF + D], b_down[0]).then_inc(bias_in, 16)
            sp.wait_ge(mpv_done, 1)
            sp.dma_start(w_o, w_out[0].rearrange("(j p) n -> p j n", p=PARTS)).then_inc(w_out_in, 16)
            gu_k = w_gate_up[0].rearrange("e (k p) n -> e p k n", p=PARTS)
            dn_k = w_down[0].rearrange("e (k p) n -> e p k n", p=PARTS)
            sp.wait_ge(unit_read, 2 * (NS - 1))
            sp.dma_start(ln2_gain, ln2_g[0][None, :].broadcast_to([PARTS, D])).then_inc(ln2_in, 16)
            sp.dma_start(ln2_bias, ln2_b[0][None, :].broadcast_to([PARTS, D])).then_inc(ln2_in, 16)
            sp.wait_ge(pieces_ready, 3)

            def load_gate_up(*tiles_k):
                for k in tiles_k:
                    sp.dma_start(gate_up_w[:, k, :], gu_k[0, :, k, :]).then_inc(gu_in[k], 16)

            def load_down(*tiles_k):
                for k in tiles_k:
                    sp.dma_start(down_w[:, k, :], dn_k[0, :, k, :]).then_inc(dn_in[k], 16)

            load_down(*range(at_scores // D))
            load_gate_up(3)
            sp.wait_ge(unit_read, 2 * NS)
            sp.wait_ge(pv_done, NS)
            load_down(*range(at_scores // D, KC))
            sp.wait_ge(oc_copied, 2)
            load_gate_up(2)
            sp.wait_ge(proj_ready, 3)
            load_gate_up(4, 5, 6, 7)
            sp.wait_ge(x1_ready, 3)
            load_gate_up(0, 1)
            sp.wait_ge(table_ready, 1)
            with sp.Fori(1, E) as e:
                last = sp.value_load(last_block[0:1, bass.ds(e - 1, 1)], min_val=0, max_val=MAX_BLOCKS - 1)
                for k in range(KC):
                    sp.wait_ge(gu_used, last * KC + (k + 1))
                    sp.dma_start(gate_up_w[:, k, :],
                                 gu_k[bass.ds(e, 1), :, k, :].rearrange("a p n -> (a p) n")).then_inc(gu_in[k], 16)
                for k in range(KC):
                    sp.wait_ge(dn_used, last * KC + (k + 1))
                    sp.dma_start(down_w[:, k, :],
                                 dn_k[bass.ds(e, 1), :, k, :].rearrange("a p n -> (a p) n")).then_inc(dn_in[k], 16)
            sp.wait_ge(y_ready, 2)
            sp.dma_start(y_prompt[0].rearrange("(c p) d -> p c d", p=PARTS), x_rows[:, 0:2, :]).then_inc(out_done, 16)
            sp.wait_ge(y_ready, 3)
            sp.dma_start(y_sample[:, 0, :], x_rows[0:NS, 2, :]).then_inc(out_done, 16)
            sp.wait_ge(out_done, 16 * 3)
            sp.wait_ge(rows_stored, 16 * 6)
            sp.wait_ge(conv_stored, 16 * 4)

        @block.tensor
        def _(pe):
            def tile_wait(i):
                if i >= 4:
                    pe.wait_ge(tile_copied, i - 3)

            def copied(t):
                pe.wait_ge(tile_copied, tile_no[t] + 1)

            def spread(b):
                if b >= 2:
                    pe.wait_ge(k_scored, 2 * (b - 1))
                pe.matmul(bank[6 + b % 2][:, :], row_pick(b), q_new, start=True, stop=True).then_inc(qb_ready, 1)

            def row_pick(b):
                return ident[0:NS, b:b + 1].broadcast_to([NS, PARTS])

            pe.wait_ge(eye_ready, 1)
            for i, (kind, n) in enumerate(tiles):
                out = bank[i % 4]
                tile_wait(i)
                if kind == "small":
                    if n == 0:
                        pe.wait_ge(smalls_in, 48)
                        last = pe.transpose(out[:, 0:KC], stage[0:KC, 0:PARTS], ident[0:KC, 0:KC])
                    elif n == 1:
                        for j in range(2):
                            last = pe.transpose(out[:, j * 3:j * 3 + 3], stage[0:3, 256 + j * 128:384 + j * 128], ident[0:3, 0:3])
                    else:
                        for j in range(2):
                            last = pe.transpose(out[:, j * 16:j * 16 + 16], stage[0:16, 512 + j * 128:640 + j * 128],
                                                ident[0:16, 0:16])
                elif kind == "xt":
                    pe.wait_ge(x_in, 32)
                    for c in range(3):
                        rows = PARTS if c < 2 else NS
                        last = pe.transpose(out[:, c * PARTS:c * PARTS + rows],
                                            x_rows[0:rows, c, n * PARTS:(n + 1) * PARTS], ident[0:rows, 0:rows])
                elif kind == "proj":
                    pe.wait_ge(w_q_in if n < CK else w_k_in if n < CV else w_v_in if n < CM else w_m_in if n < CC else w_ch_in, 16)
                    copied(("xt", KC - 1))
                    for k in range(KC):
                        w = w_in_a[:, k, n * PARTS:(n + 1) * PARTS] if n < 16 else \
                            w_in_b[:, k, (n - 16) * PARTS:(n - 15) * PARTS]
                        last = pe.matmul(out[:, 0:T], w, x_cols[:, k, :], start=(k == 0), stop=(k == KC - 1))
                elif kind == "mt":
                    pe.wait_ge(mem_in, 16)
                    for c in range(2):
                        last = pe.transpose(out[:, c * PARTS:(c + 1) * PARTS],
                                            mem_rows[:, c, n * PARTS:(n + 1) * PARTS], ident[:, :])
                elif kind == "mkv":
                    pe.wait_ge(w_mem_in, 16)
                    copied(("mt", KC - 1))
                    for k in range(KC):
                        last = pe.matmul(out[:, 0:NMEM], w_mem[:, k, n * PARTS:(n + 1) * PARTS], mem_x[:, k, :],
                                         start=(k == 0), stop=(k == KC - 1))
                elif kind in ("qs", "ks", "vs", "qms"):
                    first, chunks = {"qs": (CQ, 4), "ks": (CK, 4), "vs": (CV, 4), "qms": (CM, 2)}[kind]
                    copied(("proj", first + chunks - 1))
                    for j in range(chunks):
                        last = pe.transpose(out[0:NS, j * PARTS:(j + 1) * PARTS], p_cols[:, first + j, NP:T], ident[:, :])
                else:
                    copied(("mkv", 3))
                    for j in range(4):
                        src = mem_cols[:, j, n * PARTS:(n + 1) * PARTS] if kind == "mr" else \
                            p_cols[:, (CK if kind == "kr" else CV) + j, n * PARTS:(n + 1) * PARTS]
                        last = pe.transpose(out[:, j * PARTS:(j + 1) * PARTS], src, ident[:, :])
                last.then_inc(tile_ready, 1)
                for b in SPREAD_AFTER.get((kind, n), ()):
                    copied(("qs", 0))
                    spread(b)

            def turn_page(m):
                slot = 2 * TURN_FROM + m // TURN_PAGES
                b, part = slot // 2, slot % 2
                g = (part + 1) * PAGES // 2 - TURN_PAGES + m % TURN_PAGES
                if m % TURN_PAGES == 0:
                    pe.wait_ge(ring_in[K_HALF[b]][part], keys_total(b))
                if m >= 2:
                    pe.wait_ge(page_copied, m - 1)
                for j in range(4):
                    last = pe.transpose(bank[(1, 5)[m % 2]][:, j * PARTS:(j + 1) * PARTS],
                                        ring[K_HALF[b]][:, g * AW + j * PARTS:g * AW + (j + 1) * PARTS], ident[:, :])
                last.then_inc(page_turned, 1)

            def score_page(m):
                b = TURN_FROM + m // (2 * TURN_PAGES)
                if m == 0:
                    pe.wait_ge(q_cols_ready, 1)
                pe.wait_ge(page_copied, m + 1)
                for j in range(4):
                    last = pe.matmul(bank[3][:, m * HEADS:(m + 1) * HEADS], k_turned[m % 2][:, j * PARTS:(j + 1) * PARTS],
                                     q_head_cols[:, j, b, :], start=(j == 0), stop=(j == 3))
                last.then_inc(page_scored, 1)

            pe.wait_ge(tile_copied, len(tiles))
            for i in range(NU + 2):
                if i in SPREAD_BEFORE_UNIT:
                    spread(SPREAD_BEFORE_UNIT[i])
                if i < NU:
                    mem, h = units[i]
                    p = HD * (h % 2)
                    if i >= 1:
                        pe.wait_ge(exp_done, 2 * i)
                    k = mem_cols[p:p + HD, h // 2, :] if mem else p_cols[p:p + HD, CK + h // 2, 0:NP]
                    for c in range(2):
                        out = bank[0][:, c * NP:(c + 1) * NP]
                        q = p_cols[p:p + HD, (CM if mem else CQ) + h // 2, c * PARTS:(c + 1) * PARTS]
                        last = pe.matmul(out, q, k, start=True, stop=mem)
                        if not mem:
                            if i == MHEADS:
                                pe.wait_ge(eyes_ready, 1)
                            last = pe.matmul(out, head_slope_eye[:, h, :], dist[:, PARTS * (1 - c):PARTS * (3 - c)],
                                             start=False, stop=True)
                    last.then_inc(sc_ready, 1)
                if 1 <= i <= NU:
                    n = i - 1
                    pe.wait_ge(norm_done, n + 1)
                    if n >= 1:
                        pe.wait_ge(pt_copied, n)
                    for g in range(2):
                        for c in range(2):
                            last = pe.transpose(bank[2][:, (2 * g + c) * PARTS:(2 * g + c + 1) * PARTS],
                                                probs[:, n % 2, (2 * c + g) * PARTS:(2 * c + g + 1) * PARTS], ident[:, :])
                    last.then_inc(pt_ready, 1)
                if 2 <= i:
                    n = i - 2
                    mem, h = units[n]
                    p = HD * (h % 2)
                    pe.wait_ge(pt_copied, n + 1)
                    if n >= 2:
                        pe.wait_ge(o_copied, n - 1)
                    for g in range(2):
                        v = mkv_rows[:, g, MW + h * HD:MW + (h + 1) * HD] if mem else v_rows[:, g, h * HD:(h + 1) * HD]
                        last = pe.matmul(bank[4][p:p + HD, (n % 2) * NP:(n % 2 + 1) * NP], v,
                                         probs_t[:, g * NP:(g + 1) * NP], start=(g == 0), stop=(g == 1))
                    last.then_inc(pv_ready, 1)
                for m in pages_beside(i):
                    turn_page(m)
                    if m:
                        score_page(m - 1)
            score_page(TURNED - 1)

            pe.wait_ge(o_copied, NU)
            pe.wait_ge(so_ready, 1)
            pe.matmul(bank[5][0:ROWS, 511:512], so_spread, ones[0:NS, 0:1], start=True, stop=True).then_inc(own_ready, 1)
            pe.wait_ge(k_scored, SCORE_SLOTS)
            pe.wait_ge(page_kept, NS - TURN_FROM)
            for g in range(PAGES):
                last = pe.transpose(bank[g // 4][0:ROWS, (g % 4) * PARTS:(g % 4 + 1) * PARTS], scores[:, g, :], ident[:, :])
                if g % 4 == 3:
                    last.then_inc(l_ready, 1)
            def memory_queries(i):
                if i == 3:
                    pe.wait_ge(mem_scored, 2)
                for b in (2 * i, 2 * i + 1):
                    last = pe.matmul(MEM_BANK[i][:, (b % 2) * MW:(b % 2 + 1) * MW], row_pick(b), qm_new,
                                     start=True, stop=True)
                last.then_inc(qb_ready, 1)

            memory_queries(0)
            pe.wait_ge(sm_p, 1)
            for g in range(PAGES):
                last = pe.transpose(bank[2 + g // 8][:, (g % 8) * ROWS:(g % 8 + 1) * ROWS],
                                    logits[:, g * PARTS:(g + 1) * PARTS], ident[0:ROWS, 0:ROWS])
            last.then_inc(ptt_ready, 1)
            pe.matmul(bank[5][0:NS, 320:320 + ROWS], po_spread, ident[0:ROWS, 0:ROWS], start=True, stop=True)\
                .then_inc(po_ready, 1)
            memory_queries(1)

            def out_proj(c, banks, halves=(0, 1)):
                rows = PARTS if c < 2 else NS
                for half in halves:
                    for j in range(KC):
                        last = pe.matmul(banks[half][0:rows, :], o_cols[:, j, c * PARTS:c * PARTS + rows],
                                         w_o[:, j, half * HALF:(half + 1) * HALF], start=(j == 0), stop=(j == KC - 1))
                if halves[-1] == 1:
                    last.then_inc(proj_ready, 1)

            def turn_x1(c):
                rows = PARTS if c < 2 else NS
                pe.wait_ge(x1_ready, c + 1)
                if c:
                    pe.wait_ge(x1t_copied, 2 * c)
                for k in range(KC):
                    last = pe.transpose(bank[2 + k // 4][:, (k % 4) * PARTS:(k % 4) * PARTS + rows],
                                        x_rows[0:rows, c, k * PARTS:(k + 1) * PARTS], ident[0:rows, 0:rows])
                    if k % 4 == 3:
                        last.then_inc(x1t_ready, 1)

            def prompt_logits():
                pe.wait_ge(x1t_copied, 4)
                pe.wait_ge(router_in, 32)
                for k in range(KC):
                    grp = k % 4
                    last = pe.matmul(bank[0][32 * grp:32 * grp + E, 0:NP], w_r[:, k, :], o_cols[:, k, 0:NP],
                                     start=(k < 4), stop=(k >= 4))
                last.then_inc(lgt_ready, 1)
                pe.wait_ge(lgt_copied, 1)
                pe.wait_ge(lgt_ones, 1)
                for c in range(2):
                    last = pe.matmul(bank[4][:, c * E:(c + 1) * E], logit_parts[:, c * PARTS:(c + 1) * PARTS], sum_logits,
                                     start=True, stop=True)
                last.then_inc(lg_ready, 1)

            def square_sums():
                pe.wait_ge(sq_ready, 1)
                sections = ((OATT, 4, bank[4][:, 0:NP]), (OCONV, 2, bank[4][:, NP:2 * NP]), (OMEM, 2, bank[5][:, 0:NP]))
                for first, n, out in sections:
                    for j in range(n):
                        last = pe.matmul(out, ones, squares[:, first + j, :], start=(j == 0), stop=(j == n - 1))
                last.then_inc(ss_ready, 1)

            def memory_rows():
                pe.wait_ge(mem_scored, NS // 2)
                pe.wait_ge(rt_ready, 1)
                for g in range(2):
                    last = pe.transpose(bank[4][0:MROWS, g * PARTS:(g + 1) * PARTS], mem_scores[:, g, :], ident[:, :])
                last.then_inc(mm_ready, 1)
                pe.wait_ge(mm_norm, 1)
                for g in range(2):
                    last = pe.transpose(bank[4][:, 256 + g * MROWS:256 + (g + 1) * MROWS],
                                        mem_probs[:, g * PARTS:(g + 1) * PARTS], ident[0:MROWS, 0:MROWS])
                last.then_inc(mmt_ready, 1)
                pe.wait_ge(mmt_copied, 1)
                for b in range(NS):
                    grp, q = b % 4, b // 4
                    for g in range(2):
                        last = pe.matmul(bank[1][32 * grp:32 * grp + 32, q * MW:(q + 1) * MW], mem_pt[:, g, :],
                                         mem_v[:, b, g, :], start=(g == 0), stop=(g == 1))
                last.then_inc(mpv_done, 1)
                pe.wait_ge(mom_ready, 1)
                for q in range(2):
                    for j in range(2):
                        last = pe.matmul(bank[5][:, 256 + j * NS + 4 * q:256 + j * NS + 4 * q + 4],
                                         mem_masked[:, q, j * PARTS:(j + 1) * PARTS], grp_sel, start=True, stop=True)

            pe.wait_ge(ptt_copied, 2)
            for b in range(NS):
                out = bank[6 + b % 2]
                cols = slice(32 * (b // 4), 32 * (b // 4) + 32)
                if b >= 2:
                    pe.wait_ge(om_ready, b - 1)
                for g in range(PAGES):
                    if g % (PAGES // 2) == 0:
                        if g:
                            last.then_inc(unit_read, 1)
                        pe.wait_ge(ring_in[b % 2][g // (PAGES // 2)], ring_total(b))
                    grp = g % 4
                    last = pe.matmul(out[32 * grp:32 * grp + 32, :], scores[:, g, cols],
                                     ring[b % 2][:, g * AW:(g + 1) * AW], start=(g < 4), stop=(g >= PAGES - 4 and grp > 0))
                last.then_inc(unit_read, 1)
                if b == 0:
                    pe.wait_ge(po_copied, 1)
                pe.matmul(out[0:32, :], po_new[:, cols], v_new, start=False, stop=True).then_inc(pv_done, 1)
                if b == 1:
                    pe.wait_ge(rt_ready, 1)
                if b >= 1:
                    columns_of(pe, b - 1)
                if b == 0:
                    memory_queries(2)
                    pe.wait_ge(mem_scored, 1)
                    square_sums()
                    memory_queries(3)
                elif b == MEMORY_AFTER:
                    memory_rows()
                elif MEMORY_AFTER < b <= MEMORY_AFTER + 4:
                    if b == MEMORY_AFTER + 1:
                        pe.wait_ge(mix_ready, 1)
                        pe.wait_ge(w_out_in, 16)
                    step_no = b - MEMORY_AFTER - 1
                    out_proj(step_no // 2, bank[0:2] if step_no < 2 else bank[2:4], [step_no % 2])
            columns_of(pe, NS - 1)

            turn_x1(0)
            pe.wait_ge(sq_ready, 2)
            sections = ((OATT, 4), (OATT, 4), (OCONV, 2), (OMEM, 2))
            for grp, (first, n) in enumerate(sections):
                for j in range(n):
                    last = pe.matmul(bank[5][32 * grp:32 * grp + 32, 256:257], sq_s[:, first + j, :], ones[:, 0:1],
                                     start=(j == 0), stop=(j == n - 1))
            last.then_inc(ss_ready, 1)
            pe.wait_ge(mix_ready, 2)
            for half in range(2):
                for j in (0, 2, 4, 6, 1, 3, 5, 7):
                    grp = j // 2
                    last = pe.matmul(bank[half][32 * grp:32 * grp + 32, :], o_cols[:, j, T - 32:T],
                                     w_o[:, j, half * HALF:(half + 1) * HALF], start=(j % 2 == 0), stop=(j % 2 == 1))
                last.then_inc(parts_ready, 1)
            for half in range(2):
                pe.wait_ge(parts_copied, half + 1)
                last = pe.matmul(bank[6 + half][0:NS, :], sum_groups, sample_parts[:, half, :], start=True, stop=True)
            last.then_inc(proj_ready, 1)
            turn_x1(1)
            prompt_logits()
            turn_x1(2)
            pe.wait_ge(x1t_copied, 6)
            pe.wait_ge(prompt_logits_read, 1)
            for k in range(KC):
                last = pe.matmul(bank[4][0:NS, 2 * E:3 * E], o_cols[:, k, NP:T], w_r[:, k, :],
                                 start=(k == 0), stop=(k == KC - 1))
            last.then_inc(lg_ready, 1)
            pe.wait_ge(ch_ready, 1)
            c0, c1, c2 = chosen[:, 0, :], chosen[:, 1, :], chosen[0:NS, 2, :]
            ranks, counts = bank[6], bank[6][:, 3 * E:4 * E]
            pe.matmul(ranks[:, 0:E], tri_b, c0, start=True, stop=True)
            pe.matmul(ranks[:, E:2 * E], ones_b, c0, start=True, stop=False)
            pe.matmul(ranks[:, E:2 * E], tri_b, c1, start=False, stop=True)
            pe.matmul(ranks[0:NS, 2 * E:3 * E], ones_b[:, 0:NS], c0, start=True, stop=False)
            pe.matmul(ranks[0:NS, 2 * E:3 * E], ones_b[:, 0:NS], c1, start=False, stop=False)
            pe.matmul(ranks[0:NS, 2 * E:3 * E], tri_b[0:NS, 0:NS], c2, start=False, stop=True)
            pe.matmul(counts, ones_b, c0, start=True, stop=False)
            pe.matmul(counts, ones_b, c1, start=False, stop=False)
            pe.matmul(counts, ones_b[0:NS, :], c2, start=False, stop=True).then_inc(cnt_ready, 1)
            pe.wait_ge(rp_ready, 1)
            for a, row in enumerate((starts, ends)):
                for r in range(3):
                    last = pe.matmul(bank[7][r * E:(r + 1) * E, a:a + 1], row, ident[:, 0:1], start=True, stop=True)
            last.then_inc(rg_ready, 1)

            p_gate, p_up, p_gather, p_hid_t, p_x_t, p_down = bank[0:6]

            def gather(b_next):
                pe.wait_ge(hot_ready, b_next)
                for c in range(3):
                    rows = PARTS if c < 2 else NS
                    for half in range(2):
                        last = pe.matmul(p_gather[half * SLOTS:(half + 1) * SLOTS, :], slot_hot[0:rows, c, :],
                                         x_rows[0:rows, c, half * HALF:(half + 1) * HALF], start=(c == 0), stop=(c == 2))
                last.then_inc(gat_ready, 1)

            def turn_gathered(b_next, weights=None):
                pe.wait_ge(gat_copied, b_next)
                if weights is not None:
                    pe.wait_ge(weight_copied, weights)
                for j in range(4):
                    last = pe.transpose(p_x_t[:, j * PARTS:(j + 1) * PARTS], xg[:, j * PARTS:(j + 1) * PARTS], ident[:, :])
                last.then_inc(xgt_ready, 1)

            def add_rows(n, j):
                half, cols = j // 4, slice((j % 4) * PARTS, (j % 4 + 1) * PARTS)
                parts = slice(half * SLOTS, (half + 1) * SLOTS)
                pe.wait_ge(sum_added, n * KC + (j + 1))
                pe.matmul(bank[6 + j % 2][:, 0:T], out_rows[parts, cols], slot_weight_t[parts, 0:T],
                          start=True, stop=True).then_inc(sum_ready, 1)

            gather(1)
            turn_gathered(1)
            pe.wait_ge(table_ready, 1)
            pe.wait_ge(pieces_ready, 3)
            count = pe.value_load(n_blocks[0:1, 0:1], min_val=E, max_val=MAX_BLOCKS)
            with pe.Fori(0, MAX_BLOCKS) as b:
                with pe.If(b < count):
                    e = pe.value_load(block_expert[0:1, bass.ds(b, 1)], min_val=0, max_val=E - 1)
                    pe.wait_ge(xgt_copied, b + 1)
                    pe.wait_ge(bias_hot_ready, b + 1)
                    for half in range(2):
                        rows = slice(half * SLOTS, (half + 1) * SLOTS)
                        for out, at_col in ((p_gate, half * HALF), (p_up, FF + half * HALF)):
                            pe.matmul(out[rows, :], bias_hot, bias_up[:, at_col:at_col + HALF], start=True, stop=False)
                    for k in range(KC):
                        pe.wait_ge(gu_in[k], e * 16 + 16)
                        for half in range(2):
                            rows = slice(half * SLOTS, (half + 1) * SLOTS)
                            for out, at_col in ((p_gate, half * HALF), (p_up, FF + half * HALF)):
                                last = pe.matmul(out[rows, :], xg_t[:, k % 4, k // 4, :],
                                                 gate_up_w[:, k, at_col:at_col + HALF], start=False, stop=(k == KC - 1))
                        last.then_inc(gu_used, 1)
                        if k == 0:
                            pe.wait_ge(dn_copied, b + 1)
                        add_rows(b, k)
                    pe.wait_ge(weight_ready, b + 1)
                    for c in range(3):
                        rows = PARTS if c < 2 else NS
                        last = pe.transpose(p_x_t[:, c * PARTS:c * PARTS + rows], slot_weight[0:rows, c, :],
                                            ident[0:rows, 0:rows])
                    last.then_inc(weight_turned, 1)
                    for half in range(2):
                        last = pe.matmul(p_down[half * SLOTS:(half + 1) * SLOTS, :], bias_hot,
                                         bias_down[:, half * HALF:(half + 1) * HALF],
                                         start=True, stop=False)
                    last.then_inc(hot_used, 1)
                    gather(b + 2)
                    pe.wait_ge(hd_ready, b + 1)
                    for j in range(4):
                        last = pe.transpose(p_hid_t[:, j * PARTS:(j + 1) * PARTS], hid[:, j * PARTS:(j + 1) * PARTS],
                                            ident[:, :])
                    last.then_inc(hdt_ready, 1)
                    turn_gathered(b + 2, b + 1)
                    pe.wait_ge(hdt_copied, b + 1)
                    for k in range(KC):
                        pe.wait_ge(dn_in[k], e * 16 + 16)
                        for half in range(2):
                            last = pe.matmul(p_down[half * SLOTS:(half + 1) * SLOTS, :], hid_t[:, k % 4, k // 4, :],
                                             down_w[:, k, half * HALF:(half + 1) * HALF], start=False, stop=(k == KC - 1))
                        last.then_inc(dn_used, 1)
                with pe.Else():
                    pass
            pe.wait_ge(dn_copied, count + 1)
            for j in range(KC):
                add_rows(count, j)
            for c in range(3):
                rows = PARTS if c < 2 else NS
                for j in range(KC):
                    if c == 0:
                        pe.wait_ge(sum_added, count * KC + (j + 3))
                    last = pe.transpose(bank[2 * c + j // 4][0:rows, (j % 4) * PARTS:(j % 4 + 1) * PARTS],
                                        expert_sum[:, j, c * PARTS:c * PARTS + rows], ident[:, :])
                last.then_inc(moe_ready, 1)

        @block.scalar
        def _(act):
            act.dma_start(stage[0:KC, 0:PARTS], g_mix[0].rearrange("(j p) -> j p", p=PARTS)).then_inc(smalls_in, 16)
            act.dma_start(stage[0:3, 256:512], w_conv[0]).then_inc(smalls_in, 16)
            act.dma_start(stage[0:2 * NS, 512:768], state_conv[0].rearrange("b r c -> (b r) c")).then_inc(smalls_in, 16)
            for i, (kind, n) in enumerate(tiles):
                src = bank[i % 4]
                act.wait_ge(tile_ready, i + 1)
                scale = 1.0
                if kind == "small":
                    dst, src = ((g_cols, src[:, 0:KC]), (w_cols, src[:, 0:6].rearrange("p (j i) -> p j i", j=2)),
                                (s_cols, src[:, 0:32].rearrange("p (j b r) -> p j b r", j=2, b=NS)))[n]
                elif kind == "xt":
                    dst, src = x_cols[:, n, :], src[:, 0:T]
                elif kind == "proj":
                    dst, src = p_cols[:, n, :], src[:, 0:T]
                    if n < CK or CM <= n < CB:
                        scale = QSCALE
                elif kind == "mt":
                    dst, src = mem_x[:, n, :], src[:, 0:NMEM]
                elif kind == "mkv":
                    dst, src = mem_cols[:, n, :], src[:, 0:NMEM]
                elif kind in ("qs", "ks", "vs"):
                    dst, src = {"qs": q_new, "ks": k_new, "vs": v_new}[kind], src[0:NS, :]
                elif kind == "qms":
                    dst, src = qm_new, src[0:NS, 0:MW]
                else:
                    dst = {"kr": k_rows, "vr": v_rows, "mr": mkv_rows}[kind][:, n, :]
                act.activation(dst, src, ACT.Copy, scale=scale).then_inc(tile_copied, 1)

            act.dma_start(conv_sample[0, :, 0, :], state_conv[0, :, 1, :]).then_inc(out_done, 16)
            act.wait_ge(tile_copied, len(tiles))
            rows_of = lambda t: t.rearrange("(c p) h d -> p c (h d)", p=PARTS)
            act.dma_start(rows_of(k_prompt[0, 0]), k_rows).then_inc(rows_stored, 16)
            act.dma_start(rows_of(v_prompt[0, 0]), v_rows).then_inc(rows_stored, 16)
            act.dma_start(rows_of(mem_k_prompt[0, 0]), mkv_rows[:, :, 0:MW]).then_inc(rows_stored, 16)
            act.dma_start(rows_of(mem_v_prompt[0, 0]), mkv_rows[:, :, MW:2 * MW]).then_inc(rows_stored, 16)
            act.dma_start(k_sample[0, :, 0].rearrange("b h d -> b (h d)"), k_new).then_inc(rows_stored, 16)
            act.dma_start(v_sample[0, :, 0].rearrange("b h d -> b (h d)"), v_new).then_inc(rows_stored, 16)

            for i in range(NU + 2):
                if i < NU:
                    act.wait_ge(mx_ready, i + 1)
                    if i >= 2:
                        act.wait_ge(pt_ready, i - 1)
                    for c in range(2):
                        act.activation(probs[:, i % 2, c * NP:(c + 1) * NP], bank[0][:, c * NP:(c + 1) * NP], ACT.Exp,
                                       bias=neg_max[:, i % 2, c:c + 1],
                                       accum_out=row_sum[:, i % 2, c:c + 1]).then_inc(exp_done, 1)
                if 1 <= i <= NU:
                    n = i - 1
                    act.wait_ge(pt_ready, n + 1)
                    if n == 0:
                        act.wait_ge(rows_stored, 16 * 6)
                    if n >= 1:
                        act.wait_ge(pv_ready, n)
                    act.activation(probs_t, bank[2][:, :], ACT.Copy).then_inc(pt_copied, 1)
                if 2 <= i:
                    n = i - 2
                    mem, h = units[n]
                    p = HD * (h % 2)
                    act.wait_ge(pv_ready, n + 1)
                    act.activation(o_cols[p:p + HD, (OMEM if mem else OATT) + h // 2, 0:NP],
                                   bank[4][p:p + HD, (n % 2) * NP:(n % 2 + 1) * NP], ACT.Copy).then_inc(o_copied, 1)
                for m in pages_beside(i):
                    act.wait_ge(page_turned, m + 1)
                    if m >= 2:
                        act.wait_ge(page_scored, m - 1)
                    act.activation(k_turned[m % 2][:, :], bank[(1, 5)[m % 2]][:, :], ACT.Copy).then_inc(page_copied, 1)
            act.wait_ge(page_scored, TURNED)
            wide = 2 * TURN_PAGES * HEADS
            for b in range(TURN_FROM, NS):
                src = bank[3][:, (b - TURN_FROM) * wide:(b - TURN_FROM + 1) * wide]
                dst = scores[:, :, b * HEADS:(b + 1) * HEADS].rearrange("p (c j) r -> p c j r", c=2)
                act.activation(dst[:, :, PAGES // 2 - TURN_PAGES:, :],
                               src.rearrange("p (c j r) -> p c j r", c=2, j=TURN_PAGES), ACT.Copy).then_inc(page_kept, 1)

            def layernorm_root(n, rows, c):
                act.wait_ge(res_ready, n)
                act.activation(ln_square(c)[0:rows], x_rows[0:rows, c, :], ACT.Square, bias=ln_s[0:rows, c, 2:3],
                               accum_out=ln_s[0:rows, c, 3:4]).then_inc(var_ready, 1)
                act.wait_ge(var_ready, n)
                act.activation(ln_s[0:rows, c, 4:5], ln_s[0:rows, c, 3:4], ACT.Sqrt, bias=eps[0:rows], scale=1.0 / D)\
                   .then_inc(root_ready, 1)

            act.wait_ge(sm_max, 1)
            act.activation(logits, logits, ACT.Exp, bias=stat[:, 2:3], accum_out=stat[:, 3:4]).then_inc(sm_exp, 1)
            act.activation(stat[:, 4:5], own, ACT.Exp, bias=stat[:, 2:3]).then_inc(sm_exp, 1)
            act.wait_ge(ptt_ready, 1)
            for i in range(2):
                act.activation(scores[:, 8 * i:8 * i + 8, :], bank[2 + i][:, :].rearrange("p (g r) -> p g r", g=8), ACT.Copy)\
                   .then_inc(ptt_copied, 1)
            act.wait_ge(po_ready, 1)
            act.activation(po_new, bank[5][0:NS, 320:320 + ROWS], ACT.Copy).then_inc(po_copied, 1)
            act.wait_ge(ss_ready, 1)
            act.activation(rms_p[:, 0, :], bank[4][:, 0:NP], ACT.Sqrt, bias=eps, scale=1.0 / AW)
            act.activation(rms_p[:, 1, :], bank[4][:, NP:2 * NP], ACT.Sqrt, bias=eps, scale=1.0 / MW)
            act.activation(rms_p[:, 2, :], bank[5][:, 0:NP], ACT.Sqrt, bias=eps, scale=1.0 / MW).then_inc(rt_ready, 1)
            act.wait_ge(mm_max, 1)
            act.activation(mem_probs, bank[4][0:MROWS, 0:NMEM], ACT.Exp, bias=mstat[:, 0:1],
                           accum_out=mstat[:, 1:2]).then_inc(mm_exp, 1)
            act.wait_ge(mmt_ready, 1)
            act.activation(mem_pt, bank[4][:, 256:256 + 2 * MROWS].rearrange("p (g r) -> p g r", g=2), ACT.Copy)\
               .then_inc(mmt_copied, 1)
            act.wait_ge(bias_in, 16 * 6)
            act.wait_ge(mix_ready, 1)
            for i in range(3):
                rows = (3 - i) * E
                if i > 0:
                    act.wait_ge(left_ready, i)
                act.activation(bias_up[0:rows], bias_left[0:rows, 0:2 * FF], ACT.Copy)
                act.activation(bias_down[0:rows], bias_left[0:rows, 2 * FF:2 * FF + D], ACT.Copy).then_inc(pieces_ready, 1)
            layernorm_root(1, PARTS, 0)
            layernorm_root(2, PARTS, 1)

            def x1_columns(c):
                for i in range(2):
                    act.wait_ge(x1t_ready, 2 * c + i + 1)
                    act.activation(o_cols[:, 4 * i:4 * i + 4, c * PARTS:(c + 1) * PARTS],
                                   bank[2 + i][:, :].rearrange("p (k t) -> p k t", k=4), ACT.Copy).then_inc(x1t_copied, 1)

            act.wait_ge(oc_ready, NS)
            act.activation(o_cols[:, OATT:OATT + 4, NP:T], bank[5][:, 320:320 + 4 * NS].rearrange("p (j b) -> p j b", j=4),
                           ACT.Copy).then_inc(oc_copied, 1)
            act.activation(o_cols[:, OMEM:OMEM + 2, NP:T], bank[5][:, 256:256 + 2 * NS].rearrange("p (j b) -> p j b", j=2),
                           ACT.Copy).then_inc(oc_copied, 1)
            x1_columns(0)
            act.wait_ge(ss_ready, 2)
            act.activation(rms_s[0:HD], bank[5][0:HD, 256:257], ACT.Sqrt, bias=eps[0:HD], scale=1.0 / AW)
            act.activation(rms_s[HD:PARTS], bank[5][HD:PARTS, 256:257], ACT.Sqrt, bias=eps[HD:PARTS], scale=1.0 / MW)\
               .then_inc(rt_ready, 1)
            for half in range(2):
                act.wait_ge(parts_ready, half + 1)
                act.wait_ge(inverse_ready, 1)
                act.activation(sample_parts[:, half, :], bank[half][:, :], ACT.Copy, scale=rms_s).then_inc(parts_copied, 1)
            x1_columns(1)
            layernorm_root(3, NS, 2)
            act.wait_ge(lgt_ready, 1)
            act.activation(logit_parts, bank[0][:, 0:NP], ACT.Copy).then_inc(lgt_copied, 1)
            for i in range(2):
                act.wait_ge(x1t_ready, 5 + i)
                act.activation(o_cols[:, 4 * i:4 * i + 4, NP:T],
                               bank[2 + i][:, :].rearrange("p (k t) -> p k t", k=4)[:, :, 0:NS], ACT.Copy)\
                   .then_inc(x1t_copied, 1)
            act.wait_ge(xm_ready, 1)
            act.activation(w4, w4, ACT.Exp).then_inc(xe_ready, 1)
            act.wait_ge(rg_ready, 1)
            act.activation(expert_range, bank[7][0:3 * E, 0:2], ACT.Copy).then_inc(rg_copied, 1)

            def copy_gathered(n):
                act.wait_ge(gat_ready, n)
                act.activation(xg, bank[2][:, :], ACT.Copy).then_inc(gat_copied, 1)

            def copy_turned(n):
                act.wait_ge(xgt_ready, n)
                act.activation(xg_t.rearrange("p j h s -> p (j h s)"), bank[4][:, :], ACT.Copy).then_inc(xgt_copied, 1)

            copy_gathered(1)
            copy_turned(1)
            act.wait_ge(table_ready, 1)
            count = act.value_load(n_blocks[0:1, 0:1], min_val=E, max_val=MAX_BLOCKS)
            act.wait_ge(sums_zeroed, 1)
            act.sem_inc(dn_copied, 1)
            with act.Fori(0, MAX_BLOCKS) as b:
                with act.If(b < count):
                    act.wait_ge(g_ready, b + 1)
                    act.activation(sig_v, gate_v, ACT.Sigmoid, scale=SW_ALPHA).then_inc(sg_ready, 1)
                    act.wait_ge(weight_turned, b + 1)
                    act.activation(slot_weight_t[:, 0:T], bank[4][:, 0:T], ACT.Copy).then_inc(weight_copied, 1)
                    copy_gathered(b + 2)
                    act.wait_ge(hdt_ready, b + 1)
                    act.activation(hid_t.rearrange("p j h s -> p (j h s)"), bank[3][:, :], ACT.Copy).then_inc(hdt_copied, 1)
                    copy_turned(b + 2)
                    act.wait_ge(dn_used, b * KC + KC)
                    act.activation(out_rows, bank[5][:, :], ACT.Copy).then_inc(dn_copied, 1)
                with act.Else():
                    pass
            for c in range(3):
                rows = PARTS if c < 2 else NS
                act.wait_ge(fin_sq, c + 1)
                act.activation(gate_up_w[0:rows, c, 0:D], x_rows[0:rows, c, :], ACT.Square, bias=ln_s[0:rows, c, 2:3],
                               accum_out=ln_s[0:rows, c, 3:4]).then_inc(fin_rt, 1)
                act.wait_ge(fin_rt, 2 * c + 1)
                act.activation(ln_s[0:rows, c, 4:5], ln_s[0:rows, c, 3:4], ACT.Sqrt, bias=eps[0:rows], scale=1.0 / D)\
                   .then_inc(fin_rt, 1)

        @block.gpsimd
        def _(pool):
            def step(instruction):
                pool.wait_ge(pool_n.sem, pool_n.on(instruction))

            def iota(dst, pattern, base=0, cm=0):
                return pool.iota(dst, pattern, base=base, channel_multiplier=cm, allow_small_or_imprecise_dtypes=True)

            step(pool.memset(ident, 0.0))
            pool.affine_select(ident, ident, [[-1, PARTS]], ALU.not_equal, 1.0, base=0, channel_multiplier=1)\
                .then_inc(eye_ready, 1)
            pool.iota(rowi[:, 0:1], [[1, 1]], base=0, channel_multiplier=1).then_inc(rowi_ready, 1)
            pool.memset(ones, 1.0)
            step(pool.memset(tri, 1.0))
            step(pool.affine_select(tri, tri, [[1, PARTS]], ALU.is_ge, 0.0, base=-1, channel_multiplier=-1))
            pool.memset(ones_b, 1.0)
            step(pool.tensor_copy(tri_b, tri))
            pool.memset(eps, EPS)
            iota(iota8, [[1, 8]])
            for h in range(HEADS):
                pool.memset(slope8[:, h:h + 1], 2.0 ** (-8.0 * (h + 1) / HEADS))
            step(iota(dist, [[-1, 3 * PARTS]], base=PARTS, cm=1))
            step(pool.affine_select(dist, dist, [[-1, 3 * PARTS]], ALU.is_ge, BIG, base=PARTS, channel_multiplier=1))
            step(pool.memset(delta8, 1.0))
            step(pool.affine_select(delta8, delta8, [[1, NS], [0, HEADS]], ALU.is_equal, 0.0, base=0, channel_multiplier=-1))
            pool.memset(lg.rearrange("p c e -> p (c e)"), 0.0)
            iota(iota32, [[1, E]])
            iota(slot_id, [[1, SLOTS]]).then_inc(const_ready, 1)
            pool.wait_ge(const_ready, 1)

            cache_row = "n (r t) h d -> (n r) (t h d)"
            rows_k = cache_k[0].rearrange(cache_row, r=2 * PARTS // PAGES)
            rows_v = cache_v[0].rearrange(cache_row, r=2 * PARTS // PAGES)

            def load_part(rows, b, half, part):
                width = PAGES * AW // 2
                pool.indirect_dma_start(ring[half][:, part * width:(part + 1) * width], None, rows,
                                        bass.IndirectOffsetOnAxis(ap=page_row[:, 2 * b + part:2 * b + part + 1], axis=0),
                                        bounds_check=2 * NPHYS * (PARTS // PAGES) - 1).then_inc(ring_in[half][part], 16)

            def load_keys(b):
                for part in range(2):
                    before = max((i for i in range(b) if K_HALF[i] == K_HALF[b]), default=None)
                    if b == 2:
                        pool.wait_ge(tile_ready, tile_no[(("proj", CH + 1), ("mkv", 3))[part]] + 1)
                    elif before is not None:
                        pool.wait_ge(k_scored, 2 * before + part + 1)
                        if turned_total(before, part):
                            pool.wait_ge(page_turned, turned_total(before, part))
                    load_part(rows_k, b, K_HALF[b], part)

            pool.wait_ge(page_rows_ready, 1)
            for b in range(NS - 2):
                load_keys(b)
            pool.wait_ge(tile_copied, len(tiles))
            for h in range(HEADS):
                last = pool.tensor_scalar(head_slope_eye[:, h, :], ident, -2.0 ** (-8.0 * (h + 1) / HEADS), None, ALU.mult)
            last.then_inc(eyes_ready, 1)
            load_keys(NS - 2)
            iota(logits, [[1, PAGES], [PAGES, PARTS]], base=-PAST).then_inc(logits_iota, 1)
            u = p_cols[:, CC:CC + 2, :]
            step(pool.tensor_tensor(u, u, p_cols[:, CH:CH + 2, :], ALU.mult))
            for j in range(2):
                o = o_cols[:, OCONV + j, 0:NP]
                t = p_cols[:, CH + j, 0:NP]
                step(pool.tensor_scalar(o, u[:, j, 0:NP], w_cols[:, j, 2:3], None, ALU.mult))
                for back in (1, 2):
                    step(pool.tensor_scalar(t[:, 0:NP - back], u[:, j, 0:NP - back], w_cols[:, j, 2 - back:3 - back], None,
                                            ALU.mult))
                    step(pool.tensor_tensor(o[:, back:NP], o[:, back:NP], t[:, 0:NP - back], ALU.add))
                step(pool.tensor_tensor(o, o, p_cols[:, CB + j, 0:NP], ALU.mult))
                so_, ts = o_cols[:, OCONV + j, NP:T], c_s[:, j, :]
                step(pool.tensor_scalar(so_, u[:, j, NP:T], w_cols[:, j, 2:3], None, ALU.mult))
                for back in (1, 2):
                    step(pool.tensor_scalar(ts, s_cols[:, j, :, 2 - back], w_cols[:, j, 2 - back:3 - back], None, ALU.mult))
                    step(pool.tensor_tensor(so_, so_, ts, ALU.add))
                step(pool.tensor_tensor(so_, so_, p_cols[:, CB + j, NP:T], ALU.mult))
                if j == 0:
                    load_keys(NS - 1)
            pool.sem_inc(conv_done, 1)
            for j in range(2):
                cols = slice(j * PARTS, (j + 1) * PARTS)
                with nc.allow_non_contiguous_dma(reason="two rows of the convolution state"):
                    pool.dma_start(conv_prompt[0, 0][:, cols].rearrange("r p -> p r"), u[:, j, NP - 2:NP]).then_inc(conv_stored, 16)
                    pool.dma_start(conv_sample[0, :, 1, cols].rearrange("b p -> p b"), u[:, j, NP:T]).then_inc(conv_stored, 16)

            def load_router():
                pool.wait_ge(pv_ready, NU)
                iota(block_iota, [[1, MAX_BLOCKS + 1]]).then_inc(table_iota, 1)
                with nc.allow_non_contiguous_dma(reason="rows of 128 bytes"):
                    pool.dma_start(w_r, w_router[0].rearrange("(k p) e -> p k e", p=PARTS)).then_inc(router_in, 16)
                pool.dma_start(br_row, b_router[0][None, :].broadcast_to([PARTS, E])).then_inc(router_in, 16)

            for b in range(NS):
                if b == 3:
                    load_router()
                for part in range(2):
                    if b < 2:
                        pool.wait_ge(k_scored, 2 * (NS - 2 + b) + part + 1)
                        pool.wait_ge(page_turned, turned_total(NS - 2 + b, part))
                    else:
                        pool.wait_ge(unit_read, 2 * (b - 2) + part + 1)
                    load_part(rows_v, b, b % 2, part)

        @block.vector
        def _(dve):
            def step(instruction):
                dve.wait_ge(dve_n.sem, dve_n.on(instruction))

            dve.wait_ge(rowi_ready, 1)
            step(dve.tensor_scalar(rowi[:, 1:2], rowi[:, 0:1], HEADS - 1, None, ALU.bitwise_and))
            step(dve.tensor_scalar(rowi[:, 2:3], rowi[:, 0:1], 3, 3, ALU.logical_shift_right, ALU.bitwise_and))
            step(dve.tensor_scalar(rowi[:, 3:4], rowi[:, 0:1], 5, None, ALU.logical_shift_right))
            step(dve.tensor_scalar(rowi[:, 4:5], rowi[:, 0:1], 3, None, ALU.bitwise_and))
            step(dve.tensor_scalar(rowi[:, 5:6], rowi[:, 0:1], 2, 7, ALU.logical_shift_right, ALU.bitwise_and))
            step(dve.tensor_scalar(rowi[:, 6:7], rowi[:, 0:1], 3, None, ALU.logical_shift_right))
            step(dve.tensor_scalar(rowi[:, 7:8], rowi[:, 0:1], 31, None, ALU.bitwise_and))
            step(dve.tensor_scalar(rowi[:, 8:9], rowi[:, 0:1], 6, None, ALU.logical_shift_right))
            step(dve.tensor_copy(row_f, rowi[:, :]))
            dve.wait_ge(pages_in, 16 * NS)
            step(dve.tensor_copy(page_f, page_of[:, :]))
            step(dve.tensor_scalar(page_f, page_f, float(PARTS // PAGES), row_f[:, 1:2], ALU.mult, ALU.add))
            for i in range(2):
                step(dve.tensor_scalar(page_rows_f[:, :, i], page_f, 2.0, float(i), ALU.mult, ALU.add))
            dve.tensor_copy(page_row[:, :], page_rows_f.rearrange("p b i -> p (b i)")).then_inc(page_rows_ready, 1)
            dve.wait_ge(const_ready, 1)
            step(dve.tensor_scalar(hot8, iota8, row_f[:, 1:2], None, ALU.is_equal))
            step(dve.tensor_tensor(slope8, slope8, hot8, ALU.mult))
            step(dve.tensor_reduce(slope, slope8, AX.X, ALU.add))
            step(dve.tensor_scalar(row_sel, iota8[:, 0:4], row_f[:, 2:3], None, ALU.is_equal))
            step(dve.tensor_scalar(sum_groups, iota8, 32.0 - NS, row_f[:, 7:8], ALU.add, ALU.is_equal))
            step(dve.tensor_scalar(grp_sel, iota8[:, 0:4], row_f[:, 3:4], None, ALU.is_equal))
            step(dve.tensor_scalar(q_sel, iota8[:, 0:2], 4.0, row_f[:, 3:4], ALU.mult, ALU.add))
            step(dve.tensor_scalar(q_sel, q_sel, row_f[:, 5:6], None, ALU.is_equal))
            for q in range(2):
                step(dve.tensor_scalar(hot4[:, q, :], iota8[:, 0:MHEADS], row_f[:, 4:5], q_sel[:, q:q + 1],
                                       ALU.is_equal, ALU.mult))
            step(dve.tensor_scalar(dsel, iota8[0:ROWS], row_f[0:ROWS, 6:7], None, ALU.is_equal))

            dve.wait_ge(tile_copied, tile_no[("proj", CQ + 3)] + 1)
            for j in range(4):
                step(dve.tensor_scalar(hot_chunk[:, j, :], iota8, -2.0 * j, row_f[:, 8:9], ALU.add, ALU.is_equal))
                last = dve.tensor_tensor(q_head_cols[:, j], p_cols[:, CQ + j, NP:T].unsqueeze(2).broadcast_to([PARTS, NS, HEADS]),
                                         hot_chunk[:, j, :].unsqueeze(1).broadcast_to([PARTS, NS, HEADS]), ALU.mult)
            last.then_inc(q_cols_ready, 1)

            def score_keys(slot):
                b, part = slot // 2, slot % 2
                half, first = K_HALF[b], part * PAGES // 2
                n = PAGES // 2 - (TURN_PAGES if b >= TURN_FROM else 0)
                r = ring[half][:, first * AW:(first + n) * AW]
                dve.wait_ge(ring_in[half][part], keys_total(b))
                if part == 0:
                    dve.wait_ge(qb_ready, b + 1)
                pages_r = r.rearrange("p (g n) -> p g n", g=n)
                q = bank[6 + b % 2][:, :].unsqueeze(1).broadcast_to([PARTS, n, AW])
                step(dve.tensor_tensor(pages_r, pages_r, q, ALU.mult))
                unit_steps(2 * (slot - FIRST_SLOT) + 1)
                dve.tensor_reduce(scores[:, first:first + n, b * HEADS:(b + 1) * HEADS],
                                  r.rearrange("p (g h d) -> p g h d", g=n, h=HEADS), AX.X, ALU.add).then_inc(k_scored, 1)

            def unit_steps(i):
                n = i - 1
                if 0 <= n < NU:
                    dve.wait_ge(exp_done, 2 * (n + 1))
                    if n >= 2:
                        dve.wait_ge(norm_done, n - 1)
                    step(dve.reciprocal(row_inv[:, n % 2, :], row_sum[:, n % 2, :]))
                    pn = probs[:, n % 2, :].rearrange("p (c k) -> p c k", c=2)
                    dve.tensor_tensor(pn, pn, row_inv[:, n % 2, :].unsqueeze(2).broadcast_to([PARTS, 2, NP]), ALU.mult)\
                       .then_inc(norm_done, 1)
                if 0 <= i < NU:
                    dve.wait_ge(sc_ready, i + 1)
                    dve.tensor_reduce(neg_max[:, i % 2, :], bank[0][:, :].rearrange("p (c k) -> p c k", c=2), AX.X,
                                      ALU.max, negate=True).then_inc(mx_ready, 1)

            for slot in range(SCORE_SLOTS):
                unit_steps(2 * (slot - FIRST_SLOT))
                score_keys(slot)
            for i in range(2 * (SCORE_SLOTS - FIRST_SLOT), NU + 1):
                unit_steps(i)

            dve.wait_ge(tile_copied, len(tiles))
            own_prod = gate_up_w[0:NS, 2, 2 * AW:3 * AW]
            step(dve.tensor_tensor(own_prod, q_new, k_new, ALU.mult))
            step(dve.tensor_reduce(so, own_prod.rearrange("p (h d) -> p h d", h=HEADS), AX.X, ALU.add))
            dve.tensor_tensor(so_spread.rearrange("p (b h) -> p b h", b=NS), delta8.rearrange("p (b h) -> p b h", b=NS),
                              so.unsqueeze(1).broadcast_to([NS, NS, HEADS]), ALU.mult).then_inc(so_ready, 1)
            def layernorm_center(c, banks, order):
                rows = PARTS if c < 2 else NS
                x, s = x_rows[0:rows, c, :], ln_s[0:rows, c]
                dve.wait_ge(proj_ready, order)
                for half in range(2):
                    cols = slice(half * HALF, (half + 1) * HALF)
                    step(dve.scalar_tensor_tensor(x[:, cols], x[:, cols], ALPHA, banks[half][0:rows, :], ALU.mult, ALU.add,
                                                  accum_out=s[:, half:half + 1]))
                step(dve.tensor_scalar(s[:, 2:3], s[:, 0:1], s[:, 1:2], -1.0 / D, ALU.add, ALU.mult))
                dve.sem_inc(res_ready, 1)
                if order == 1:
                    dve.wait_ge(ln1_in, 32)
                step(dve.scalar_tensor_tensor(ln_gained[0:rows], x, s[:, 2:3], ln1_gain[0:rows], ALU.add, ALU.mult))

            def layernorm_scale(c, order):
                rows = PARTS if c < 2 else NS
                x, s = x_rows[0:rows, c, :], ln_s[0:rows, c]
                dve.wait_ge(root_ready, order)
                step(dve.reciprocal(s[:, 5:6], s[:, 4:5]))
                dve.scalar_tensor_tensor(x, ln_gained[0:rows], s[:, 5:6], ln1_bias[0:rows], ALU.mult, ALU.add)\
                   .then_inc(x1_ready, 1)

            dve.wait_ge(own_ready, 1)
            step(dve.tensor_copy(own, bank[5][0:ROWS, 511:512]))
            for i in range(4):
                dve.wait_ge(l_ready, i + 1)
                step(dve.tensor_reduce(gate_part[:, :, i], bank[i][0:ROWS, :].rearrange("p (j n q) -> p n j q", j=4, n=NBLK),
                                       AX.XY, ALU.add))
            step(dve.tensor_reduce(gate8, gate_part, AX.X, ALU.add))
            step(dve.max(top8, gate8))
            step(dve.max_index(seli[:, :], top8, gate8))
            step(dve.tensor_copy(seli_f, seli[:, :]))
            step(dve.tensor_scalar(pen, iota8[0:ROWS], seli_f[:, 0:1], None, ALU.is_equal))
            for i in (1, 2):
                step(dve.scalar_tensor_tensor(pen, iota8[0:ROWS], seli_f[:, i:i + 1], pen, ALU.is_equal, ALU.add))
            step(dve.tensor_scalar(pen, pen, -1.0, BIG, ALU.add, ALU.mult))
            dve.wait_ge(logits_iota, 1)
            for i in range(4):
                l = logits[:, i * 512:(i + 1) * 512]
                step(dve.scalar_tensor_tensor(l, l, slope[0:ROWS], bank[i][0:ROWS, :], ALU.mult, ALU.add))
            lb = logits.rearrange("p (j n q) -> p j n q", j=PAGES, n=NBLK)
            step(dve.tensor_tensor(lb, lb, pen.unsqueeze(1).unsqueeze(3).broadcast_to([ROWS, PAGES, NBLK, BLK // PAGES]),
                                   ALU.add))
            step(dve.tensor_reduce(stat[:, 0:1], logits, AX.X, ALU.max))
            step(dve.tensor_tensor(stat[:, 1:2], stat[:, 0:1], own, ALU.max))
            dve.tensor_scalar(stat[:, 2:3], stat[:, 1:2], -1.0, None, ALU.mult).then_inc(sm_max, 1)

            def score_memory(i):
                dve.wait_ge(mem_kv_in, 32)
                dve.wait_ge(qb_ready, NS + i + 1)
                r = mem_k[:, 2 * i:2 * i + 2]
                q = MEM_BANK[i][:, :].rearrange("p (b n) -> p b n", b=2).unsqueeze(2).broadcast_to([PARTS, 2, 2, MW])
                step(dve.tensor_tensor(r, r, q, ALU.mult))
                for b in (2 * i, 2 * i + 1):
                    last = dve.tensor_reduce(mem_scores[:, :, b * MHEADS:(b + 1) * MHEADS],
                                             mem_k[:, b].rearrange("p g (h d) -> p g h d", h=MHEADS), AX.X, ALU.add)
                last.then_inc(mem_scored, 1)

            score_memory(0)
            dve.wait_ge(sm_exp, 2)
            step(dve.tensor_tensor(stat[:, 5:6], stat[:, 3:4], stat[:, 4:5], ALU.add))
            step(dve.reciprocal(stat[:, 6:7], stat[:, 5:6]))
            step(dve.tensor_tensor(stat[:, 7:8], stat[:, 4:5], stat[:, 6:7], ALU.mult))
            step(dve.tensor_scalar(po_spread, dsel, stat[:, 7:8], None, ALU.mult))
            dve.tensor_scalar(logits, logits, stat[:, 6:7], None, ALU.mult).then_inc(sm_p, 1)

            score_memory(1)
            dve.wait_ge(o_copied, NU)
            dve.wait_ge(conv_done, 1)
            dve.tensor_tensor(squares, o_cols[:, :, 0:NP], o_cols[:, :, 0:NP], ALU.mult).then_inc(sq_ready, 1)

            def mask_values(b):
                dve.wait_ge(pv_done, b + 1)
                if b >= 2:
                    dve.wait_ge(oc_ready, b - 1)
                dve.scalar_tensor_tensor(o_masked[:, b % 2, :].rearrange("p (h d) -> p h d", h=HEADS),
                                         bank[6 + b % 2][:, :].rearrange("p (h d) -> p h d", h=HEADS),
                                         row_sel[:, b % 4:b % 4 + 1], hot_head, ALU.mult, ALU.mult).then_inc(om_ready, 1)

            hot_head = hot8.unsqueeze(2).broadcast_to([PARTS, HEADS, HD])
            score_memory(2)
            mask_values(0)
            score_memory(3)
            mask_values(1)
            dve.wait_ge(mm_ready, 1)
            dve.tensor_reduce(mstat[:, 0:1], bank[4][0:MROWS, 0:NMEM], AX.X, ALU.max, negate=True).then_inc(mm_max, 1)
            dve.wait_ge(mm_exp, 1)
            step(dve.reciprocal(mstat[:, 2:3], mstat[:, 1:2]))
            dve.tensor_scalar(mem_probs, mem_probs, mstat[:, 2:3], None, ALU.mult).then_inc(mm_norm, 1)
            dve.wait_ge(rt_ready, 1)
            step(dve.reciprocal(rms_p, rms_p))
            for s, (first, n) in enumerate(((OATT, 4), (OCONV, 2), (OMEM, 2))):
                for j in range(first, first + n):
                    last = dve.scalar_tensor_tensor(o_cols[:, j, 0:NP], o_cols[:, j, 0:NP], g_cols[:, j:j + 1],
                                                    rms_p[:, s, :], ALU.mult, ALU.mult)
            last.then_inc(mix_ready, 1)
            dve.wait_ge(mpv_done, 1)
            dve.tensor_tensor(mem_masked.rearrange("p q (h d) -> p (q h) d", h=MHEADS),
                              bank[1][:, :].rearrange("p (q d) -> p q d", d=HD),
                              hot4.rearrange("p q h -> p (q h)").unsqueeze(2).broadcast_to([PARTS, 2 * MHEADS, HD]),
                              ALU.mult).then_inc(mom_ready, 1)
            for b in range(2, NS):
                mask_values(b)
                if b < 4:
                    dve.wait_ge(pieces_ready, b - 1)
                    rows = (4 - b) * E
                    left = bias_left[0:rows]
                    dve.tensor_tensor(left[:, 0:2 * FF], left[:, 0:2 * FF], bias_up[0:rows], ALU.subtract)
                    dve.tensor_tensor(left[:, 2 * FF:], left[:, 2 * FF:], bias_down[0:rows], ALU.subtract)\
                       .then_inc(left_ready, 1)
                elif b == 4:
                    layernorm_center(0, bank[0:2], 1)
                elif b == 5:
                    layernorm_scale(0, 1)
                elif b == 6:
                    layernorm_center(1, bank[2:4], 2)
                    layernorm_scale(1, 2)
            dve.wait_ge(oc_copied, 2)
            dve.tensor_tensor(sq_s, o_cols[:, :, T - 32:T], o_cols[:, :, T - 32:T], ALU.mult).then_inc(sq_ready, 1)
            dve.wait_ge(sq_ready, 2)
            dve.tensor_tensor(o_cols[:, :, NP:T], o_cols[:, :, NP:T], g_cols.unsqueeze(2).broadcast_to([PARTS, KC, NS]),
                              ALU.mult).then_inc(mix_ready, 1)
            dve.wait_ge(rt_ready, 2)
            dve.reciprocal(rms_s, rms_s).then_inc(inverse_ready, 1)
            dve.tensor_scalar(sum_logits, iota32, row_f[:, 7:8], None, ALU.is_equal).then_inc(lgt_ones, 1)
            dve.wait_ge(pv_done, NS)
            dve.wait_ge(unit_read, 2 * NS)
            step(dve.memset(expert_sum.rearrange("p j t -> p (j t)"), 0.0))
            step(dve.memset(slot_weight_t, 0.0))
            dve.memset(out_rows, 0.0).then_inc(sums_zeroed, 1)
            layernorm_center(2, bank[6:8], 3)
            layernorm_scale(2, 3)

            dve.wait_ge(router_in, 32)
            pl = bank[4][:, 0:3 * E].rearrange("p (c e) -> p c e", c=3)
            dve.wait_ge(lg_ready, 1)
            step(dve.tensor_tensor(lg[:, 0:2, :], pl[:, 0:2, :], br_row.unsqueeze(1).broadcast_to([PARTS, 2, E]), ALU.add))
            dve.sem_inc(prompt_logits_read, 1)
            for c in range(3):
                if c == 2:
                    dve.wait_ge(lg_ready, 2)
                    step(dve.tensor_tensor(lg[0:NS, 2, :], pl[0:NS, 2, :], br_row[0:NS], ALU.add))
                step(dve.max(max8[:, c, :], lg[:, c, :]))
                step(dve.max_index(topi[:, c, :], max8[:, c, :], lg[:, c, :]))
            step(dve.tensor_copy(topf, topi[:, :, :]))
            dve.tensor_tensor(w4, max8[:, :, 0:TOPK], max8[:, :, 0:1].broadcast_to([PARTS, 3, TOPK]), ALU.subtract)\
               .then_inc(xm_ready, 1)
            step(dve.tensor_tensor(onehot, iota32.unsqueeze(1).unsqueeze(1).broadcast_to([PARTS, 3, TOPK, E]),
                                   topf[:, :, 0:TOPK].unsqueeze(3).broadcast_to([PARTS, 3, TOPK, E]), ALU.is_equal))
            with nc.allow_low_precision(reason="zeros and ones"):
                dve.tensor_reduce(chosen, onehot.rearrange("p c k e -> p c e k"), AX.X, ALU.add).then_inc(ch_ready, 1)
            dve.wait_ge(cnt_ready, 1)
            cnt = bank[6][:, 3 * E:4 * E]
            step(dve.tensor_scalar(nb, cnt, float(SLOTS), 1.0, ALU.is_gt, ALU.add))
            for m in range(2, -(-T // SLOTS)):
                step(dve.scalar_tensor_tensor(nb, cnt, float(m * SLOTS), nb, ALU.is_gt, ALU.add))
            step(dve.tensor_tensor_scan(ends, ones[:, 0:E], nb, 0.0, ALU.mult, ALU.add))
            step(dve.tensor_tensor(starts, ends, nb, ALU.subtract))
            dve.sem_inc(rp_ready, 1)
            step(dve.memset(slots_g.rearrange("p c e -> p (c e)"), 0.0))
            st = starts.unsqueeze(1).broadcast_to([PARTS, 2, E])
            step(dve.scalar_tensor_tensor(slots_g[:, 0:2, :], st, float(SLOTS),
                                          bank[6][:, 0:2 * E].rearrange("p (c e) -> p c e", c=2), ALU.mult, ALU.add))
            step(dve.scalar_tensor_tensor(slots_g[0:NS, 2, :], starts[0:NS], float(SLOTS), bank[6][0:NS, 2 * E:3 * E],
                                          ALU.mult, ALU.add))
            step(dve.tensor_tensor(oh_g, onehot, slots_g.unsqueeze(2).broadcast_to([PARTS, 3, TOPK, E]), ALU.mult))
            step(dve.tensor_reduce(slot4, oh_g, AX.X, ALU.add))

            def slots(wait_used, n):
                if wait_used is not None:
                    dve.wait_ge(gat_ready, wait_used)
                    dve.wait_ge(step_b, wait_used)
                    dve.wait_ge(weight_ready, wait_used)
                dve.tensor_tensor(slot_eq, slot_id.unsqueeze(1).unsqueeze(1).broadcast_to([PARTS, 3, TOPK, SLOTS]),
                                  slot4.unsqueeze(3).broadcast_to([PARTS, 3, TOPK, SLOTS]), ALU.is_equal).then_inc(step_a, 1)
                dve.wait_ge(step_a, n)
                dve.tensor_scalar(slot_id, slot_id, float(SLOTS), None, ALU.add).then_inc(step_b, 1)
                dve.tensor_reduce(slot_hot, slot_eq.rearrange("p c k s -> p c s k"), AX.X, ALU.add).then_inc(hot_ready, 1)

            def slot_weights(n, turned=None):
                if turned is not None:
                    dve.wait_ge(weight_turned, turned)
                dve.wait_ge(hot_ready, n)
                dve.tensor_tensor(slot_eq, slot_eq, w4.unsqueeze(3).broadcast_to([PARTS, 3, TOPK, SLOTS]), ALU.mult)\
                   .then_inc(weighted, 1)
                dve.wait_ge(weighted, n)
                for i in range(2):
                    last = dve.tensor_reduce(slot_weight[:, :, i * SLOTS:(i + 1) * SLOTS],
                                             slot_eq.rearrange("p c k s -> p c s k"), AX.X, ALU.add)
                last.then_inc(weight_ready, 1)

            def add_round(n, j):
                dve.wait_ge(sum_ready, n * KC + (j + 1))
                dve.wait_ge(sum_added, n * KC + (j + 1))
                dve.tensor_tensor(expert_sum[:, j, :], expert_sum[:, j, :], bank[6 + j % 2][:, 0:T], ALU.add)\
                   .then_inc(sum_added, 1)

            def bias_rows(n):
                dve.wait_ge(step_c, n)
                dve.tensor_scalar(block_ge, block_id, expert_range[:, 0:1], None, ALU.is_ge).then_inc(step_d, 1)
                dve.wait_ge(step_d, n)
                dve.scalar_tensor_tensor(bias_hot, block_id, expert_range[:, 1:2], block_ge, ALU.is_lt, ALU.mult)\
                   .then_inc(bias_hot_ready, 1)
                dve.wait_ge(bias_hot_ready, n)
                dve.tensor_scalar(block_id, block_id, 1.0, None, ALU.add).then_inc(step_c, 1)

            slots(None, 1)
            step(dve.memset(block_id, 0.0))
            bi = MAX_BLOCKS + 1
            dve.wait_ge(table_iota, 1)
            step(dve.tensor_tensor(ends_cmp, block_iota.unsqueeze(2).broadcast_to([1, bi, E]),
                                   ends[0:1].unsqueeze(1).broadcast_to([1, bi, E]), ALU.is_ge))
            step(dve.tensor_reduce(block_ef, ends_cmp, AX.X, ALU.add))
            step(dve.tensor_scalar(block_ef, block_ef, float(E - 1), None, ALU.min))
            step(dve.tensor_copy(block_expert[:, :], block_ef))
            step(dve.tensor_scalar(block_ef[:, 0:E], ends[0:1], -1.0, None, ALU.add))
            step(dve.tensor_copy(last_block[:, :], block_ef[:, 0:E]))
            dve.tensor_copy(n_blocks[:, :], ends[0:1, E - 1:E]).then_inc(table_ready, 1)
            dve.wait_ge(xe_ready, 1)
            step(dve.tensor_reduce(w4s, w4, AX.X, ALU.add))
            step(dve.reciprocal(w4s, w4s))
            step(dve.tensor_tensor(w4, w4, w4s.unsqueeze(2).broadcast_to([PARTS, 3, TOPK]), ALU.mult))
            dve.wait_ge(rg_copied, 1)
            dve.sem_inc(step_c, 1)
            bias_rows(1)
            slot_weights(1)
            dve.wait_ge(sums_zeroed, 1)
            dve.sem_inc(sum_added, 2)
            dve.wait_ge(table_ready, 1)
            count = dve.value_load(n_blocks[0:1, 0:1], min_val=E, max_val=MAX_BLOCKS)
            with dve.Fori(0, MAX_BLOCKS) as b:
                with dve.If(b < count):
                    slots(b + 1, b + 2)
                    for j in range(KC - 1):
                        add_round(b, j)
                    dve.wait_ge(gu_used, b * KC + KC)
                    dve.tensor_scalar(gate_v, bank[0][:, :], LIMIT, None, ALU.min).then_inc(g_ready, 1)
                    dve.tensor_scalar(up_v, bank[1][:, :], -LIMIT, LIMIT, ALU.max, ALU.min).then_inc(gu_read, 1)
                    dve.wait_ge(g_ready, b + 1)
                    dve.wait_ge(gu_read, b + 1)
                    dve.scalar_tensor_tensor(up_v, up_v, 1.0, gate_v, ALU.add, ALU.mult).then_inc(up_ready, 1)
                    dve.wait_ge(up_ready, b + 1)
                    dve.wait_ge(sg_ready, b + 1)
                    dve.tensor_tensor(hid, up_v, sig_v, ALU.mult).then_inc(hd_ready, 1)
                    add_round(b, KC - 1)
                    dve.wait_ge(hot_used, b + 1)
                    bias_rows(b + 2)
                    slot_weights(b + 2, b + 1)
                with dve.Else():
                    pass

            dve.wait_ge(ln2_in, 32)
            for j in range(KC):
                add_round(count, j)
            for c in range(3):
                rows = PARTS if c < 2 else NS
                x, s = x_rows[0:rows, c, :], ln_s[0:rows, c]
                dve.wait_ge(moe_ready, c + 1)
                for half in range(2):
                    cols = slice(half * HALF, (half + 1) * HALF)
                    step(dve.scalar_tensor_tensor(x[:, cols], x[:, cols], ALPHA, bank[2 * c + half][0:rows, :], ALU.mult,
                                                  ALU.add, accum_out=s[:, half:half + 1]))
                step(dve.tensor_scalar(s[:, 2:3], s[:, 0:1], s[:, 1:2], -1.0 / D, ALU.add, ALU.mult))
                dve.sem_inc(fin_sq, 1)
                dve.scalar_tensor_tensor(gate_up_w[0:rows, c, D:2 * D], x, s[:, 2:3], ln2_gain[0:rows], ALU.add, ALU.mult)\
                   .then_inc(gained, 1)
            for c in range(3):
                rows = PARTS if c < 2 else NS
                x, s = x_rows[0:rows, c, :], ln_s[0:rows, c]
                dve.wait_ge(fin_rt, 2 * c + 2)
                dve.wait_ge(gained, c + 1)
                step(dve.reciprocal(s[:, 5:6], s[:, 4:5]))
                dve.scalar_tensor_tensor(x, gate_up_w[0:rows, c, D:2 * D], s[:, 5:6], ln2_bias[0:rows], ALU.mult, ALU.add)\
                   .then_inc(y_ready, 1)


_INS = ['x_prompt', 'x_sample', 'cache_k', 'cache_v', 'cache_mem_k', 'cache_mem_v', 'state_conv', 'page_table',
        'mem_prompt', 'w_in', 'w_mem_kv', 'w_conv', 'g_mix', 'w_out', 'ln1_g', 'ln1_b', 'w_router', 'b_router',
        'w_gate_up', 'b_gate_up', 'w_down', 'b_down', 'ln2_g', 'ln2_b']


def kernel(**inputs):
    import numpy as np
    import concourse.bacc as bacc
    from concourse.bass_utils import run_bass_kernel_spmd

    nc = bacc.Bacc("TRN2", target_bir_lowering=False, num_devices=1)
    arrays, args = {}, []
    for name in _INS:
        a = np.ascontiguousarray(inputs[name])
        arrays[f"in_{name}"] = a
        args.append(nc.dram_tensor(f"in_{name}", a.shape, mybir.dt.from_np(a.dtype), kind="ExternalInput").ap())
    xp, xs, ck, mk, st = (inputs[n].shape for n in ('x_prompt', 'x_sample', 'cache_k', 'cache_mem_k', 'state_conv'))
    heads = (ck[3], ck[4])
    outs = [xp, xs, (1, 1, xp[1], *heads), (1, 1, xp[1], *heads), (1, 1, *st[2:]), (1, 1, *mk[2:]), (1, 1, *mk[2:]),
            (1, xs[0], 1, *heads), (1, xs[0], 1, *heads), tuple(st)]
    for i, shape in enumerate(outs):
        args.append(nc.dram_tensor(f"out_{i}", shape, F32, kind="ExternalOutput").ap())
    layer_kernel(nc, *args)
    r = run_bass_kernel_spmd(nc, [arrays], core_ids=[0])
    return tuple(r.results[0][f"out_{i}"] for i in range(len(outs)))
```
